# Optimizing a Trainium2 kernel written in Bass

```python
import math
import jax, jax.numpy as jnp
from jax import lax
import numpy as np

D_MODEL = 1024
BATCH = 1
SEQ = 256
DEPTH = 2

N_MIXERS = 2
N_META = 16
D_FF = 2816
CONV_WIDTH = 3
HEAD_DIM = 64
V_DIM = 2 * HEAD_DIM
N_HEADS = D_MODEL // (2 * HEAD_DIM)
ROT_DIM = HEAD_DIM // 4
ROPE_THETA = 500000.0
Q_BLOCK = 128
FRONT_PAD = Q_BLOCK - N_META
N_CONV_LAYERS = (DEPTH + N_MIXERS - 1) // N_MIXERS
N_ATTN_LAYERS = DEPTH // N_MIXERS
NORM_EPS = 1e-6
SUBLN_EPS = 1e-5
NEG_INF = -1e30


def rms_norm(t, g, eps=NORM_EPS):
    t32 = t.astype(jnp.float32)
    t32 = t32 * lax.rsqrt(jnp.mean(t32 * t32, axis=-1, keepdims=True) + eps)
    return t32.astype(t.dtype) * g.astype(t.dtype)

def swiglu(h, w_gu, w_down):
    g, u = jnp.split(h @ w_gu, 2, axis=-1)
    return (jax.nn.silu(g) * u) @ w_down

def short_conv_mixer(h, w_in, conv_w, w_out):
    b, c, xt = jnp.split(h @ w_in, 3, axis=-1)
    u = c * xt
    u = lax.conv_general_dilated(
        u, conv_w[:, None, :].astype(u.dtype),
        window_strides=(1,), padding=((CONV_WIDTH - 1, 0),),
        dimension_numbers=('NWC', 'WIO', 'NWC'),
        feature_group_count=u.shape[-1])
    return (b * u) @ w_out

def partial_rope(t, cos, sin):
    half = ROT_DIM // 2
    t1 = t[..., :half]
    t2 = t[..., half:ROT_DIM]
    c = cos[None, :, None, None, :]
    s = sin[None, :, None, None, :]
    return jnp.concatenate([t1 * c - t2 * s, t1 * s + t2 * c, t[..., ROT_DIM:]], axis=-1)

def diff_attention_mixer(h, w_qkv, lam_p, subln_g, w_o, lambda_init):
    bsz, seq_len, d = h.shape
    dt = h.dtype
    q, k, v = jnp.split(h @ w_qkv, 3, axis=-1)
    q = q.reshape(bsz, seq_len, N_HEADS, 2, HEAD_DIM)
    k = k.reshape(bsz, seq_len, N_HEADS, 2, HEAD_DIM)
    v = v.reshape(bsz, seq_len, N_HEADS, V_DIM)
    pos = jnp.arange(seq_len, dtype=jnp.float32)
    inv_freq = ROPE_THETA ** (-jnp.arange(0, ROT_DIM, 2, dtype=jnp.float32) / ROT_DIM)
    ang = pos[:, None] * inv_freq[None, :]
    cos = jnp.cos(ang).astype(dt)
    sin = jnp.sin(ang).astype(dt)
    q = partial_rope(q, cos, sin)
    k = partial_rope(k, cos, sin)
    q = jnp.pad(q, ((0, 0), (FRONT_PAD, 0), (0, 0), (0, 0), (0, 0))).transpose(0, 2, 3, 1, 4)
    k = jnp.pad(k, ((0, 0), (FRONT_PAD, 0), (0, 0), (0, 0), (0, 0))).transpose(0, 2, 3, 1, 4)
    v = jnp.pad(v, ((0, 0), (FRONT_PAD, 0), (0, 0), (0, 0))).transpose(0, 2, 1, 3)
    lp = seq_len + FRONT_PAD
    lam32 = lam_p.astype(jnp.float32)
    lam = (jnp.exp(jnp.sum(lam32[0] * lam32[1])) - jnp.exp(jnp.sum(lam32[2] * lam32[3]))
           + lambda_init)
    scale = HEAD_DIM ** -0.5
    outs = []
    for j in range(lp // Q_BLOCK):
        q0, q1 = j * Q_BLOCK, (j + 1) * Q_BLOCK
        qb = q[:, :, :, q0:q1]
        kb = k[:, :, :, :q1]
        vb = v[:, :, :q1]
        s = jnp.einsum('bhcqd,bhckd->bhcqk', qb, kb).astype(jnp.float32) * scale
        qi = jnp.arange(q0, q1)[:, None]
        ki = jnp.arange(q1)[None, :]
        mask = (ki <= qi) & (ki >= FRONT_PAD)
        p = jax.nn.softmax(jnp.where(mask, s, NEG_INF), axis=-1)
        a = p[:, :, 0] - lam * p[:, :, 1]
        outs.append(jnp.einsum('bhqk,bhkv->bhqv', a.astype(dt), vb))
    o = jnp.concatenate(outs, axis=2)[:, :, FRONT_PAD:]
    o = rms_norm(o, subln_g, SUBLN_EPS) * (1.0 - lambda_init)
    o = o.transpose(0, 2, 1, 3).reshape(bsz, seq_len, d)
    return o @ w_o

def first_inputs(seed: int = 0) -> dict:
    key = jax.random.key(seed)
    ks = jax.random.split(key, 20)

    def nrm(k, shape, scale):
        return jax.random.normal(k, shape, jnp.float32) * scale

    def gains(k, shape):
        return 1.0 + nrm(k, shape, 0.02)

    D = D_MODEL
    return {
        'x': nrm(ks[0], (BATCH, SEQ, D), 1.0),
        'meta_tokens': nrm(ks[1], (N_META, D), 1.0),
        'ln_ffn1': gains(ks[2], (DEPTH, 2, D)),
        'ffn1_w_gu': nrm(ks[3], (DEPTH, D, 2 * D_FF), D ** -0.5),
        'ffn1_w_down': nrm(ks[4], (DEPTH, D_FF, D), D_FF ** -0.5),
        'ln_mix': gains(ks[5], (DEPTH, 2, D)),
        'conv_w_in': nrm(ks[6], (N_CONV_LAYERS, D, 3 * D), D ** -0.5),
        'conv_w': nrm(ks[7], (N_CONV_LAYERS, CONV_WIDTH, D), CONV_WIDTH ** -0.5),
        'conv_w_out': nrm(ks[8], (N_CONV_LAYERS, D, D), D ** -0.5),
        'attn_w_qkv': nrm(ks[9], (N_ATTN_LAYERS, D, 3 * D), D ** -0.5),
        'attn_lambda': nrm(ks[10], (N_ATTN_LAYERS, 4, HEAD_DIM), 0.1),
        'attn_subln_g': gains(ks[11], (N_ATTN_LAYERS, V_DIM)),
        'attn_w_o': nrm(ks[12], (N_ATTN_LAYERS, D, D), D ** -0.5),
        'ln_ffn2': gains(ks[13], (DEPTH, 2, D)),
        'ffn2_w_gu': nrm(ks[14], (DEPTH, D, 2 * D_FF), D ** -0.5),
        'ffn2_w_down': nrm(ks[15], (DEPTH, D_FF, D), D_FF ** -0.5),
    }

def first_block(x, meta_tokens, ln_ffn1, ffn1_w_gu, ffn1_w_down, ln_mix,
              conv_w_in, conv_w, conv_w_out, attn_w_qkv, attn_lambda,
              attn_subln_g, attn_w_o, ln_ffn2, ffn2_w_gu, ffn2_w_down):
    bsz = x.shape[0]
    meta = jnp.broadcast_to(meta_tokens.astype(x.dtype)[None], (bsz, N_META, x.shape[-1]))
    h = jnp.concatenate([meta, x], axis=1)
    for i in range(DEPTH):
        f = swiglu(rms_norm(h, ln_ffn1[i, 0]), ffn1_w_gu[i], ffn1_w_down[i])
        h = h + 0.5 * rms_norm(f, ln_ffn1[i, 1])
        hn = rms_norm(h, ln_mix[i, 0])
        j = i // N_MIXERS
        if i % N_MIXERS == 0:
            m = short_conv_mixer(hn, conv_w_in[j], conv_w[j], conv_w_out[j])
        else:
            lambda_init = 0.8 - 0.6 * math.exp(-0.3 * i)
            m = diff_attention_mixer(hn, attn_w_qkv[j], attn_lambda[j],
                                     attn_subln_g[j], attn_w_o[j], lambda_init)
        h = h + rms_norm(m, ln_mix[i, 1])
        f = swiglu(rms_norm(h, ln_ffn2[i, 0]), ffn2_w_gu[i], ffn2_w_down[i])
        h = h + 0.5 * rms_norm(f, ln_ffn2[i, 1])
    return h[:, N_META:]


DEPTH_2 = 1

D_MIX = D_MODEL
GLA_WIDTH = D_MIX // 2
GLA_HEADS = 4
GLA_DK = GLA_WIDTH // 2 // GLA_HEADS
GLA_DV = GLA_WIDTH // GLA_HEADS
GLA_RANK = 16
GLA_TAU = 16.0
GLA_CHUNK = 64
DSA_WIDTH = D_MIX - GLA_WIDTH
DSA_HEADS = 8
DSA_DH = DSA_WIDTH // DSA_HEADS
DSA_PATTERN = ((128, 1), (512, 4), (2048, 16))
DSA_BLOCK = 128
REL_BUCKETS = 32
REL_MAX_DIST = 2048
D_FF_2 = 4 * D_MODEL
EPS = 1e-6
NEG = -1e30

IN_SPLITS = (
    GLA_HEADS * GLA_DK,
    GLA_HEADS * GLA_DK,
    GLA_WIDTH,
    GLA_WIDTH,
    GLA_RANK,
    DSA_WIDTH,
    DSA_WIDTH,
    DSA_WIDTH,
)
D_IN = sum(IN_SPLITS)


def rmsnorm(x, g):
    xf = x.astype(jnp.float32)
    y = xf * lax.rsqrt(jnp.mean(xf * xf, axis=-1, keepdims=True) + EPS)
    return (y * g.astype(jnp.float32)).astype(x.dtype)

def t5_bucket(dist):
    max_exact = REL_BUCKETS // 2
    n = np.maximum(dist, 0)
    large = max_exact + (np.log(np.maximum(n, 1) / max_exact)
                         / math.log(REL_MAX_DIST / max_exact)
                         * (REL_BUCKETS - max_exact)).astype(np.int32)
    large = np.minimum(large, REL_BUCKETS - 1)
    return np.where(n < max_exact, n, large).astype(np.int32)

def gla_mixer(q, k, v, glog):
    B, S, H, dk = q.shape
    dv = v.shape[-1]
    C = GLA_CHUNK
    n = S // C
    f32 = jnp.float32
    q = (q.astype(f32) * dk ** -0.5).reshape(B, n, C, H, dk)
    k = k.astype(f32).reshape(B, n, C, H, dk)
    v = v.astype(f32).reshape(B, n, C, H, dv)
    b = jnp.cumsum(glog.astype(f32).reshape(B, n, C, H, dk), axis=2)
    b_last = b[:, :, -1]
    q_dec = q * jnp.exp(b)
    k_inv = k * jnp.exp(-b)
    k_end = k * jnp.exp(b_last[:, :, None] - b)
    causal = jnp.tril(jnp.ones((C, C), dtype=bool))
    att = jnp.einsum('bnihk,bnjhk->bnhij', q_dec, k_inv)
    att = jnp.where(causal, att, 0.0)
    o_intra = jnp.einsum('bnhij,bnjhv->bnihv', att, v)
    inc = jnp.einsum('bnjhk,bnjhv->bnhkv', k_end, v)

    def step(state, inp):
        decay, upd = inp
        return decay[..., None] * state + upd, state

    _, s_prev = lax.scan(step, jnp.zeros((B, H, dk, dv), f32),
                         (jnp.exp(b_last).swapaxes(0, 1), inc.swapaxes(0, 1)))
    s_prev = s_prev.swapaxes(0, 1)
    o_inter = jnp.einsum('bnihk,bnhkv->bnihv', q_dec, s_prev)
    return (o_intra + o_inter).reshape(B, S, H, dv)

def dilated_branch(q, k, v, rel_bias, window, dilation):
    B, S, H, Dh = q.shape
    L = DSA_BLOCK
    span = window // dilation
    unit = dilation * L
    Sp = -(-S // unit) * unit
    n = Sp // dilation
    nb = n // L
    f32 = jnp.float32

    def to_sub(t):
        t = jnp.pad(t, ((0, 0), (0, Sp - S), (0, 0), (0, 0)))
        return t.reshape(B, n, dilation, H, Dh).transpose(0, 2, 3, 1, 4)

    def band(t):
        tb = jnp.pad(t, ((0, 0), (0, 0), (0, 0), (L, 0), (0, 0))).reshape(B, dilation, H, nb + 1, L, Dh)
        return jnp.concatenate([tb[:, :, :, :-1], tb[:, :, :, 1:]], axis=4)

    qb = to_sub(q).reshape(B, dilation, H, nb, L, Dh)
    kb = band(to_sub(k))
    vb = band(to_sub(v))

    steps = L + np.arange(L)[:, None] - np.arange(2 * L)[None, :]
    in_band = (steps >= 0) & (steps <= span)
    key_idx = np.arange(nb)[:, None, None] * L + np.arange(2 * L)[None, None, :] - L
    mask = jnp.asarray(in_band[None] & (key_idx >= 0))
    bias = jnp.transpose(rel_bias[t5_bucket(steps * dilation)], (2, 0, 1)).astype(f32)

    s = jnp.einsum('bdhcqe,bdhcke->bdhcqk', qb, kb).astype(f32) + bias[:, None]
    s = jnp.where(mask, s, NEG)
    m = jnp.max(s, axis=-1, keepdims=True)
    p = jnp.exp(s - m)
    den = jnp.sum(p, axis=-1, keepdims=True)
    o = jnp.einsum('bdhcqk,bdhcke->bdhcqe', p, vb.astype(f32)) / den
    lse = (m + jnp.log(den))[..., 0]
    o = o.reshape(B, dilation, H, n, Dh).transpose(0, 3, 1, 2, 4).reshape(B, Sp, H, Dh)[:, :S]
    lse = lse.reshape(B, dilation, H, n).transpose(0, 3, 1, 2).reshape(B, Sp, H)[:, :S]
    return o, lse

def dilated_mixer(q, k, v, rel_bias):
    q = q * DSA_DH ** -0.5
    outs, lses = [], []
    for window, dilation in DSA_PATTERN:
        o, lse = dilated_branch(q, k, v, rel_bias, window, dilation)
        outs.append(o)
        lses.append(lse)
    w = jax.nn.softmax(jnp.stack(lses, axis=0), axis=0)
    return jnp.sum(w[..., None] * jnp.stack(outs, axis=0), axis=0)

def second_inputs(seed: int = 0) -> dict:
    key = jax.random.key(seed)
    ks = jax.random.split(key, 16)
    f32 = jnp.float32
    nrm = lambda k, shape, scale: jax.random.normal(k, shape, f32) * scale
    return {
        "x": jax.random.normal(ks[0], (BATCH, SEQ, D_MODEL), f32),
        "attn_norm_g": 1.0 + nrm(ks[1], (DEPTH_2, D_MODEL), 0.02),
        "w_in": nrm(ks[2], (DEPTH_2, D_MODEL, D_IN), D_MODEL ** -0.5),
        "gla_gate_w2": nrm(ks[3], (DEPTH_2, GLA_RANK, GLA_HEADS * GLA_DK), GLA_RANK ** -0.5),
        "gla_gate_b": nrm(ks[4], (DEPTH_2, GLA_HEADS * GLA_DK), 0.1),
        "gla_norm_g": 1.0 + nrm(ks[5], (DEPTH_2, GLA_WIDTH), 0.02),
        "rel_bias": nrm(ks[6], (REL_BUCKETS, DSA_HEADS), 0.1),
        "w_out": nrm(ks[7], (DEPTH_2, D_MIX, D_MODEL), D_MIX ** -0.5),
        "mlp_norm_g": 1.0 + nrm(ks[8], (DEPTH_2, D_MODEL), 0.02),
        "w_ff1": nrm(ks[9], (DEPTH_2, D_MODEL, D_FF_2), D_MODEL ** -0.5),
        "w_ff2": nrm(ks[10], (DEPTH_2, D_FF_2, D_MODEL), D_FF_2 ** -0.5),
        "final_norm_g": 1.0 + nrm(ks[11], (D_MODEL,), 0.02),
    }

def second_block(x, attn_norm_g, w_in, gla_gate_w2, gla_gate_b, gla_norm_g, rel_bias,
              w_out, mlp_norm_g, w_ff1, w_ff2, final_norm_g):
    B, S, _ = x.shape
    split_at = [int(i) for i in np.cumsum(IN_SPLITS)[:-1]]
    h = x
    for l in range(DEPTH_2):
        nx = rmsnorm(h, attn_norm_g[l])
        proj = jnp.einsum('bsd,dp->bsp', nx, w_in[l])
        gq, gk, gv, gr, glow, dq, dk_, dv_ = jnp.split(proj, split_at, axis=-1)

        gate_pre = (jnp.einsum('bsr,rk->bsk', glow, gla_gate_w2[l]) + gla_gate_b[l]).astype(jnp.float32)
        glog = jax.nn.log_sigmoid(gate_pre) / GLA_TAU
        o_a = gla_mixer(gq.reshape(B, S, GLA_HEADS, GLA_DK),
                        gk.reshape(B, S, GLA_HEADS, GLA_DK),
                        gv.reshape(B, S, GLA_HEADS, GLA_DV),
                        glog.reshape(B, S, GLA_HEADS, GLA_DK))
        o_a = o_a * lax.rsqrt(jnp.mean(o_a * o_a, axis=-1, keepdims=True) + EPS)
        o_a = o_a * gla_norm_g[l].astype(jnp.float32).reshape(GLA_HEADS, GLA_DV)
        o_a = o_a.reshape(B, S, GLA_WIDTH) * jax.nn.silu(gr.astype(jnp.float32))

        o_b = dilated_mixer(dq.reshape(B, S, DSA_HEADS, DSA_DH),
                            dk_.reshape(B, S, DSA_HEADS, DSA_DH),
                            dv_.reshape(B, S, DSA_HEADS, DSA_DH),
                            rel_bias).reshape(B, S, DSA_WIDTH)

        mixed = jnp.concatenate([o_a, o_b], axis=-1).astype(h.dtype)
        h = h + jnp.einsum('bsm,md->bsd', mixed, w_out[l])

        nm = rmsnorm(h, mlp_norm_g[l])
        a = jnp.square(jax.nn.relu(jnp.einsum('bsd,df->bsf', nm, w_ff1[l])))
        h = h + jnp.einsum('bsf,fd->bsd', a, w_ff2[l])
    return rmsnorm(h, final_norm_g)


def setup_inputs(seed=0):
    out = dict(first_inputs(seed))
    for name, value in second_inputs(seed + 1).items():
        if name != "x":
            out[name + "_2"] = value
    return out


def reference(
    x, meta_tokens, ln_ffn1, ffn1_w_gu, ffn1_w_down, ln_mix, conv_w_in, conv_w, conv_w_out,
    attn_w_qkv, attn_lambda, attn_subln_g, attn_w_o, ln_ffn2, ffn2_w_gu, ffn2_w_down,
    attn_norm_g_2, w_in_2, gla_gate_w2_2, gla_gate_b_2, gla_norm_g_2, rel_bias_2, w_out_2,
    mlp_norm_g_2, w_ff1_2, w_ff2_2, final_norm_g_2,
):
    x = first_block(
        x, meta_tokens, ln_ffn1, ffn1_w_gu, ffn1_w_down, ln_mix, conv_w_in, conv_w, conv_w_out,
        attn_w_qkv, attn_lambda, attn_subln_g, attn_w_o, ln_ffn2, ffn2_w_gu, ffn2_w_down,
    )
    return second_block(
        x, attn_norm_g_2, w_in_2, gla_gate_w2_2, gla_gate_b_2, gla_norm_g_2, rel_bias_2,
        w_out_2, mlp_norm_g_2, w_ff1_2, w_ff2_2, final_norm_g_2,
    )


_drawn_inputs = setup_inputs


def setup_inputs(seed=0):
    import zlib

    import numpy as np

    out = dict(_drawn_inputs(seed))
    spreads = {}
    factors = {'attn_subln_g': 4.401,
     'ln_ffn2': 2.945,
     'attn_norm_g_2': 5.919,
     'gla_gate_b_2': 5.355,
     'gla_norm_g_2': 21.641,
     'rel_bias_2': 64.294,
     'mlp_norm_g_2': 14.701,
     'final_norm_g_2': 2.677}
    for name, (base, spread) in spreads.items():
        noise = np.random.default_rng([zlib.crc32(name.encode()), seed]).standard_normal(out[name].shape)
        drawn = base * np.exp(spread * noise) if base else spread * noise
        out[name] = __import__('jax').numpy.asarray(drawn.astype(out[name].dtype))
    for name, factor in factors.items():
        out[name] = (out[name] * factor).astype(out[name].dtype)
    return out
```

```python
import math
from contextlib import ExitStack

import numpy as np
import concourse.bass as bass
from concourse import mybir

F32 = mybir.dt.float32
F32R = mybir.dt.float32r
ALU = mybir.AluOpType
ACT = mybir.ActivationFunctionType
AX = mybir.AxisListType

P = 128
D = 1024
KD = D // P
META = 16
SEQ = 256
T = META + SEQ
D_FF = 2816
KF = D_FF // P
D_FF2 = 4096
KF2 = D_FF2 // P
HEADS = 8
QT = SEQ // P
LAMBDA_INIT = 0.8 - 0.6 * math.exp(-0.3 * 1)
NORM_EPS, SUBLN_EPS = 1e-6, 1e-5
NEG = -1e30
ROT_HALF = 8
GLA_HEADS, GLA_CHUNK, GLA_TAU = 4, 64, 16.0
LN_EXP_SET = "natural_log_exp_and_others"

GU_T, DN_T, TRI_T, PROJ_T, FF_T = 2 * KD, KF, 3 * KD, 2 * KD, 2 * KD
RAW, SPLIT = 4, 2
SLOT = TRI_T * P
GU_N, DN_N, TRI_N, PROJ_N, FF1_N, FF2_N = KF, KD, KD, KD // 2, KF2 // 2, 2 * KD

STREAM = [
    ("gu0", GU_N, GU_T), ("dn0", DN_N, DN_T),
    ("conv_in", TRI_N, TRI_T), ("conv_out", PROJ_N, PROJ_T),
    ("gu1", GU_N, GU_T), ("dn1", DN_N, DN_T),
    ("gu2", GU_N, GU_T), ("dn2", DN_N, DN_T),
    ("qkv", TRI_N, TRI_T), ("attn_out", PROJ_N, PROJ_T),
    ("gu3", GU_N, GU_T), ("dn3", DN_N, DN_T),
    ("mix_in", TRI_N, TRI_T), ("mix_out", PROJ_N, PROJ_T),
    ("ff1", FF1_N, FF_T), ("ff2", FF2_N, FF_T),
]
FIRST = {}
WIDTH = []
for _name, _n, _t in STREAM:
    FIRST[_name] = len(WIDTH)
    WIDTH += [_t * P] * _n
BLOCKS = len(WIDTH)

COL = {}
_at = 0
for _name, _n in [("ffn1_pre0", 8), ("ffn1_post0", 8), ("mix_pre0", 8), ("mix_post0", 8), ("ffn2_pre0", 8),
                  ("ffn2_post0", 8), ("ffn1_pre1", 8), ("ffn1_post1", 8), ("mix_pre1", 8), ("mix_post1", 8),
                  ("ffn2_pre1", 8), ("ffn2_post1", 8), ("attn_norm", 8), ("mlp_norm", 8), ("final_norm", 8),
                  ("conv_w", 24), ("subln", 1), ("gla_norm", 4), ("lambda", 4)]:
    COL[_name] = _at
    _at += _n
PARAMS = _at


def shape_constants():
    ident = np.eye(P, dtype=np.float32)
    rotate = np.zeros((P, P), np.float32)
    for c in range(2):
        for i in range(ROT_HALF):
            a, b = 64 * c + i, 64 * c + ROT_HALF + i
            rotate[b, a] = -1.0
            rotate[a, b] = 1.0
    j, i = np.arange(P)[:, None], np.arange(P)[None, :]
    same = j // GLA_CHUNK == i // GLA_CHUNK
    upto = (same & (j <= i)).astype(np.float32) / np.float32(GLA_TAU)
    after = (same & (j > i)).astype(np.float32) / np.float32(GLA_TAU)
    squares = np.concatenate([ident, rotate, upto, after], axis=1)

    pos = np.arange(T, dtype=np.float32)
    inv_freq = (np.float32(500000.0) ** (-np.arange(0, 16, 2, dtype=np.float32) / np.float32(16))).astype(np.float32)
    ang = pos[None, :] * inv_freq[:, None]
    cos, sin = np.ones((P, T), np.float32), np.zeros((P, T), np.float32)
    for c in range(2):
        for h in range(2):
            rows = slice(64 * c + ROT_HALF * h, 64 * c + ROT_HALF * (h + 1))
            cos[rows], sin[rows] = np.cos(ang), np.sin(ang)
    q, k = np.arange(P)[:, None], np.arange(T)[None, :]
    mask = np.where(k <= META + P + q, 0.0, NEG).astype(np.float32)
    rope_mask = np.concatenate([cos, sin, mask, mask], axis=1)

    d = np.arange(512) - (SEQ - 1)
    n = np.maximum(d, 0)
    large = 16 + (np.log(np.maximum(n, 1) / 16) / math.log(2048 / 16) * 16).astype(np.int32)
    bucket = np.where(n < 16, n, np.minimum(large, 31)).astype(np.int32)
    count = np.zeros(512)
    for window, dilation in ((128, 1), (512, 4), (2048, 16)):
        count += (d >= 0) & (d % dilation == 0) & (d <= window)
    seen = (count > 0) & (d < SEQ)
    onehot = np.zeros((P, 512), np.float32)
    onehot[bucket[seen], np.arange(512)[seen]] = 1.0
    weight = np.where(seen, np.log(np.maximum(count, 1)), NEG).astype(np.float32)
    weight = np.broadcast_to(weight, (HEADS, 512)).copy()
    return squares, rope_mask, onehot, weight


def two_blocks(nc, w, params, h_in, squares, rope_mask, onehot, weight, w_glow, gate_w, rel_bias, out):
    with ExitStack() as ctx:
        def sb(name, shape, dt=F32, at=ctx):
            return at.enter_context(nc.sbuf_tensor(name, shape, dt))

        def sem(name):
            return ctx.enter_context(nc.semaphore(name))

        w_raw = [sb(f"w_raw{i}", [P, SLOT]) for i in range(RAW)]
        w_hi = [sb(f"w_hi{i}", [P, SLOT], F32R) for i in range(SPLIT)]
        w_lo = [sb(f"w_lo{i}", [P, SLOT], F32R) for i in range(SPLIT)]
        x_hi = sb("x_hi", [P, KD, T], F32R)
        x_lo = sb("x_lo", [P, KD, T], F32R)
        h = sb("h", [P, KD, T])
        fx = sb("fx", [P, KD, T])
        par = sb("par", [P, PARAMS])
        sq4 = sb("sq4", [P, 4 * P])
        ident, rotate, upto, after = (sq4[:, P * i:P * (i + 1)] for i in range(4))
        ones = sb("ones", [P, P])
        ms = sb("ms", [P, T])
        r0 = sb("r0", [P, T])
        rstd = sb("rstd", [P, T])
        small = sb("small", [P, 32])
        with ExitStack() as s:
            act_out = sb("act_out", [P, 2 * SEQ], at=s)
            hid = [sb(f"hid{i}", [P, 2 * SEQ], at=s) for i in range(2)]
        with ExitStack() as s:
            square = [sb(f"square{i}", [P, T], at=s) for i in range(2)]
            sumsq = sb("sumsq", [P, T], at=s)
            scaled = [sb(f"scaled{i}", [P, T], at=s) for i in range(2)]
        sb("shared_by_both", [P, 3 * 2 * SEQ])
        with ExitStack() as s:
            hid_hi = sb("hid_hi", [P, KF2 * SEQ], F32R, at=s)
            hid_lo = sb("hid_lo", [P, KF2 * SEQ], F32R, at=s)
        with ExitStack() as s:
            y_hi = sb("y_hi", [P, KD, T], F32R, at=s)
            y_lo = sb("y_lo", [P, KD, T], F32R, at=s)
            cv_c = sb("cv_c", [P, T], at=s)
            cv_u = sb("cv_u", [P, T + 2], at=s)
            cv_a = sb("cv_a", [P, T], at=s)
            cv_y = sb("cv_y", [P, T], at=s)
        with ExitStack() as s:
            q_rot = sb("q_rot", [P, HEADS, SEQ], at=s)
            k_rot = sb("k_rot", [P, HEADS, 2, T], at=s)
            v_tok = sb("v_tok", [P, HEADS, 3, P], at=s)
            v_sb = [sb(f"v_sb{i}", [P, T], at=s) for i in range(2)]
            q_sb = [sb(f"q_sb{i}", [P, SEQ], at=s) for i in range(2)]
            k_sb = [sb(f"k_sb{i}", [P, T], at=s) for i in range(2)]
            tabs = sb("tabs", [P, 4 * T], at=s)
            cos_t, sin_t = tabs[:, 0:T], tabs[:, T:2 * T]
            mask = tabs[:, 2 * T:4 * T].rearrange("p (c k) -> p c k", c=2)
            with ExitStack() as s2:
                rope_s = sb("rope_s", [P, T], at=s2)
                rope_c = sb("rope_c", [P, T], at=s2)
            with ExitStack() as s2:
                s_sb = sb("s_sb", [P, 2, 2, T], at=s2)
                a_sb = sb("a_sb", [P, 2, T], at=s2)
                a_tok = sb("a_tok", [P, 5, P], at=s2)
            with ExitStack() as s2:
                sub_sq = sb("sub_sq", [P, 512], at=s2)
                sub_ms = sb("sub_ms", [P, 512], at=s2)
                sub_r0 = sb("sub_r0", [P, 512], at=s2)
                sub_r = sb("sub_r", [P, 512], at=s2)
        with ExitStack() as s:
            proj = sb("proj", [P, 3 * TRI_N, SEQ], at=s)
            bias = sb("bias", [P, HEADS, SEQ], at=s)
            gv_tok = sb("gv_tok", [P, QT, 4 * P], at=s)
            dv_tok = sb("dv_tok", [P, QT, 4 * P], at=s)
            w_glow_sb = sb("w_glow_sb", [P, KD, 16], at=s)
            gate_w_sb = sb("gate_w_sb", [P, SEQ], at=s)
            glow = sb("glow", [P, SEQ], at=s)
            with ExitStack() as s2:
                onehot_sb = sb("onehot_sb", [P, 512], at=s2)
                weight_sb = sb("weight_sb", [HEADS, 512], at=s2)
                by_dist = sb("by_dist", [HEADS, 512], at=s2)
                rel_sb = sb("rel_sb", [P, HEADS], at=s2)
            with ExitStack() as s2:
                g_a = sb("g_a", [P, QT, SEQ], at=s2)
                g_ls = sb("g_ls", [P, QT, SEQ], at=s2)
                g_eb = sb("g_eb", [P, QT, SEQ], at=s2)
                g_et = sb("g_et", [P, QT, SEQ], at=s2)
                g_q = sb("g_q", [P, GLA_HEADS, SEQ], at=s2)
                g_k = sb("g_k", [P, 2, SEQ], at=s2)
                g_s = sb("g_s", [P, 3, 2, SEQ], at=s2)
            with ExitStack() as s2:
                d_k = [sb(f"d_k{i}", [P, SEQ], at=s2) for i in range(2)]
                d_s = sb("d_s", [P, 3 * P], at=s2)
                d_p = sb("d_p", [P, 3 * P], at=s2)
                d_pt = sb("d_pt", [P, 3, P], at=s2)
            with ExitStack() as s2:
                n_sq = sb("n_sq", [P, GLA_HEADS, SEQ], at=s2)
                n_r0 = sb("n_r0", [P, GLA_HEADS, SEQ], at=s2)
                n_r = sb("n_r", [P, GLA_HEADS, SEQ], at=s2)
                n_ms = sb("n_ms", [P, GLA_HEADS, SEQ], at=s2)
        GQ, GK, GV, GR, DQ, DK, DV = 0, 2, 4, 8, 12, 16, 20
        g_ke = proj[:, GV:GV + 4, :].rearrange("p (t c) s -> p t c s", t=2)
        g_att = proj[:, DV:DV + 4, :].rearrange("p a s -> p (a s)").rearrange("p (n i) -> p n i", n=8)

        by_dist_dram = nc.dram_tensor("by_dist_dram", [HEADS, 512], F32, kind="Internal").ap()
        ps = ctx.enter_context(nc.psum_tensor("ps", [P, 8, 512], F32))
        SUM = 6

        landed = [sem(f"landed{i}") for i in range(RAW)]
        hi_ready, lo_ready, block_used = sem("hi_ready"), sem("lo_ready"), sem("block_used")
        h_loaded, consts_loaded, ones_ready = sem("h_loaded"), sem("consts_loaded"), sem("ones_ready")
        h_sq_ready, h_sq_summed, sumsq_summed = sem("h_sq_ready"), sem("h_sq_summed"), sem("sumsq_summed")
        ms_ready, ln_ready, r0_ready, newton, rstd_ready = (
            sem("ms_ready"), sem("ln_ready"), sem("r0_ready"), sem("newton"), sem("rstd_ready"))
        xn_ready, x_hi_ready, x_lo_ready = sem("xn_ready"), sem("x_hi_ready"), sem("x_lo_ready")
        scaled_ready, h_ready = sem("scaled_ready"), sem("h_ready")
        act_ready, hid_ready, hid_hi_ready, hid_lo_ready = (
            sem("act_ready"), sem("hid_ready"), sem("hid_hi_ready"), sem("hid_lo_ready"))
        f_sq_ready, f_ready, sumsq_ready = sem("f_sq_ready"), sem("f_ready"), sem("sumsq_ready")
        cv_c_ready, cv_u_ready, cv_a_ready, cv_step, cv_y_ready, cv_hi_ready, cv_lo_ready = (
            sem("cv_c_ready"), sem("cv_u_ready"), sem("cv_a_ready"), sem("cv_step"), sem("cv_y_ready"),
            sem("cv_hi_ready"), sem("cv_lo_ready"))
        tabs_loaded, k_zeroed, part_done, part_copied = (
            sem("tabs_loaded"), sem("k_zeroed"), sem("part_done"), sem("part_copied"))
        rotated, v_turned, v_tok_ready, rope_step = (
            sem("rotated"), sem("v_turned"), sem("v_tok_ready"), sem("rope_step"))
        lam_step, lam_sum, lam_exp = sem("lam_step"), sem("lam_sum"), sem("lam_exp")
        scores_done, s_ready, max_step, exp_ready, rs_step, a_step, a_turned, a_tok_ready, o_done, o_copied = (
            sem("scores_done"), sem("s_ready"), sem("max_step"), sem("exp_ready"), sem("rs_step"), sem("a_step"),
            sem("a_turned"), sem("a_tok_ready"), sem("o_done"), sem("o_copied"))
        sub_sq_ready, sub_summed, sub_step, sub_ln, sub_r0_ready, sub_y_ready, out_hi_ready, out_lo_ready = (
            sem("sub_sq_ready"), sem("sub_summed"), sem("sub_step"), sem("sub_ln"), sem("sub_r0_ready"),
            sem("sub_y_ready"), sem("out_hi_ready"), sem("out_lo_ready"))
        mix_loaded, mix_zeroed, proj_copied = sem("mix_loaded"), sem("mix_zeroed"), sem("proj_copied")
        dist_done, dist_ready, dist_stored, bias_loaded = (
            sem("dist_done"), sem("dist_ready"), sem("dist_stored"), sem("bias_loaded"))
        g_pe, g_act, g_dve, g_pool = sem("g_pe"), sem("g_act"), sem("g_dve"), sem("g_pool")
        d_k_ready, d_scores, d_s_ready, d_max_step, d_exp, d_p_step, d_turned, d_pt_ready, d_o_done, d_o_copied = (
            sem("d_k_ready"), sem("d_scores"), sem("d_s_ready"), sem("d_max_step"), sem("d_exp"), sem("d_p_step"),
            sem("d_turned"), sem("d_pt_ready"), sem("d_o_done"), sem("d_o_copied"))
        out_ready, stored = sem("out_ready"), sem("stored")

        HID_CREDIT, F_CREDIT, CV_CREDIT = 2, 4, 2

        SUB = [("ffn", "ffn1_pre0", "ffn1_post0", 0), ("conv", "mix_pre0", "mix_post0", None),
               ("ffn", "ffn2_pre0", "ffn2_post0", 1), ("ffn", "ffn1_pre1", "ffn1_post1", 2),
               ("attn", "mix_pre1", "mix_post1", None), ("ffn", "ffn2_pre1", "ffn2_post1", 3)]

        def first_col(u):
            return 0 if u <= 4 else META

        def loop(eng, count, body, peel=0):
            rounds = (count - peel) // 4
            if rounds > 1:
                with eng.Fori(0, rounds) as it:
                    for j in range(4):
                        body(it * 4 + j, j)
            else:
                rounds = 0
            for i in range(rounds * 4, count):
                body(i, i % 4)

        block = ctx.enter_context(nc.Block())

        @block.sync
        def _(sp):
            sp.dma_start(h[:, :, :], h_in).then_inc(h_loaded, 16)
            sp.dma_start(par[:, :], params).then_inc(consts_loaded, 16)
            sp.dma_start(sq4[:, :], squares).then_inc(consts_loaded, 16)
            for name, count, tiles in STREAM:
                n0 = FIRST[name]

                def load(i, j):
                    slot = (n0 + j) % RAW
                    if not (isinstance(i, int) and n0 + i < RAW):
                        sp.wait_ge(lo_ready, i + (n0 - RAW + 1))
                    src = w[name][i, :, :] if isinstance(i, int) else w[name][bass.ds(i, 1), :, :].rearrange("a p c -> (a p) c")
                    sp.dma_start(w_raw[slot][:, 0:tiles * P], src).then_inc(landed[slot], 16)

                if n0 == 0:
                    for i in range(RAW):
                        load(i, i)
                    rounds = (count - RAW) // 4
                    with sp.Fori(1, 1 + rounds) as it:
                        for j in range(4):
                            load(it * 4 + j, j)
                    for i in range(4 + rounds * 4, count):
                        load(i, i % 4)
                else:
                    loop(sp, count, load)
            for k in range(KD):
                sp.wait_ge(out_ready, k + 1)
                sp.dma_start(out[k * P:(k + 1) * P, :], fx[:, k, META:T]).then_inc(stored, 16)
            sp.wait_ge(stored, 16 * KD)

        @block.gpsimd
        def _(pool):
            pool.memset(ones[:, :], 1.0).then_inc(ones_ready, 1)
            pool.wait_ge(block_used, FIRST["qkv"])
            pool.dma_start(tabs[:, :], rope_mask).then_inc(tabs_loaded, 16)
            pool.memset(k_rot[:, :, :, :], 0.0).then_inc(k_zeroed, 1)
            pool.memset(v_tok[:, :, 0, :], 0.0).then_inc(k_zeroed, 1)
            pool.memset(a_tok[:, :, :], 0.0).then_inc(k_zeroed, 1)
            pool.wait_ge(block_used, FIRST["mix_in"])
            pool.memset(rel_sb[:, :], 0.0).then_inc(mix_zeroed, 1)
            pool.memset(gate_w_sb[:, :], 0.0).then_inc(mix_zeroed, 1)
            pool.memset(glow[:, :], 0.0).then_inc(mix_zeroed, 1)
            pool.wait_ge(mix_zeroed, 3)
            pool.memset(glow[32:33, :], 1.0).then_inc(mix_zeroed, 1)
            pool.dma_start(onehot_sb[:, :], onehot).then_inc(mix_loaded, 16)
            pool.dma_start(weight_sb[:, :], weight).then_inc(mix_loaded, 16)
            pool.dma_start(rel_sb[0:32, :], rel_bias).then_inc(mix_loaded, 16)
            pool.dma_start(w_glow_sb[:, :, :], w_glow).then_inc(mix_loaded, 16)
            pool.dma_start(gate_w_sb[0:16, :], gate_w[0:16, :]).then_inc(mix_loaded, 16)
            pool.dma_start(gate_w_sb[32:33, :], gate_w[16:17, :]).then_inc(mix_loaded, 16)
            pool.wait_ge(dist_ready, 1)
            pool.dma_start(by_dist_dram, by_dist[:, :]).then_inc(dist_stored, 16)
            pool.wait_ge(dist_stored, 16)
            toeplitz = bass.AP(tensor=by_dist_dram.tensor, offset=P, ap=[[1, P], [512, HEADS], [1, SEQ]])
            pool.dma_start(bias[:, :, :], toeplitz).then_inc(bias_loaded, 16)
            pool.memset(g_q[:, :, :], 0.0).then_inc(g_pool, 1)
            pool.wait_ge(g_act, 2)
            pool.memset(g_ke[:, :, :, :], 0.0).then_inc(g_pool, 1)
            pool.memset(g_att[:, :, :], 0.0).then_inc(g_pool, 1)
            pool.wait_ge(g_dve, 19)
            pool.affine_select(out=g_att, in_=g_att, compare_op=ALU.is_ge, fill=0.0, base=0,
                               pattern=[[0, 8], [1, P]], channel_multiplier=-1).then_inc(g_pool, 1)
            pool.wait_ge(g_dve, GD_DONE)
            pool.memset(d_k[0][:, :], 0.0).then_inc(g_pool, 1)
            pool.memset(d_k[1][:, :], 0.0).then_inc(g_pool, 1)

        @block.scalar
        def _(act):
            def split_hi(n, j, width):
                act.wait_ge(landed[j], (n // 4 + 1) * 16 if isinstance(n, int) else n * 4 + (16 - 4 * j))
                if not (isinstance(n, int) and n < SPLIT):
                    act.wait_ge(block_used, n - (SPLIT - 1))
                act.activation(w_hi[j % SPLIT][:, 0:width], w_raw[j][:, 0:width], ACT.Copy).then_inc(hi_ready, 1)

            def next_hi(name, count, i, j):
                n0 = FIRST[name]
                if isinstance(i, int):
                    if n0 + i + 2 < BLOCKS:
                        split_hi(n0 + i + 2, (n0 + i + 2) % 4, WIDTH[n0 + i + 2])
                else:
                    split_hi(i + (n0 + 2), (n0 + j + 2) % 4, WIDTH[n0])

            def root(s, c0):
                act.wait_ge(ms_ready, s + 1)
                act.activation(r0[:, c0:T], ms[:, c0:T], ACT.Ln).then_inc(ln_ready, 1)
                act.wait_ge(ln_ready, s + 1)
                act.activation(r0[:, c0:T], r0[:, c0:T], ACT.Exp, scale=-0.5).then_inc(r0_ready, 1)

            def pre_norm(q, s, c0, split=True):
                for k in range(KD):
                    if q == 0:
                        act.wait_ge(h_loaded, 16)
                    else:
                        act.wait_ge(h_ready, KD * (q - 1) + k + 1)
                    if KD * q + k >= 2:
                        act.wait_ge(h_sq_summed, KD * q + k - 1)
                    act.activation(square[k % 2][:, c0:T], h[:, k, c0:T], ACT.Square).then_inc(h_sq_ready, 1)
                root(s, c0)
                if split:
                    for k in range(KD):
                        act.wait_ge(xn_ready, KD * q + k + 1)
                        act.activation(x_hi[:, k, c0:T], fx[:, k, c0:T], ACT.Copy).then_inc(x_hi_ready, 1)

            def take_out(u, m, bank, c0, gain):
                act.wait_ge(sumsq_ready, 9 * u + m)
                act.activation(square[m % 2 if isinstance(m, int) else m_par[0]][:, c0:T], ps[:, bank, c0:T], ACT.Square).then_inc(f_sq_ready, 1)
                g = par[:, bass.ds(m + COL[gain], 1)]
                act.activation(fx[:, m if isinstance(m, int) else bass.ds(m, 1), c0:T], ps[:, bank, c0:T],
                               ACT.Copy, scale=g).then_inc(f_ready, 1)

            m_par = [0]

            def hidden(name, f, c0):
                n0, width = FIRST[name], T - c0

                def step(i, j):
                    act.wait_ge(block_used, i + (n0 + 1))
                    act.activation(act_out[:, 0:width], ps[:, 2 * (j % 2), c0:T], ACT.Silu).then_inc(act_ready, 1)
                    next_hi(name, GU_N, i, j)
                    act.wait_ge(hid_ready, i + (KF * f + 1 + HID_CREDIT))
                    at = i * T + c0
                    act.activation(hid_hi[:, bass.ds(at, width)], hid[j % 2][:, 0:width], ACT.Copy)\
                       .then_inc(hid_hi_ready, 1)

                loop(act, GU_N, step, peel=2)

            def out_projection(name, count, per, u, c0, gain):
                n0 = FIRST[name]

                def step(i, j):
                    act.wait_ge(block_used, i + (n0 + 1))
                    for s in range(per):
                        m_par[0] = (j * per + s) % 2
                        take_out(u, i * per + s, (j * per + s) % 4, c0, gain)
                    next_hi(name, count, i, j)

                loop(act, count - 1, step, peel=1)
                act.wait_ge(block_used, n0 + count)
                for s in range(per):
                    m = (count - 1) * per + s
                    take_out(u, m, m % 4, c0, gain)

            def convolution():
                n0 = FIRST["conv_in"]

                def step(i, j):
                    b = 3 * (j % 2)
                    act.wait_ge(block_used, i + (n0 + 1))
                    act.activation(cv_c[:, :], ps[:, b + 1, 0:T], ACT.Copy).then_inc(cv_c_ready, 1)
                    next_hi("conv_in", TRI_N, i, j)
                    act.wait_ge(cv_u_ready, i + 2)
                    act.activation(cv_a[:, :], cv_u[:, 0:T], ACT.Copy,
                                   scale=par[:, bass.ds(i + COL["conv_w"], 1)]).then_inc(cv_a_ready, 1)
                    act.wait_ge(cv_y_ready, i + (1 + CV_CREDIT))
                    act.activation(y_hi[:, i, :], cv_y[:, :], ACT.Copy).then_inc(cv_hi_ready, 1)

                loop(act, TRI_N, step, peel=2)

            def heads_in():
                n0 = FIRST["qkv"]
                for i in range(HEADS):
                    b, r = 3 * (i % 2), i % 2
                    act.wait_ge(part_done, 2 * i + 1)
                    if i >= 2:
                        act.wait_ge(v_turned, i - 1)
                    act.activation(v_sb[r][:, :], ps[:, b, 0:T], ACT.Copy).then_inc(part_copied, 1)
                    act.wait_ge(part_done, 2 * i + 2)
                    if i >= 2:
                        act.wait_ge(rope_step, 7 * (i - 1))
                    act.activation(q_sb[r][:, :], ps[:, b + 1, 0:SEQ], ACT.Copy, scale=0.125).then_inc(part_copied, 1)
                    act.wait_ge(block_used, n0 + i + 1)
                    act.activation(k_sb[r][:, :], ps[:, b + 2, 0:T], ACT.Copy).then_inc(part_copied, 1)
                    next_hi("qkv", TRI_N, i, i % 4)
                    act.wait_ge(v_turned, i + 1)
                    if i == 0:
                        act.wait_ge(k_zeroed, 3)
                    act.activation(v_tok[:, i, 1:3, :], ps[:, 7, 0:2 * P].rearrange("p (c v) -> p c v", c=2),
                                   ACT.Copy).then_inc(v_tok_ready, 1)
                    act.activation(v_tok[0:META, i, 0, :], ps[0:META, 7, 2 * P:3 * P], ACT.Copy).then_inc(v_tok_ready, 1)

            def softmax_heads():
                act.wait_ge(lam_sum, 1)
                act.activation(small[:, 2:4], ps[:, 0, 0:2], ACT.Exp).then_inc(lam_exp, 1)
                for i in range(HEADS):
                    for t in range(QT):
                        keys = META + P * (t + 1)
                        for c in range(2):
                            act.wait_ge(max_step, 4 * i + 2 * t + 2)
                            n = 4 * (i % 2) + 2 * t + c
                            act.activation(s_sb[:, t, c, 0:keys], s_sb[:, t, c, 0:keys], ACT.Exp,
                                           bias=small[:, 8 + n:9 + n], accum_out=small[:, 16 + n:17 + n])\
                               .then_inc(exp_ready, 1)
                    for t in range(QT):
                        act.wait_ge(a_turned, 2 * i + t + 1)
                        if t == 0:
                            if i >= 1:
                                act.wait_ge(o_done, i)
                            act.activation(a_tok[0:META, 0, :], ps[0:META, 7, 0:P], ACT.Copy).then_inc(a_tok_ready, 1)
                            act.activation(a_tok[:, 1, :], ps[:, 7, P:2 * P], ACT.Copy).then_inc(a_tok_ready, 1)
                        else:
                            act.activation(a_tok[0:META, 2, :], ps[0:META, 6, 0:P], ACT.Copy).then_inc(a_tok_ready, 1)
                            act.activation(a_tok[:, 3:5, :], ps[:, 6, P:3 * P].rearrange("p (c q) -> p c q", c=2),
                                           ACT.Copy).then_inc(a_tok_ready, 1)
                    act.wait_ge(o_done, i + 1)
                    act.activation(fx[:, i, META:T], ps[:, 7, SEQ:2 * SEQ], ACT.Copy).then_inc(o_copied, 1)

            def sub_norm():
                for g in range(4):
                    o2 = fx[:, 2 * g:2 * g + 2, META:T]
                    act.wait_ge(o_copied, HEADS)
                    if g == 0:
                        act.wait_ge(o_done, HEADS)
                        act.wait_ge(a_step, 4 * HEADS)
                    if g >= 1:
                        act.wait_ge(sub_summed, g)
                    act.activation(sub_sq[:, :].rearrange("p (c s) -> p c s", c=2), o2, ACT.Square).then_inc(sub_sq_ready, 1)
                    act.wait_ge(sub_step, 4 * g + 1)
                    act.activation(sub_r0[:, :], sub_ms[:, :], ACT.Ln).then_inc(sub_ln, 1)
                    act.wait_ge(sub_ln, g + 1)
                    act.activation(sub_r0[:, :], sub_r0[:, :], ACT.Exp, scale=-0.5).then_inc(sub_r0_ready, 1)
                    for i in (2 * g, 2 * g + 1):
                        act.wait_ge(sub_y_ready, i + 1)
                        act.activation(x_hi[:, i, META:T], fx[:, i, META:T], ACT.Copy).then_inc(out_hi_ready, 1)

            def mix_in():
                n0 = FIRST["mix_in"]
                for i in range(TRI_N):
                    act.wait_ge(block_used, n0 + i + 1)
                    act.activation(proj[:, 3 * i:3 * i + 3, :], ps[:, 3 * (i % 2):3 * (i % 2) + 3, 0:SEQ], ACT.Copy)\
                       .then_inc(proj_copied, 1)
                    if i < TRI_N - 1:
                        next_hi("mix_in", TRI_N, i, i % 4)

            def gated():
                act.wait_ge(g_pe, 2)
                act.activation(gv_tok[:, :, :], ps[:, 0:2, :], ACT.Copy).then_inc(g_act, 1)
                act.activation(dv_tok[:, :, :], ps[:, 2:4, :], ACT.Copy).then_inc(g_act, 1)
                act.wait_ge(g_pe, 3)
                act.activation(glow[0:16, :], ps[0:16, 4, 0:SEQ], ACT.Copy).then_inc(g_act, 1)
                act.wait_ge(g_pe, 4)
                act.wait_ge(dist_stored, 16)
                pre = ps[:, 5, :].rearrange("p (t f) -> p t f", t=2)
                act.activation(g_a[:, :, :], pre, ACT.Abs).then_inc(g_act, 1)
                act.wait_ge(g_act, 4)
                act.activation(g_a[:, :, :], g_a[:, :, :], ACT.Exp, scale=-1.0).then_inc(g_act, 1)
                act.wait_ge(g_act, 5)
                act.activation(g_a[:, :, :], g_a[:, :, :], ACT.Ln, bias=1.0).then_inc(g_act, 1)
                act.wait_ge(g_pe, 6)
                b_t = ps[:, 4, :].rearrange("p (c s) -> p c s", c=2)
                act.activation(g_eb[:, :, :], b_t, ACT.Exp).then_inc(g_act, 1)
                act.activation(g_a[:, :, :], b_t, ACT.Exp, scale=-1.0).then_inc(g_act, 1)
                act.activation(g_et[:, :, :], ps[:, 6, :].rearrange("p (t f) -> p t f", t=2), ACT.Exp).then_inc(g_act, 1)
                act.wait_ge(g_pe, 10)
                act.wait_ge(g_dve, 25)
                act.activation(n_sq[:, :, :].rearrange("p a s -> p (a s)").rearrange("p (b s) -> p b s", b=2),
                               ps[:, 4:6, :], ACT.Square).then_inc(g_act, 1)
                act.wait_ge(g_dve, 26)
                act.activation(n_r0[:, :, :], n_ms[:, :, :], ACT.Ln).then_inc(g_act, 1)
                act.wait_ge(g_act, 11)
                act.activation(n_r0[:, :, :], n_r0[:, :, :], ACT.Exp, scale=-0.5).then_inc(g_act, 1)
                act.preload_act_table(ACT.Silu)
                act.activation(proj[:, GR:GR + 4, :], proj[:, GR:GR + 4, :], ACT.Silu).then_inc(g_act, 1)
                act.preload_act_table_set(LN_EXP_SET)

            def dilated():
                for i in range(HEADS):
                    for t in range(QT):
                        a, b = (0, P) if t == 0 else (P, 3 * P)
                        act.wait_ge(d_max_step, 4 * i + 2 * t + 2)
                        n = 2 * (i % 2) + t
                        act.activation(d_s[:, a:b], d_s[:, a:b], ACT.Exp, bias=small[:, 8 + n:9 + n],
                                       accum_out=small[:, 16 + n:17 + n]).then_inc(d_exp, 1)
                    act.wait_ge(d_turned, i + 1)
                    if i >= 1:
                        act.wait_ge(d_o_done, i)
                    act.activation(d_pt[:, :, :], ps[:, 2, 0:3 * P].rearrange("p (c q) -> p c q", c=3), ACT.Copy)\
                       .then_inc(d_pt_ready, 1)
                    act.wait_ge(d_o_done, i + 1)
                    half = slice(64 * (i % 2), 64 * (i % 2) + 64)
                    act.activation(fx[half, 4 + i // 2, META:T], ps[half, 3, 0:SEQ], ACT.Copy).then_inc(d_o_copied, 1)
                for k in range(KD):
                    if k < 4:
                        act.wait_ge(g_dve, GD_DONE - 3 + k)
                    else:
                        act.wait_ge(d_o_copied, 2 * (k - 3))
                    act.activation(x_hi[:, k, META:T], fx[:, k, META:T], ACT.Copy).then_inc(out_hi_ready, 1)

            def wide_hidden():
                n0 = FIRST["ff1"]

                def step(i, j):
                    act.wait_ge(block_used, i + (n0 + 1))
                    act.activation(act_out[:, :].rearrange("p (c s) -> p c s", c=2),
                                   ps[:, 2 * (j % 2):2 * (j % 2) + 2, 0:SEQ], ACT.Relu).then_inc(act_ready, 1)
                    next_hi("ff1", FF1_N, i, j)
                    act.wait_ge(hid_ready, i + (4 * KF + 1 + HID_CREDIT))
                    act.activation(hid_hi[:, bass.ds(i * 2 * SEQ, 2 * SEQ)], hid[j % 2][:, :], ACT.Copy)\
                       .then_inc(hid_hi_ready, 1)

                loop(act, FF1_N, step, peel=2)

            act.preload_act_table_set(LN_EXP_SET)
            split_hi(0, 0, WIDTH[0])
            split_hi(1, 1, WIDTH[1])
            act.wait_ge(consts_loaded, 32)
            s = 0
            for u, (kind, pre, post, f) in enumerate(SUB):
                c0 = first_col(u)
                pre_norm(u, s, c0)
                s += 1
                if u > 0:
                    n = FIRST[{0: "gu0", 1: "conv_in", 2: "gu1", 3: "gu2", 4: "qkv", 5: "gu3"}[u]] + 1
                    split_hi(n, n % 4, WIDTH[n])
                if kind == "ffn":
                    act.preload_act_table(ACT.Silu)
                    hidden(f"gu{f}", f, c0)
                    act.preload_act_table_set(LN_EXP_SET)
                    out_projection(f"dn{f}", DN_N, 1, u, c0, post)
                elif kind == "conv":
                    convolution()
                    out_projection("conv_out", PROJ_N, 2, u, c0, post)
                else:
                    c0 = META
                    heads_in()
                    softmax_heads()
                    sub_norm()
                    out_projection("attn_out", PROJ_N, 2, u, c0, post)
                root(s, c0)
                s += 1
            pre_norm(6, s, META)
            s += 1
            n = FIRST["mix_in"] + 1
            split_hi(n, n % 4, WIDTH[n])
            mix_in()
            gated()
            dilated()
            n = FIRST["mix_out"] + 1
            split_hi(n, n % 4, WIDTH[n])
            for i in range(PROJ_N - 1):
                next_hi("mix_out", PROJ_N, i, i % 4)
            pre_norm(7, s, META)
            s += 1
            n = FIRST["ff1"] + 1
            split_hi(n, n % 4, WIDTH[n])
            wide_hidden()
            loop(act, FF2_N - 2, lambda i, j: next_hi("ff2", FF2_N, i, j), peel=0)
            pre_norm(8, s, META, split=False)

        @block.vector
        def _(dve):
            def split_lo(n, j, width):
                dve.wait_ge(hi_ready, n + 1)
                dve.tensor_tensor(w_lo[j % SPLIT][:, 0:width], w_raw[j][:, 0:width],
                                  w_hi[j % SPLIT][:, 0:width].bitcast(F32), ALU.subtract).then_inc(lo_ready, 1)

            def next_lo(name, count, i, j):
                n0 = FIRST[name]
                if isinstance(i, int):
                    if n0 + i + 2 < BLOCKS:
                        split_lo(n0 + i + 2, (n0 + i + 2) % 4, WIDTH[n0 + i + 2])
                else:
                    split_lo(i + (n0 + 2), (n0 + j + 2) % 4, WIDTH[n0])

            def root(s, c0, summed, count, eps):
                dve.wait_ge(summed, count)
                dve.tensor_scalar(ms[:, c0:T], ps[:, SUM, c0:T], 1.0 / D, eps, ALU.mult, ALU.add).then_inc(ms_ready, 1)
                dve.wait_ge(r0_ready, s + 1)
                dve.tensor_tensor(rstd[:, c0:T], r0[:, c0:T], r0[:, c0:T], ALU.mult).then_inc(newton, 1)
                dve.wait_ge(newton, 2 * s + 1)
                dve.scalar_tensor_tensor(out=rstd[:, c0:T], in0=rstd[:, c0:T], scalar=-0.5, in1=ms[:, c0:T],
                                         op0=ALU.mult, op1=ALU.mult).then_inc(newton, 1)
                dve.wait_ge(newton, 2 * s + 2)
                dve.scalar_tensor_tensor(out=rstd[:, c0:T], in0=rstd[:, c0:T], scalar=1.5, in1=r0[:, c0:T],
                                         op0=ALU.add, op1=ALU.mult).then_inc(rstd_ready, 1)
                dve.wait_ge(rstd_ready, s + 1)

            def normed(k, c0, gain, sem_):
                g = COL[gain] + k
                dve.scalar_tensor_tensor(out=fx[:, k, c0:T], in0=h[:, k, c0:T], scalar=par[:, g:g + 1],
                                         in1=rstd[:, c0:T], op0=ALU.mult, op1=ALU.mult).then_inc(sem_, 1)

            def pre_norm(q, s, c0, gain):
                root(s, c0, h_sq_summed, KD * (q + 1), NORM_EPS)
                for k in range(KD + 1):
                    if k < KD:
                        normed(k, c0, gain, xn_ready)
                    if k >= 1:
                        dve.wait_ge(x_hi_ready, KD * q + k)
                        dve.tensor_tensor(x_lo[:, k - 1, c0:T], fx[:, k - 1, c0:T],
                                          x_hi[:, k - 1, c0:T].bitcast(F32), ALU.subtract).then_inc(x_lo_ready, 1)

            def post_norm(u, s, c0, factor):
                root(s, c0, sumsq_summed, u + 1, NORM_EPS)
                for k in range(KD + 1):
                    if k < KD:
                        if k >= 2:
                            dve.wait_ge(h_ready, KD * u + k - 1)
                        dve.tensor_tensor(scaled[k % 2][:, c0:T], fx[:, k, c0:T], rstd[:, c0:T], ALU.mult)\
                           .then_inc(scaled_ready, 1)
                    if k >= 1:
                        dve.wait_ge(scaled_ready, KD * u + k)
                        dve.scalar_tensor_tensor(out=h[:, k - 1, c0:T], in0=scaled[(k - 1) % 2][:, c0:T], scalar=factor,
                                                 in1=h[:, k - 1, c0:T], op0=ALU.mult, op1=ALU.add).then_inc(h_ready, 1)
                dve.wait_ge(h_ready, KD * (u + 1))

            def hidden(name, f, c0):
                width = T - c0

                def step(i, j):
                    t = hid[j % 2][:, 0:width]
                    dve.wait_ge(act_ready, i + (KF * f + 1))
                    dve.tensor_tensor(t, act_out[:, 0:width], ps[:, 2 * (j % 2) + 1, c0:T], ALU.mult)\
                       .then_inc(hid_ready, 1)
                    next_lo(name, GU_N, i, j)
                    dve.wait_ge(hid_hi_ready, i + (KF * f + 1))
                    at = i * T + c0
                    dve.tensor_tensor(hid_lo[:, bass.ds(at, width)], t, hid_hi[:, bass.ds(at, width)].bitcast(F32),
                                      ALU.subtract).then_inc(hid_lo_ready, 1)

                loop(dve, GU_N, step, peel=2)

            def add_square(u, m, par_, c0):
                dve.wait_ge(f_sq_ready, m + (KD * u + 1))
                dve.wait_ge(sumsq_ready, m + (9 * u + 1))
                dve.tensor_tensor(sumsq[:, c0:T], sumsq[:, c0:T], square[par_][:, c0:T], ALU.add).then_inc(sumsq_ready, 1)

            def out_projection(name, count, per, u, c0):
                if u > 0:
                    dve.wait_ge(h_ready, KD * u)
                dve.wait_ge(hid_lo_ready, 1)
                dve.memset(sumsq[:, :], 0.0).then_inc(sumsq_ready, 1)

                def step(i, j):
                    for s in range(per):
                        add_square(u, i * per + s, (j * per + s) % 2, c0)
                    next_lo(name, count, i, j)

                loop(dve, count - 1, step, peel=1)
                for s in range(per):
                    m = (count - 1) * per + s
                    add_square(u, m, m % 2, c0)

            def convolution():
                dve.memset(cv_u[:, 0:2], 0.0).then_inc(cv_u_ready, 1)

                def step(i, j):
                    b = 3 * (j % 2)
                    w1 = par[:, bass.ds(i + (COL["conv_w"] + KD), 1)]
                    w2 = par[:, bass.ds(i + (COL["conv_w"] + 2 * KD), 1)]
                    dve.wait_ge(cv_c_ready, i + 1)
                    dve.tensor_tensor(cv_u[:, 2:T + 2], cv_c[:, :], ps[:, b + 2, 0:T], ALU.mult).then_inc(cv_u_ready, 1)
                    next_lo("conv_in", TRI_N, i, j)
                    dve.wait_ge(cv_a_ready, i + 1)
                    dve.scalar_tensor_tensor(out=cv_a[:, :], in0=cv_u[:, 1:T + 1], scalar=w1, in1=cv_a[:, :],
                                             op0=ALU.mult, op1=ALU.add).then_inc(cv_step, 1)
                    dve.wait_ge(cv_step, i * 2 + 1)
                    dve.scalar_tensor_tensor(out=cv_a[:, :], in0=cv_u[:, 2:T + 2], scalar=w2, in1=cv_a[:, :],
                                             op0=ALU.mult, op1=ALU.add).then_inc(cv_step, 1)
                    dve.wait_ge(cv_step, i * 2 + 2)
                    dve.tensor_tensor(cv_y[:, :], cv_a[:, :], ps[:, b, 0:T], ALU.mult).then_inc(cv_y_ready, 1)
                    dve.wait_ge(cv_hi_ready, i + 1)
                    dve.tensor_tensor(y_lo[:, i, :], cv_y[:, :], y_hi[:, i, :].bitcast(F32), ALU.subtract)\
                       .then_inc(cv_lo_ready, 1)

                loop(dve, TRI_N, step, peel=2)

            def lam():
                c = COL["lambda"]
                dve.wait_ge(k_zeroed, 3)
                dve.tensor_tensor(small[:, 0:2], par[:, c:c + 4:2], par[:, c + 1:c + 4:2], ALU.mult).then_inc(lam_step, 1)

            def heads_in():
                dve.wait_ge(tabs_loaded, 16)
                dve.wait_ge(k_zeroed, 3)
                for i in range(HEADS):
                    r = i % 2
                    n = 7 * i
                    dve.wait_ge(rotated, 2 * i + 1)
                    if i >= 1:
                        dve.wait_ge(rope_step, n)
                    dve.tensor_tensor(rope_s[:, 0:SEQ], sin_t[:, META:T], ps[:, 3 * r + 1, SEQ:2 * SEQ], ALU.mult).then_inc(rope_step, 1)
                    dve.tensor_tensor(rope_c[:, 0:SEQ], q_sb[r][:, :], cos_t[:, META:T], ALU.mult).then_inc(rope_step, 1)
                    dve.wait_ge(rope_step, n + 2)
                    dve.tensor_tensor(q_rot[:, i, :], rope_s[:, 0:SEQ], rope_c[:, 0:SEQ], ALU.add).then_inc(rope_step, 1)
                    dve.wait_ge(rotated, 2 * i + 2)
                    dve.wait_ge(rope_step, n + 3)
                    dve.tensor_tensor(rope_s[:, :], sin_t, ps[:, 6, 0:T], ALU.mult).then_inc(rope_step, 1)
                    dve.tensor_tensor(rope_c[:, :], k_sb[r][:, :], cos_t, ALU.mult).then_inc(rope_step, 1)
                    dve.wait_ge(rope_step, n + 5)
                    for c in range(2):
                        rows = slice(64 * c, 64 * c + 64)
                        dve.tensor_tensor(k_rot[rows, i, c, :], rope_s[rows, :], rope_c[rows, :], ALU.add)\
                           .then_inc(rope_step, 1)
                    next_lo("qkv", TRI_N, i, i % 4)

            def softmax_heads():
                dve.wait_ge(lam_exp, 1)
                dve.scalar_tensor_tensor(out=small[:, 4:5], in0=small[:, 3:4], scalar=-LAMBDA_INIT, in1=small[:, 2:3],
                                         op0=ALU.add, op1=ALU.subtract).then_inc(lam_step, 1)
                c = COL["subln"]
                dve.tensor_scalar(small[:, 5:6], par[:, c:c + 1], 1.0 - LAMBDA_INIT, None, ALU.mult).then_inc(lam_step, 1)
                dve.wait_ge(rope_step, 7 * HEADS)
                for i in range(HEADS):
                    b = 3 * (i % 2)
                    o = 4 * (i % 2)
                    if i >= 1:
                        dve.wait_ge(a_step, 4 * i)
                    for t in range(QT):
                        keys = META + P * (t + 1)
                        dve.wait_ge(scores_done, 2 * i + t + 1)
                        if t == 0:
                            src = ps[:, b, 0:2 * keys].rearrange("p (c k) -> p c k", c=2)
                            m = mask[:, :, P:T]
                        else:
                            src, m = ps[:, b + 1:b + 3, 0:keys], mask
                        dve.tensor_tensor(s_sb[:, t, :, 0:keys], src, m, ALU.add).then_inc(s_ready, 1)
                    for t in range(QT):
                        keys = META + P * (t + 1)
                        dve.wait_ge(s_ready, 2 * i + t + 1)
                        n = 24 + 2 * t
                        if i >= 1 or t >= 1:
                            dve.wait_ge(max_step, 4 * i + 2 * t)
                        dve.tensor_reduce(small[:, n:n + 2], s_sb[:, t, :, 0:keys], AX.X, ALU.max).then_inc(max_step, 1)
                        dve.wait_ge(max_step, 4 * i + 2 * t + 1)
                        dve.tensor_scalar(small[:, 8 + o + 2 * t:10 + o + 2 * t], small[:, n:n + 2], -1.0, None, ALU.mult)\
                           .then_inc(max_step, 1)
                    dve.wait_ge(exp_ready, 4 * i + 4)
                    if i >= 1:
                        dve.wait_ge(a_turned, 2 * i)
                    rs, cl = small[:, 16 + o:20 + o], small[:, 28:30]
                    dve.reciprocal(rs, rs).then_inc(rs_step, 1)
                    dve.wait_ge(rs_step, 2 * i + 1)
                    dve.tensor_scalar(cl, small[:, 17 + o:20 + o:2], small[:, 4:5], None, ALU.mult).then_inc(rs_step, 1)
                    for t in range(QT):
                        keys = META + P * (t + 1)
                        dve.tensor_scalar(a_sb[:, t, 0:keys], s_sb[:, t, 0, 0:keys],
                                          small[:, 16 + o + 2 * t:17 + o + 2 * t], None, ALU.mult).then_inc(a_step, 1)
                    dve.wait_ge(rs_step, 2 * i + 2)
                    for t in range(QT):
                        keys = META + P * (t + 1)
                        dve.wait_ge(a_step, 4 * i + 2)
                        dve.scalar_tensor_tensor(out=a_sb[:, t, 0:keys], in0=s_sb[:, t, 1, 0:keys],
                                                 scalar=small[:, 28 + t:29 + t], in1=a_sb[:, t, 0:keys],
                                                 op0=ALU.mult, op1=ALU.add).then_inc(a_step, 1)

            def newton_steps(ms_, r0_, r_, step_sem, base):
                dve.tensor_tensor(r_, r0_, r0_, ALU.mult).then_inc(step_sem, 1)
                dve.wait_ge(step_sem, base + 1)
                dve.scalar_tensor_tensor(out=r_, in0=r_, scalar=-0.5, in1=ms_, op0=ALU.mult, op1=ALU.mult).then_inc(step_sem, 1)
                dve.wait_ge(step_sem, base + 2)
                dve.scalar_tensor_tensor(out=r_, in0=r_, scalar=1.5, in1=r0_, op0=ALU.add, op1=ALU.mult).then_inc(step_sem, 1)
                dve.wait_ge(step_sem, base + 3)

            def sub_norm():
                for g in range(4):
                    dve.wait_ge(sub_summed, g + 1)
                    dve.tensor_scalar(sub_ms[:, :], ps[:, g, :], 1.0 / P, SUBLN_EPS, ALU.mult, ALU.add).then_inc(sub_step, 1)
                    dve.wait_ge(sub_r0_ready, g + 1)
                    newton_steps(sub_ms[:, :], sub_r0[:, :], sub_r[:, :], sub_step, 4 * g + 1)
                    for i in (2 * g, 2 * g + 1):
                        dve.scalar_tensor_tensor(out=fx[:, i, META:T], in0=fx[:, i, META:T], scalar=small[:, 5:6],
                                                 in1=sub_r[:, (i % 2) * SEQ:(i % 2 + 1) * SEQ],
                                                 op0=ALU.mult, op1=ALU.mult).then_inc(sub_y_ready, 1)
                    for i in (2 * g, 2 * g + 1):
                        dve.wait_ge(out_hi_ready, i + 1)
                        dve.tensor_tensor(x_lo[:, i, META:T], fx[:, i, META:T], x_hi[:, i, META:T].bitcast(F32),
                                          ALU.subtract).then_inc(out_lo_ready, 1)

            def distances():
                dve.wait_ge(dist_done, 1)
                dve.tensor_tensor(by_dist[:, :], weight_sb[:, :], ps[0:HEADS, 7, :], ALU.add).then_inc(dist_ready, 1)

            def mix_in():
                for i in range(TRI_N - 1):
                    next_lo("mix_in", TRI_N, i, i % 4)
                    if i == 0:
                        distances()

            def gated():
                pre = ps[:, 5, :].rearrange("p (t f) -> p t f", t=2)
                dve.wait_ge(g_act, 4)
                dve.tensor_scalar(g_ls[:, :, :], pre, 0.0, None, ALU.min).then_inc(g_dve, 1)
                dve.wait_ge(g_dve, 1)
                dve.wait_ge(g_act, 6)
                dve.tensor_tensor(g_ls[:, :, :], g_ls[:, :, :], g_a[:, :, :], ALU.subtract).then_inc(g_dve, 1)
                dve.wait_ge(g_act, 7)
                dve.wait_ge(g_pool, 1)
                for i in range(GLA_HEADS):
                    rows, c = slice(64 * (i % 2), 64 * (i % 2) + 64), i // 2
                    dve.scalar_tensor_tensor(out=g_q[rows, i, :], in0=proj[rows, GQ + c, :], scalar=0.125,
                                             in1=g_eb[rows, c, :], op0=ALU.mult, op1=ALU.mult).then_inc(g_dve, 1)
                dve.wait_ge(g_act, 8)
                dve.tensor_tensor(g_k[:, :, :], proj[:, GK:GK + 2, :], g_a[:, :, :], ALU.mult).then_inc(g_dve, 1)
                dve.wait_ge(g_act, 9)
                dve.wait_ge(g_pool, 2)
                for t in range(QT):
                    for c in range(2):
                        rows = slice(64 * c, 64 * c + 64)
                        dve.tensor_tensor(g_ke[rows, t, c, :], g_et[rows, t, :], ps[rows, 7, t * SEQ:(t + 1) * SEQ],
                                          ALU.mult).then_inc(g_dve, 1)
                dve.wait_ge(g_pe, 8)
                dve.wait_ge(g_pool, 3)
                att = ps[:, 0:2, :].rearrange("p b c -> p (b c)").rearrange("p (n i) -> p n i", n=8)
                for c in range(2):
                    rows = slice(64 * c, 64 * c + 64)
                    for b in range(2):
                        half = ps[rows, b, :].rearrange("p (n i) -> p n i", n=4)[:, :, rows]
                        dve.tensor_copy(g_att[rows, 4 * b:4 * b + 4, rows], half).then_inc(g_dve, 2)
                dve.wait_ge(g_pe, 9)
                for c in range(3):
                    for p in range(2):
                        inc = ps[:, 2 + c, p * SEQ:(p + 1) * SEQ] if c < 2 else ps[:, 7, p * SEQ:(p + 1) * SEQ]
                        if c == 0:
                            dve.tensor_copy(g_s[:, 0, p, :], inc).then_inc(g_dve, 1)
                        else:
                            last = GLA_CHUNK * (c + 1) - 1
                            dve.wait_ge(g_dve, 19 + 2 * c - 1 + p)
                            dve.scalar_tensor_tensor(out=g_s[:, c, p, :], in0=g_s[:, c - 1, p, :],
                                                     scalar=g_eb[:, p, last:last + 1], in1=inc,
                                                     op0=ALU.mult, op1=ALU.add).then_inc(g_dve, 1)
                dve.wait_ge(g_pe, 11)
                dve.tensor_scalar(n_ms[:, :, :].rearrange("p a s -> p (a s)").rearrange("p (b s) -> p b s", b=2),
                                  ps[:, 2:4, :], 1.0 / P, NORM_EPS, ALU.mult, ALU.add).then_inc(g_dve, 1)
                dve.wait_ge(g_act, 12)
                newton_steps(n_ms[:, :, :], n_r0[:, :, :], n_r[:, :, :], g_dve, 26)
                for i in range(GLA_HEADS):
                    dve.tensor_tensor(n_r[:, i, :], n_r[:, i, :], ps[:, 4 + i // 2, (i % 2) * SEQ:(i % 2 + 1) * SEQ],
                                      ALU.mult).then_inc(g_dve, 1)
                dve.wait_ge(g_act, 13)
                for i in range(GLA_HEADS):
                    dve.wait_ge(g_dve, 30 + i)
                    c = COL["gla_norm"] + i
                    dve.scalar_tensor_tensor(out=fx[:, i, META:T], in0=n_r[:, i, :], scalar=par[:, c:c + 1],
                                             in1=proj[:, GR + i, :], op0=ALU.mult, op1=ALU.mult).then_inc(g_dve, 1)

            def dilated():
                def key(i):
                    rows = slice(64 * (i % 2), 64 * (i % 2) + 64)
                    if i == 0:
                        dve.wait_ge(g_pool, 6)
                    if i >= 2:
                        dve.wait_ge(d_scores, i - 1)
                    dve.tensor_scalar(d_k[i % 2][rows, :], proj[rows, DK + i // 2, :], 0.125, None, ALU.mult)\
                       .then_inc(d_k_ready, 1)

                key(0)
                dve.wait_ge(bias_loaded, 16)
                for i in range(HEADS):
                    if i + 1 < HEADS:
                        key(i + 1)
                    n = 2 * (i % 2)
                    dve.wait_ge(d_scores, i + 1)
                    if i >= 1:
                        dve.wait_ge(d_turned, i)
                        dve.wait_ge(d_p_step, 3 * i)
                    dve.tensor_tensor(d_s[:, 0:P], ps[:, i % 2, 0:P], bias[:, i, P - 1::-1], ALU.add).then_inc(d_s_ready, 1)
                    dve.tensor_tensor(d_s[:, P:3 * P], ps[:, i % 2, P:3 * P], bias[:, i, ::-1], ALU.add).then_inc(d_s_ready, 1)
                    for t in range(QT):
                        a, b = (0, P) if t == 0 else (P, 3 * P)
                        dve.wait_ge(d_s_ready, 2 * i + t + 1)
                        if i >= 1 or t >= 1:
                            dve.wait_ge(d_max_step, 4 * i + 2 * t)
                        dve.tensor_reduce(small[:, 24 + t:25 + t], d_s[:, a:b], AX.X, ALU.max).then_inc(d_max_step, 1)
                        dve.wait_ge(d_max_step, 4 * i + 2 * t + 1)
                        dve.tensor_scalar(small[:, 8 + n + t:9 + n + t], small[:, 24 + t:25 + t], -1.0, None, ALU.mult)\
                           .then_inc(d_max_step, 1)
                    dve.wait_ge(d_exp, 2 * i + 2)
                    rs = small[:, 16 + n:18 + n]
                    dve.reciprocal(rs, rs).then_inc(d_p_step, 1)
                    dve.wait_ge(d_p_step, 3 * i + 1)
                    for t in range(QT):
                        a, b = (0, P) if t == 0 else (P, 3 * P)
                        dve.tensor_scalar(d_p[:, a:b], d_s[:, a:b], small[:, 16 + n + t:17 + n + t], None, ALU.mult)\
                           .then_inc(d_p_step, 1)
                for k in range(KD):
                    dve.wait_ge(out_hi_ready, KD + k + 1)
                    dve.tensor_tensor(x_lo[:, k, META:T], fx[:, k, META:T], x_hi[:, k, META:T].bitcast(F32),
                                      ALU.subtract).then_inc(out_lo_ready, 1)

            def residual(m, j, u):
                hm = h[:, m, META:T] if isinstance(m, int) else h[:, bass.ds(m, 1), META:T]
                dve.tensor_tensor(hm, hm, ps[:, j % 4, META:T], ALU.add).then_inc(h_ready, 1)

            def wide_hidden():
                def step(i, j):
                    t = hid[j % 2][:, :]
                    dve.wait_ge(act_ready, i + (4 * KF + 1))
                    dve.tensor_tensor(t, act_out[:, :], act_out[:, :], ALU.mult).then_inc(hid_ready, 1)
                    next_lo("ff1", FF1_N, i, j)
                    dve.wait_ge(hid_hi_ready, i + (4 * KF + 1))
                    dve.tensor_tensor(hid_lo[:, bass.ds(i * 2 * SEQ, 2 * SEQ)], t,
                                      hid_hi[:, bass.ds(i * 2 * SEQ, 2 * SEQ)].bitcast(F32), ALU.subtract)\
                       .then_inc(hid_lo_ready, 1)

                loop(dve, FF1_N, step, peel=2)

            dve.memset(small[:, 30:31], 0.0).then_inc(hid_ready, HID_CREDIT)
            dve.memset(small[:, 31:32], 0.0).then_inc(cv_y_ready, CV_CREDIT)
            dve.memset(small[:, 29:30], 0.0).then_inc(f_ready, F_CREDIT)
            split_lo(0, 0, WIDTH[0])
            split_lo(1, 1, WIDTH[1])
            dve.wait_ge(consts_loaded, 32)
            s = 0
            for u, (kind, pre, post, f) in enumerate(SUB):
                c0 = first_col(u)
                pre_norm(u, s, c0, pre)
                s += 1
                if u > 0:
                    n = FIRST[{1: "conv_in", 2: "gu1", 3: "gu2", 4: "qkv", 5: "gu3"}[u]] + 1
                    split_lo(n, n % 4, WIDTH[n])
                if kind == "ffn":
                    hidden(f"gu{f}", f, c0)
                    out_projection(f"dn{f}", DN_N, 1, u, c0)
                elif kind == "conv":
                    convolution()
                    out_projection("conv_out", PROJ_N, 2, u, c0)
                else:
                    c0 = META
                    lam()
                    heads_in()
                    softmax_heads()
                    sub_norm()
                    out_projection("attn_out", PROJ_N, 2, u, c0)
                post_norm(u, s, c0, 0.5 if kind == "ffn" else 1.0)
                s += 1
            pre_norm(6, s, META, "attn_norm")
            s += 1
            n = FIRST["mix_in"] + 1
            split_lo(n, n % 4, WIDTH[n])
            mix_in()
            gated()
            dilated()
            n = FIRST["mix_out"] + 1
            split_lo(n, n % 4, WIDTH[n])
            for i in range(PROJ_N):
                dve.wait_ge(block_used, FIRST["mix_out"] + i + 1)
                residual(2 * i, 2 * i, 6)
                residual(2 * i + 1, 2 * i + 1, 6)
                if i < PROJ_N - 1:
                    next_lo("mix_out", PROJ_N, i, i)
            dve.wait_ge(h_ready, 7 * KD)
            pre_norm(7, s, META, "mlp_norm")
            s += 1
            n = FIRST["ff1"] + 1
            split_lo(n, n % 4, WIDTH[n])
            wide_hidden()
            n0 = FIRST["ff2"]
            for m in range(KD):
                dve.wait_ge(block_used, n0 + 2 * m + 1)
                if 2 * m + 2 < FF2_N:
                    next_lo("ff2", FF2_N, 2 * m, 2 * m % 4)
                dve.wait_ge(block_used, n0 + 2 * m + 2)
                residual(m, m, 7)
                if 2 * m + 3 < FF2_N:
                    next_lo("ff2", FF2_N, 2 * m + 1, (2 * m + 1) % 4)
            dve.wait_ge(h_ready, 8 * KD)
            root(s, META, h_sq_summed, 9 * KD, NORM_EPS)
            for k in range(KD):
                normed(k, META, "final_norm", out_ready)

        @block.tensor
        def _(pe):
            def product(out_ap, slot, t0, tiles, hi, lo, start=True, stop=True, before=None, step=1):
                for k in range(tiles):
                    if before:
                        before(k)
                    cols = slice((t0 + k) * P, (t0 + k + 1) * P)
                    first, last = start and k == 0, stop and k == tiles - 1
                    pe.matmul(out_ap, w_hi[slot][:, cols], hi(k), start=first, stop=False)
                    pe.matmul(out_ap, w_hi[slot][:, cols], lo(k), start=False, stop=False)
                    mm = pe.matmul(out_ap, w_lo[slot][:, cols], hi(k), start=False, stop=last)
                return mm

            def x_parts(c0):
                return (lambda k: x_hi[:, k, c0:T]), (lambda k: x_lo[:, k, c0:T])

            def split_ready(n0, i):
                pe.wait_ge(lo_ready, i + (n0 + 1))

            def when_input(q, first):
                return (lambda k: pe.wait_ge(x_lo_ready, KD * q + k + 1)) if first else None

            def hidden(name, f, q, c0):
                n0 = FIRST[name]
                hi, lo = x_parts(c0)

                def step(i, j):
                    split_ready(n0, i)
                    pe.wait_ge(hid_ready, i + (KF * f + 1))
                    product(ps[:, 2 * (j % 2), c0:T], j % 2, 0, KD, hi, lo, before=when_input(q, j == 0))
                    product(ps[:, 2 * (j % 2) + 1, c0:T], j % 2, KD, KD, hi, lo).then_inc(block_used, 1)

                loop(pe, GU_N, step)

            def down(name, f, u, c0):
                n0 = FIRST[name]
                hi = lambda k: hid_hi[:, k * T + c0:(k + 1) * T]
                lo = lambda k: hid_lo[:, k * T + c0:(k + 1) * T]

                def step(i, j):
                    split_ready(n0, i)
                    pe.wait_ge(f_ready, i + (KD * u + 1))
                    before = (lambda k: pe.wait_ge(hid_lo_ready, KF * f + k + 1) if k >= KF - 4 else None) if j == 0 else None
                    product(ps[:, j, c0:T], j % 2, 0, KF, hi, lo, before=before).then_inc(block_used, 1)

                loop(pe, DN_N, step)

            def sum_squares(u, c0):
                pe.wait_ge(sumsq_ready, 9 * (u + 1))
                pe.matmul(ps[:, SUM, c0:T], ones[:, :], sumsq[:, c0:T], start=True, stop=True).then_inc(sumsq_summed, 1)

            def pre_norm(q, c0):
                for k in range(KD):
                    pe.wait_ge(h_sq_ready, KD * q + k + 1)
                    pe.matmul(ps[:, SUM, c0:T], ones[:, :], square[k % 2][:, c0:T], start=k == 0, stop=k == KD - 1)\
                      .then_inc(h_sq_summed, 1)

            def convolution(q):
                n0 = FIRST["conv_in"]
                hi, lo = x_parts(0)

                def step(i, j):
                    b = 3 * (j % 2)
                    split_ready(n0, i)
                    pe.wait_ge(cv_y_ready, i + 1)
                    for s in range(3):
                        mm = product(ps[:, b + s, 0:T], j % 2, s * KD, KD, hi, lo,
                                     before=when_input(q, j == 0 and s == 0))
                    mm.then_inc(block_used, 1)

                loop(pe, TRI_N, step)
                pe.wait_ge(cv_y_ready, TRI_N - 1 + CV_CREDIT)

            def out_projection(name, u, hi, lo, ready, sem_, base, c0):
                n0 = FIRST[name]
                for i in range(PROJ_N):
                    split_ready(n0, i)
                    pe.wait_ge(sem_, base + 2 * i + 2)
                    for s in range(2):
                        before = (lambda k: pe.wait_ge(ready[0], ready[1] + k + 1)) if i == 0 and s == 0 else None
                        mm = product(ps[:, (2 * i + s) % 4, c0:T], i % 2, s * KD, KD, hi, lo, before=before)
                    mm.then_inc(block_used, 1)

            def heads_in(q):
                n0 = FIRST["qkv"]
                for i in range(HEADS):
                    b, r = 3 * (i % 2), i % 2
                    split_ready(n0, i)
                    for s, c0 in enumerate((0, META, 0)):
                        hi, lo = x_parts(c0)
                        if i >= 2:
                            pe.wait_ge(part_copied, 3 * (i - 2) + s + 1)
                        mm = product(ps[:, b + s, 0:T - c0], r, s * KD, KD, hi, lo,
                                     before=when_input(q, i == 0 and s == 0))
                        mm.then_inc(block_used if s == 2 else part_done, 1)
                    pe.wait_ge(part_copied, 3 * i + 1)
                    if i >= 1:
                        pe.wait_ge(v_tok_ready, 2 * i)
                        pe.wait_ge(rope_step, 7 * i)
                    pe.transpose(ps[:, 7, 0:P], v_sb[r][:, META:META + P], ident)
                    pe.transpose(ps[:, 7, P:2 * P], v_sb[r][:, META + P:T], ident)
                    pe.transpose(ps[:, 7, 2 * P:3 * P], v_sb[r][:, 0:P], ident).then_inc(v_turned, 1)
                    pe.wait_ge(part_copied, 3 * i + 2)
                    pe.matmul(ps[:, b + 1, SEQ:2 * SEQ], rotate, q_sb[r][:, :], start=True, stop=True).then_inc(rotated, 1)
                    pe.wait_ge(part_copied, 3 * i + 3)
                    pe.matmul(ps[:, 6, 0:T], rotate, k_sb[r][:, :], start=True, stop=True).then_inc(rotated, 1)

            def softmax_heads():
                pe.wait_ge(lam_step, 1)
                pe.wait_ge(part_copied, 3 * HEADS)
                pe.matmul(ps[:, 0, 0:2], ones[:, :], small[:, 0:2], start=True, stop=True).then_inc(lam_sum, 1)
                pe.wait_ge(rope_step, 7 * HEADS)
                pe.wait_ge(v_tok_ready, 2 * HEADS)
                pe.wait_ge(lam_exp, 1)

                def scores(i):
                    b = 3 * (i % 2)
                    if i >= 2:
                        pe.wait_ge(s_ready, 2 * (i - 1))
                    for t in range(QT):
                        keys = META + P * (t + 1)
                        for c in range(2):
                            o = ps[:, b, c * keys:(c + 1) * keys] if t == 0 else ps[:, b + 1 + c, 0:keys]
                            mm = pe.matmul(o, q_rot[:, i, t * P:(t + 1) * P], k_rot[:, i, c, 0:keys], start=True, stop=True)
                        mm.then_inc(scores_done, 1)

                scores(0)
                for i in range(HEADS):
                    if i + 1 < HEADS:
                        scores(i + 1)
                    if i >= 1:
                        pe.wait_ge(o_copied, i)
                        pe.wait_ge(a_tok_ready, 4 * i)
                    pe.wait_ge(a_step, 4 * i + 3)
                    pe.transpose(ps[:, 7, 0:P], a_sb[:, 0, 0:P], ident)
                    pe.transpose(ps[:, 7, P:2 * P], a_sb[:, 0, META:META + P], ident).then_inc(a_turned, 1)
                    pe.wait_ge(a_step, 4 * i + 4)
                    pe.transpose(ps[:, 6, 0:P], a_sb[:, 1, 0:P], ident)
                    pe.transpose(ps[:, 6, P:2 * P], a_sb[:, 1, META:META + P], ident)
                    pe.transpose(ps[:, 6, 2 * P:3 * P], a_sb[:, 1, META + P:T], ident).then_inc(a_turned, 1)
                    for t in range(QT):
                        pe.wait_ge(a_tok_ready, 4 * i + 2 * t + 2)
                        o = ps[:, 7, SEQ + t * P:SEQ + (t + 1) * P]
                        for n in range(t + 2):
                            mm = pe.matmul(o, v_tok[:, i, n, :], a_tok[:, 2 * t + n, :], start=n == 0, stop=n == t + 1)
                    mm.then_inc(o_done, 1)

            def sub_norm():
                for g in range(4):
                    pe.wait_ge(sub_sq_ready, g + 1)
                    pe.matmul(ps[:, g, :], ones[:, :], sub_sq[:, :], start=True, stop=True).then_inc(sub_summed, 1)

            def mix_in(q):
                n0 = FIRST["mix_in"]
                hi, lo = x_parts(META)
                for i in range(TRI_N):
                    b = 3 * (i % 2)
                    split_ready(n0, i)
                    if i >= 2:
                        pe.wait_ge(proj_copied, i - 1)
                    for s in range(3):
                        mm = product(ps[:, b + s, 0:SEQ], i % 2, s * KD, KD, hi, lo,
                                     before=when_input(q, i == 0 and s == 0))
                    mm.then_inc(block_used, 1)
                    if i == 0:
                        pe.wait_ge(mix_loaded, 6 * 16)
                        pe.wait_ge(mix_zeroed, 4)
                        pe.matmul(ps[0:HEADS, 7, :], rel_sb[:, :], onehot_sb[:, :], start=True, stop=True)\
                          .then_inc(dist_done, 1)

            def gated():
                pe.wait_ge(proj_copied, TRI_N)
                for a, c0 in enumerate((GV, DV)):
                    for t in range(QT):
                        for c in range(4):
                            mm = pe.transpose(ps[:, 2 * a + t, c * P:(c + 1) * P], proj[:, c0 + c, t * P:(t + 1) * P], ident)
                    mm.then_inc(g_pe, 1)
                for k in range(KD):
                    mm = pe.matmul(ps[0:16, 4, 0:SEQ], w_glow_sb[:, k, :], fx[:, k, META:T], start=k == 0, stop=k == KD - 1)
                mm.then_inc(g_pe, 1)
                pe.wait_ge(g_act, 3)
                for t in range(QT):
                    mm = pe.matmul(ps[:, 5, t * SEQ:(t + 1) * SEQ], glow[:, t * P:(t + 1) * P], gate_w_sb[:, :],
                                   start=True, stop=True)
                mm.then_inc(g_pe, 1)
                pe.wait_ge(dist_ready, 1)
                for t in range(QT):
                    for c in range(2):
                        pe.transpose(ps[:, 7, t * SEQ + c * P:t * SEQ + (c + 1) * P], proj[:, GK + c, t * P:(t + 1) * P], ident)
                pe.wait_ge(g_dve, 2)
                for c in range(2):
                    for t in range(QT):
                        mm = pe.matmul(ps[:, 4, c * SEQ + t * P:c * SEQ + (t + 1) * P], g_ls[:, t, c * P:(c + 1) * P], upto,
                                       start=True, stop=True)
                mm.then_inc(g_pe, 1)
                for t in range(QT):
                    mm = pe.matmul(ps[:, 6, t * SEQ:(t + 1) * SEQ], after, g_ls[:, t, :], start=True, stop=True)
                mm.then_inc(g_pe, 1)
                pe.wait_ge(g_act, 2)
                pe.wait_ge(g_dve, 7)
                for i in range(GLA_HEADS):
                    for t in range(QT):
                        n = 2 * i + t
                        mm = pe.matmul(ps[:, n // 4, (n % 4) * P:(n % 4 + 1) * P], g_k[:, i // 2, t * P:(t + 1) * P],
                                       g_q[:, i, t * P:(t + 1) * P], start=True, stop=True)
                    if i % 2:
                        mm.then_inc(g_pe, 1)
                pe.wait_ge(g_dve, 11)
                for c in range(3):
                    for p in range(2):
                        o = ps[:, 2 + c, p * SEQ:(p + 1) * SEQ] if c < 2 else ps[:, 7, p * SEQ:(p + 1) * SEQ]
                        mm = pe.matmul(o, g_ke[:, c // 2, c % 2, p * P:(p + 1) * P], gv_tok[:, c // 2, p * SEQ:(p + 1) * SEQ],
                                       start=True, stop=True)
                mm.then_inc(g_pe, 1)
                pe.wait_ge(g_pool, 4)
                pe.wait_ge(g_dve, 25)
                pe.wait_ge(g_act, 9)
                for i in range(GLA_HEADS):
                    for t in range(QT):
                        o = (i % 2) * SEQ + t * P
                        v = gv_tok[:, t, i * P:(i + 1) * P]
                        mm = pe.matmul(ps[:, 4 + i // 2, o:o + P], v, g_att[:, 2 * i + t, :], start=True, stop=False)
                        for c in range(2):
                            n = 2 * t + c
                            if n:
                                mm = pe.matmul(ps[:, 4 + i // 2, o + 64 * c:o + 64 * c + 64],
                                               g_s[:, n - 1, i // 2, (i % 2) * P:(i % 2 + 1) * P],
                                               g_q[:, i, 64 * n:64 * n + 64], start=False, stop=c == 1)
                mm.then_inc(g_pe, 1)
                pe.wait_ge(g_act, 10)
                flat = n_sq[:, :, :].rearrange("p a s -> p (a s)")
                for b in range(2):
                    mm = pe.matmul(ps[:, 2 + b, :], ones[:, :], flat[:, b * 512:(b + 1) * 512], start=True, stop=True)
                mm.then_inc(g_pe, 1)

            def dilated():
                def scores(i):
                    pe.wait_ge(d_k_ready, i + 1)
                    if i >= 2:
                        pe.wait_ge(d_s_ready, 2 * (i - 1))
                    c = DQ + i // 2
                    pe.matmul(ps[:, i % 2, 0:P], proj[:, c, 0:P], d_k[i % 2][:, 0:P], start=True, stop=True)
                    pe.matmul(ps[:, i % 2, P:3 * P], proj[:, c, P:2 * P], d_k[i % 2][:, :], start=True, stop=True)\
                      .then_inc(d_scores, 1)

                scores(0)
                for i in range(HEADS):
                    if i + 1 < HEADS:
                        scores(i + 1)
                    pe.wait_ge(d_p_step, 3 * i + 3)
                    if i >= 1:
                        pe.wait_ge(d_pt_ready, i)
                    for n in range(3):
                        mm = pe.transpose(ps[:, 2, n * P:(n + 1) * P], d_p[:, n * P:(n + 1) * P], ident)
                    mm.then_inc(d_turned, 1)
                    pe.wait_ge(d_pt_ready, i + 1)
                    if i >= 1:
                        pe.wait_ge(d_o_copied, i)
                    v = slice((i // 2) * P, (i // 2 + 1) * P)
                    pe.matmul(ps[:, 3, 0:P], dv_tok[:, 0, v], d_pt[:, 0, :], start=True, stop=True)
                    pe.matmul(ps[:, 3, P:2 * P], dv_tok[:, 0, v], d_pt[:, 1, :], start=True, stop=False)
                    pe.matmul(ps[:, 3, P:2 * P], dv_tok[:, 1, v], d_pt[:, 2, :], start=False, stop=True).then_inc(d_o_done, 1)

            def wide_hidden(q):
                n0 = FIRST["ff1"]
                hi, lo = x_parts(META)

                def step(i, j):
                    split_ready(n0, i)
                    pe.wait_ge(hid_ready, i + (4 * KF + 1))
                    for s in range(2):
                        mm = product(ps[:, 2 * (j % 2) + s, 0:SEQ], j % 2, s * KD, KD, hi, lo,
                                     before=when_input(q, j == 0 and s == 0))
                    mm.then_inc(block_used, 1)

                loop(pe, FF1_N, step)

            def wide_down():
                n0 = FIRST["ff2"]
                half = KF2 // 2

                for i in range(FF2_N):
                    m, s = i // 2, i % 2
                    hi = lambda k: hid_hi[:, (s * half + k) * SEQ:(s * half + k + 1) * SEQ]
                    lo = lambda k: hid_lo[:, (s * half + k) * SEQ:(s * half + k + 1) * SEQ]
                    split_ready(n0, i)
                    if i == 0:
                        pe.wait_ge(hid_lo_ready, 4 * KF + FF1_N - 2)
                    if i == 1:
                        pe.wait_ge(hid_lo_ready, 4 * KF + FF1_N)
                    if s == 0:
                        pe.wait_ge(h_ready, 7 * KD + max(0, m - 3))
                    product(ps[:, m % 4, META:T], i % 2, 0, half, hi, lo, start=s == 0, stop=s == 1).then_inc(block_used, 1)

            pe.wait_ge(ones_ready, 1)
            pe.wait_ge(consts_loaded, 32)
            for u, (kind, pre, post, f) in enumerate(SUB):
                c0 = first_col(u)
                pre_norm(u, c0)
                if kind == "ffn":
                    hidden(f"gu{f}", f, u, c0)
                    down(f"dn{f}", f, u, c0)
                elif kind == "conv":
                    convolution(u)
                    out_projection("conv_out", u, lambda k: y_hi[:, k, :], lambda k: y_lo[:, k, :],
                                   (cv_lo_ready, 0), f_ready, KD * u, 0)
                else:
                    c0 = META
                    heads_in(u)
                    softmax_heads()
                    sub_norm()
                    hi, lo = x_parts(META)
                    out_projection("attn_out", u, hi, lo, (out_lo_ready, 0), f_ready, KD * u, META)
                sum_squares(u, c0)
            pre_norm(6, META)
            mix_in(6)
            gated()
            dilated()
            hi, lo = x_parts(META)
            out_projection("mix_out", 6, hi, lo, (out_lo_ready, KD), h_ready, 6 * KD - F_CREDIT, META)
            pre_norm(7, META)
            wide_hidden(7)
            wide_down()
            pre_norm(8, META)


GD_DONE = 37


def blocks_of(w, pieces):
    rows = np.array([[r for r, _ in p] for p in pieces])
    cols = np.array([[c for _, c in p] for p in pieces])
    k, m = w.shape
    tiled = w.reshape(k // P, P, m // P, P).transpose(0, 2, 1, 3)
    picked = tiled[rows // P, cols // P]
    return np.ascontiguousarray(picked.transpose(0, 2, 1, 3).reshape(len(pieces), P, -1))


def columns(v):
    return v.reshape(-1, P).T


def kernel(**inputs):
    import concourse.bacc as bacc
    from concourse.bass_utils import run_bass_kernel_spmd

    a = {k: np.asarray(v) for k, v in inputs.items()}
    ks = range(KD)
    rows = lambda n: [k * P for k in range(n)]

    def swiglu_in(w):
        return blocks_of(w, [[(r, i * P) for r in rows(KD)] + [(r, D_FF + i * P) for r in rows(KD)] for i in range(KF)])

    def down(w):
        return blocks_of(w, [[(r, m * P) for r in rows(KF)] for m in ks])

    def triple(w, order):
        return blocks_of(w, [[(r, s * D + i * P) for s in order for r in rows(KD)] for i in ks])

    def pairs(w, n):
        return blocks_of(w, [[(r, (2 * b + s) * P) for s in range(2) for r in rows(KD)] for b in range(n)])

    w_in = a["w_in_2"][0]
    low = 2 * SEQ + 2 * 512
    w_mix = np.concatenate([w_in[:, :low], w_in[:, low + 16:]], axis=1)
    arrays = {
        "gu0": swiglu_in(a["ffn1_w_gu"][0]), "dn0": down(a["ffn1_w_down"][0]),
        "conv_in": triple(a["conv_w_in"][0], (0, 1, 2)), "conv_out": pairs(a["conv_w_out"][0], PROJ_N),
        "gu1": swiglu_in(a["ffn2_w_gu"][0]), "dn1": down(a["ffn2_w_down"][0]),
        "gu2": swiglu_in(a["ffn1_w_gu"][1]), "dn2": down(a["ffn1_w_down"][1]),
        "qkv": triple(a["attn_w_qkv"][0], (2, 0, 1)), "attn_out": pairs(a["attn_w_o"][0], PROJ_N),
        "gu3": swiglu_in(a["ffn2_w_gu"][1]), "dn3": down(a["ffn2_w_down"][1]),
        "mix_in": blocks_of(w_mix, [[(r, (3 * i + s) * P) for s in range(3) for r in rows(KD)] for i in ks]),
        "mix_out": pairs(a["w_out_2"][0], PROJ_N),
        "ff1": pairs(a["w_ff1_2"][0], FF1_N),
        "ff2": blocks_of(a["w_ff2_2"][0], [[((s * 16 + k) * P, m * P) for k in range(16)] for m in ks for s in range(2)]),
    }
    lam = np.zeros((P, 4), np.float32)
    lam[:64] = a["attn_lambda"][0].T
    par = [a["ln_ffn1"][0, 0], a["ln_ffn1"][0, 1], a["ln_mix"][0, 0], a["ln_mix"][0, 1], a["ln_ffn2"][0, 0],
           a["ln_ffn2"][0, 1], a["ln_ffn1"][1, 0], a["ln_ffn1"][1, 1], a["ln_mix"][1, 0], a["ln_mix"][1, 1],
           a["ln_ffn2"][1, 0], a["ln_ffn2"][1, 1], a["attn_norm_g_2"][0], a["mlp_norm_g_2"][0], a["final_norm_g_2"],
           a["conv_w"][0], a["attn_subln_g"][0], a["gla_norm_g_2"][0]]
    small = {}
    small["params"] = np.ascontiguousarray(np.concatenate([columns(v) for v in par] + [lam], axis=1))
    tokens = np.concatenate([a["meta_tokens"], a["x"][0]], axis=0)
    small["h_in"] = np.ascontiguousarray(tokens.T.reshape(KD, P, T).transpose(1, 0, 2))
    small["squares"], small["rope_mask"], small["onehot"], small["weight"] = shape_constants()
    small["w_glow"] = np.ascontiguousarray(w_in[:, low:low + 16].reshape(KD, P, 16).transpose(1, 0, 2))
    small["gate_w"] = np.concatenate([a["gla_gate_w2_2"][0], a["gla_gate_b_2"]], axis=0)
    small["rel_bias"] = np.ascontiguousarray(a["rel_bias_2"])

    nc = bacc.Bacc("TRN2", target_bir_lowering=False, num_devices=1)
    dram = lambda name, v: nc.dram_tensor(name, v.shape, F32, kind="ExternalInput").ap()
    w = {name: dram(f"w_{name}", v) for name, v in arrays.items()}
    s = {name: dram(name, v) for name, v in small.items()}
    out = nc.dram_tensor("out", (D, SEQ), F32, kind="ExternalOutput").ap()
    two_blocks(nc, w, out=out, **s)
    feed = {f"w_{name}": v for name, v in arrays.items()} | small
    r = run_bass_kernel_spmd(nc, [feed], core_ids=[0])
    return np.asarray(r.results[0]["out"]).T.reshape(1, SEQ, D)
```

```python
import math
from contextlib import ExitStack

import numpy as np
import concourse.bass as bass
from concourse import mybir

F32 = mybir.dt.float32
F32R = mybir.dt.float32r
ALU = mybir.AluOpType
ACT = mybir.ActivationFunctionType
AX = mybir.AxisListType

P = 128
D = 1024
KD = D // P
META = 16
SEQ = 256
T = META + SEQ
D_FF = 2816
KF = D_FF // P
D_FF2 = 4096
KF2 = D_FF2 // P
HEADS = 8
QT = SEQ // P
LAMBDA_INIT = 0.8 - 0.6 * math.exp(-0.3 * 1)
NORM_EPS, SUBLN_EPS = 1e-6, 1e-5
NEG = -1e30
ROT_HALF = 8
GLA_HEADS, GLA_CHUNK, GLA_TAU = 4, 64, 16.0
LN_EXP_SET = "natural_log_exp_and_others"

GU_T, DN_T, TRI_T, PROJ_T, FF_T = 2 * KD, KF, 3 * KD, 2 * KD, 2 * KD
RAW, SPLIT = 4, 2
SLOT = TRI_T * P
GU_N, DN_N, TRI_N, PROJ_N, FF1_N, FF2_N = KF, KD, KD, KD // 2, KF2 // 2, 2 * KD

STREAM = [
    ("gu0", GU_N, GU_T), ("dn0", DN_N, DN_T),
    ("conv_in", TRI_N, TRI_T), ("conv_out", PROJ_N, PROJ_T),
    ("gu1", GU_N, GU_T), ("dn1", DN_N, DN_T),
    ("gu2", GU_N, GU_T), ("dn2", DN_N, DN_T),
    ("qkv", TRI_N, TRI_T), ("attn_out", PROJ_N, PROJ_T),
    ("gu3", GU_N, GU_T), ("dn3", DN_N, DN_T),
    ("mix_in", TRI_N, TRI_T), ("mix_out", PROJ_N, PROJ_T),
    ("ff1", FF1_N, FF_T), ("ff2", FF2_N, FF_T),
]
FIRST = {}
WIDTH = []
for _name, _n, _t in STREAM:
    FIRST[_name] = len(WIDTH)
    WIDTH += [_t * P] * _n
BLOCKS = len(WIDTH)

COL = {}
_at = 0
for _name, _n in [("ffn1_pre0", 8), ("ffn1_post0", 8), ("mix_pre0", 8), ("mix_post0", 8), ("ffn2_pre0", 8),
                  ("ffn2_post0", 8), ("ffn1_pre1", 8), ("ffn1_post1", 8), ("mix_pre1", 8), ("mix_post1", 8),
                  ("ffn2_pre1", 8), ("ffn2_post1", 8), ("attn_norm", 8), ("mlp_norm", 8), ("final_norm", 8),
                  ("conv_w", 24), ("subln", 1), ("gla_norm", 4), ("lambda", 4)]:
    COL[_name] = _at
    _at += _n
PARAMS = _at


def shape_constants():
    ident = np.eye(P, dtype=np.float32)
    rotate = np.zeros((P, P), np.float32)
    for c in range(2):
        for i in range(ROT_HALF):
            a, b = 64 * c + i, 64 * c + ROT_HALF + i
            rotate[b, a] = -1.0
            rotate[a, b] = 1.0
    j, i = np.arange(P)[:, None], np.arange(P)[None, :]
    same = j // GLA_CHUNK == i // GLA_CHUNK
    upto = (same & (j <= i)).astype(np.float32) / np.float32(GLA_TAU)
    after = (same & (j > i)).astype(np.float32) / np.float32(GLA_TAU)
    squares = np.concatenate([ident, rotate, upto, after], axis=1)

    pos = np.arange(T, dtype=np.float32)
    inv_freq = (np.float32(500000.0) ** (-np.arange(0, 16, 2, dtype=np.float32) / np.float32(16))).astype(np.float32)
    ang = pos[None, :] * inv_freq[:, None]
    cos, sin = np.ones((P, T), np.float32), np.zeros((P, T), np.float32)
    for c in range(2):
        for h in range(2):
            rows = slice(64 * c + ROT_HALF * h, 64 * c + ROT_HALF * (h + 1))
            cos[rows], sin[rows] = np.cos(ang), np.sin(ang)
    q, k = np.arange(P)[:, None], np.arange(P)[None, :]
    mask = np.where(k <= q, 0.0, NEG).astype(np.float32)
    rope_mask = np.concatenate([cos, sin, mask], axis=1)

    d = np.arange(512) - (SEQ - 1)
    n = np.maximum(d, 0)
    large = 16 + (np.log(np.maximum(n, 1) / 16) / math.log(2048 / 16) * 16).astype(np.int32)
    bucket = np.where(n < 16, n, np.minimum(large, 31)).astype(np.int32)
    count = np.zeros(512)
    for window, dilation in ((128, 1), (512, 4), (2048, 16)):
        count += (d >= 0) & (d % dilation == 0) & (d <= window)
    seen = (count > 0) & (d < SEQ)
    onehot = np.zeros((P, 512), np.float32)
    onehot[bucket[seen], np.arange(512)[seen]] = 1.0
    weight = np.where(seen, np.log(np.maximum(count, 1)), NEG).astype(np.float32)
    weight = np.broadcast_to(weight, (HEADS, 512)).copy()
    return squares, rope_mask, onehot, weight


def two_blocks(nc, w, params, h_in, squares, rope_mask, onehot, weight, w_glow, gate_w, rel_bias, out):
    with ExitStack() as ctx:
        def sb(name, shape, dt=F32, at=ctx):
            return at.enter_context(nc.sbuf_tensor(name, shape, dt))

        def sem(name):
            return ctx.enter_context(nc.semaphore(name))

        w_raw = [sb(f"w_raw{i}", [P, SLOT]) for i in range(RAW)]
        w_hi = [sb(f"w_hi{i}", [P, SLOT], F32R) for i in range(SPLIT)]
        w_lo = [sb(f"w_lo{i}", [P, SLOT], F32R) for i in range(SPLIT)]
        x_hi = sb("x_hi", [P, KD, T], F32R)
        x_lo = sb("x_lo", [P, KD, T], F32R)
        h = sb("h", [P, KD, T])
        fx = sb("fx", [P, KD, T])
        par = sb("par", [P, PARAMS])
        eps_col = sb("eps_col", [P, 1])[:, :]
        subln_eps_col = sb("subln_eps_col", [P, 1])[:, :]
        sq4 = sb("sq4", [P, 4 * P])
        ident, rotate, upto, after = (sq4[:, P * i:P * (i + 1)] for i in range(4))
        ones = sb("ones", [P, P])
        ms = sb("ms", [P, T])
        r0 = sb("r0", [P, T])
        rstd = sb("rstd", [P, T])
        rstd_sq = sb("rstd_sq", [P, T])
        small = sb("small", [P, 32])
        with ExitStack() as s:
            hid = [sb(f"hid{i}", [P, 2 * SEQ], at=s) for i in range(2)]
        with ExitStack() as s:
            gate = [sb(f"gate{i}", [P, T], at=s) for i in range(2)]
            up = [sb(f"up{i}", [P, T], at=s) for i in range(2)]
        with ExitStack() as s:
            d_k = [sb(f"d_k{i}", [P, SEQ], at=s) for i in range(2)]
            d_s = [sb(f"d_s{i}", [P, 3 * P], at=s) for i in range(2)]
        with ExitStack() as s:
            square = [sb(f"square{i}", [P, T], at=s) for i in range(2)]
            sumsq = sb("sumsq", [P, T], at=s)
            scaled = [sb(f"scaled{i}", [P, T], at=s) for i in range(2)]
        sb("shared_by_all", [P, 5 * T])
        with ExitStack() as s:
            hid_hi = sb("hid_hi", [P, KF2 * SEQ], F32R, at=s)
            hid_lo = sb("hid_lo", [P, KF2 * SEQ], F32R, at=s)
        with ExitStack() as s:
            y_hi = sb("y_hi", [P, KD, T], F32R, at=s)
            y_lo = sb("y_lo", [P, KD, T], F32R, at=s)
            cv_c = sb("cv_c", [P, T], at=s)
            cv_u = sb("cv_u", [P, T + 2], at=s)
            cv_a = sb("cv_a", [P, T], at=s)
            cv_b = sb("cv_b", [P, T], at=s)
            cv_y = sb("cv_y", [P, T], at=s)
        with ExitStack() as s:
            q_rot = sb("q_rot", [P, HEADS, SEQ], at=s)
            k_rot = sb("k_rot", [P, HEADS, 2, T], at=s)
            v_tok = sb("v_tok", [P, HEADS, 3, P], at=s)
            v_sb = [sb(f"v_sb{i}", [P, T], at=s) for i in range(2)]
            q_sb = [sb(f"q_sb{i}", [P, SEQ], at=s) for i in range(2)]
            k_sb = [sb(f"k_sb{i}", [P, T], at=s) for i in range(2)]
            tabs = sb("tabs", [P, 2 * T + P], at=s)
            cos_t, sin_t, mask = tabs[:, 0:T], tabs[:, T:2 * T], tabs[:, 2 * T:2 * T + P]
            with ExitStack() as s2:
                rope_s = sb("rope_s", [P, T], at=s2)
                rope_c = sb("rope_c", [P, T], at=s2)
            with ExitStack() as s2:
                s_exp = sb("s_exp", [P, 2, 2, 2, T], at=s2)
                a_sb = sb("a_sb", [P, 2, T], at=s2)
                a_tok = sb("a_tok", [P, 5, P], at=s2)
                o_sq = sb("o_sq", [P, QT, P], at=s2)
                o_sb = [sb(f"o_sb{i}", [P, QT, P], at=s2) for i in range(2)]
                o_ss = [sb(f"o_ss{i}", [P, QT], at=s2) for i in range(2)]
                o_ms = [sb(f"o_ms{i}", [P, QT], at=s2) for i in range(2)]
                o_r0 = [sb(f"o_r0{i}", [P, QT], at=s2) for i in range(2)]
                o_r = [sb(f"o_r{i}", [P, QT], at=s2) for i in range(2)]
        with ExitStack() as s:
            proj = sb("proj", [P, 3 * TRI_N, SEQ], at=s)
            bias = sb("bias", [P, HEADS, SEQ], at=s)
            gv_tok = sb("gv_tok", [P, QT, 4 * P], at=s)
            dv_tok = sb("dv_tok", [P, QT, 4 * P], at=s)
            w_glow_sb = sb("w_glow_sb", [P, KD, 16], at=s)
            d_pt = sb("d_pt", [P, 3, P], at=s)
            with ExitStack() as s2:
                d_p = sb("d_p", [P, 3 * P], at=s2)
            gate_w_sb = sb("gate_w_sb", [P, SEQ], at=s)
            glow = sb("glow", [P, SEQ], at=s)
            with ExitStack() as s2:
                onehot_sb = sb("onehot_sb", [P, 512], at=s2)
                weight_sb = sb("weight_sb", [HEADS, 512], at=s2)
                by_dist = sb("by_dist", [HEADS, 512], at=s2)
                rel_sb = sb("rel_sb", [P, HEADS], at=s2)
            with ExitStack() as s2:
                g_a = sb("g_a", [P, QT, SEQ], at=s2)
                g_ls = sb("g_ls", [P, QT, SEQ], at=s2)
                g_eb = sb("g_eb", [P, QT, SEQ], at=s2)
                g_et = sb("g_et", [P, QT, SEQ], at=s2)
                g_q = sb("g_q", [P, GLA_HEADS, SEQ], at=s2)
                g_k = sb("g_k", [P, 2, SEQ], at=s2)
                g_s = sb("g_s", [P, 3, 2, SEQ], at=s2)
            with ExitStack() as s2:
                n_sq = sb("n_sq", [P, GLA_HEADS, SEQ], at=s2)
                n_r0 = sb("n_r0", [P, GLA_HEADS, SEQ], at=s2)
                n_r = sb("n_r", [P, GLA_HEADS, SEQ], at=s2)
                n_ms = sb("n_ms", [P, GLA_HEADS, SEQ], at=s2)
        GQ, GK, GV, GR = 0, 2, 4, 8
        DQ, DK, DV = 12, 13, 14
        g_ke = proj[:, GV:GV + 4, :].rearrange("p (t c) s -> p t c s", t=2)
        g_att = proj[:, GQ:GQ + 4, :].rearrange("p a s -> p (a s)").rearrange("p (n i) -> p n i", n=8)

        by_dist_dram = nc.dram_tensor("by_dist_dram", [HEADS, 512], F32, kind="Internal").ap()
        ps = ctx.enter_context(nc.psum_tensor("ps", [P, 8, 512], F32))
        SUM = 6

        landed = [sem(f"landed{i}") for i in range(RAW)]
        hi_ready, lo_ready, block_used = sem("hi_ready"), sem("lo_ready"), sem("block_used")
        h_loaded, par_loaded, consts_loaded = sem("h_loaded"), sem("par_loaded"), sem("consts_loaded")
        ones_ready, eps_ready = sem("ones_ready"), sem("eps_ready")
        h_sq_ready, h_sq_summed, sumsq_summed_act, sumsq_summed_dve = (
            sem("h_sq_ready"), sem("h_sq_summed"), sem("sumsq_summed_act"), sem("sumsq_summed_dve"))
        ms_ready, ln_ready, r0_ready, newton, rstd_ready = (
            sem("ms_ready"), sem("ln_ready"), sem("r0_ready"), sem("newton"), sem("rstd_ready"))
        x_hi_ready, x_lo_ready = sem("x_hi_ready"), sem("x_lo_ready")
        scaled_ready, h_ready = sem("scaled_ready"), sem("h_ready")
        gu_scaled, act_ready, relu_ready, hid_ready, hid_hi_ready, hid_lo_ready = (
            sem("gu_scaled"), sem("act_ready"), sem("relu_ready"), sem("hid_ready"), sem("hid_hi_ready"),
            sem("hid_lo_ready"))
        f_sq_ready, f_ready, sumsq_ready = sem("f_sq_ready"), sem("f_ready"), sem("sumsq_ready")
        cv_scaled, cv_u_ready, cv_a_ready, cv_step, cv_y_ready, cv_hi_ready, cv_lo_ready = (
            sem("cv_scaled"), sem("cv_u_ready"), sem("cv_a_ready"), sem("cv_step"), sem("cv_y_ready"),
            sem("cv_hi_ready"), sem("cv_lo_ready"))
        tabs_loaded, k_zeroed, part_done, part_copied = (
            sem("tabs_loaded"), sem("k_zeroed"), sem("part_done"), sem("part_copied"))
        tabs_scaled, v_scaled = sem("tabs_scaled"), sem("v_scaled")
        rotated, v_turned, v_tok_ready, rope_step = (
            sem("rotated"), sem("v_turned"), sem("v_tok_ready"), sem("rope_step"))
        lam_step, lam_sum, lam_exp = sem("lam_step"), sem("lam_sum"), sem("lam_exp")
        scores_done, max_step, exp_ready, rs_step, a_step, a_turned, a_tok_ready, o_done = (
            sem("scores_done"), sem("max_step"), sem("exp_ready"), sem("rs_step"), sem("a_step"),
            sem("a_turned"), sem("a_tok_ready"), sem("o_done"))
        o_squared, sub_step, sub_ln, sub_r0_ready, o_scaled, o_turned, out_hi_ready, out_lo_ready = (
            sem("o_squared"), sem("sub_step"), sem("sub_ln"), sem("sub_r0_ready"), sem("o_scaled"),
            sem("o_turned"), sem("out_hi_ready"), sem("out_lo_ready"))
        low_ready, glow_ready = sem("low_ready"), sem("glow_ready")
        mix_part, dv_turned, dv_ready = sem("mix_part"), sem("dv_turned"), sem("dv_ready")
        mix_loaded, mix_zeroed, proj_copied = sem("mix_loaded"), sem("mix_zeroed"), sem("proj_copied")
        dist_done, dist_ready, dist_stored, bias_loaded = (
            sem("dist_done"), sem("dist_ready"), sem("dist_stored"), sem("bias_loaded"))
        g_pe, g_act, g_dve, g_pool = sem("g_pe"), sem("g_act"), sem("g_dve"), sem("g_pool")
        d_k_ready, d_scores, d_s_ready, d_max_step, d_exp, d_p_step, d_turned, d_pt_ready, d_o_done, d_o_copied = (
            sem("d_k_ready"), sem("d_scores"), sem("d_s_ready"), sem("d_max_step"), sem("d_exp"), sem("d_p_step"),
            sem("d_turned"), sem("d_pt_ready"), sem("d_o_done"), sem("d_o_copied"))
        out_ready, stored = sem("out_ready"), sem("stored")

        GU_CREDIT, F_CREDIT, CV_CREDIT = 4, 4, 2

        SUB = [("ffn", "ffn1_pre0", "ffn1_post0", 0), ("conv", "mix_pre0", "mix_post0", None),
               ("ffn", "ffn2_pre0", "ffn2_post0", 1), ("ffn", "ffn1_pre1", "ffn1_post1", 2),
               ("attn", "mix_pre1", "mix_post1", None), ("ffn", "ffn2_pre1", "ffn2_post1", 3)]

        ENTER = ["gu0", "conv_in", "gu1", "gu2", "qkv", "gu3", "mix_in", "ff1"]

        STATE_BANK = (6, 7, 5)
        OUT_AFTER = {5: (0, 1, 2, 3), 6: (4, 5), 7: (6,)}

        def first_col(u):
            return 0 if u <= 4 else META

        def loop(eng, count, body, first=0, peel=0):
            rounds = (count - peel - first) // 4
            if rounds > 1:
                with eng.Fori(0, rounds) as it:
                    for j in range(4):
                        body(it * 4 + (first + j), (first + j) % 4)
            else:
                rounds = 0
            for i in range(first + rounds * 4, count):
                body(i, i % 4)

        def scores_at(i, t, c=None):
            keys = META + P * (t + 1)
            at = t * (META + P)
            b = 2 * (i % 2)
            return ps[:, b:b + 2, at:at + keys] if c is None else ps[:, b + c, at:at + keys]

        block = ctx.enter_context(nc.Block())

        @block.sync
        def _(sp):
            for name, count, tiles in STREAM:
                n0 = FIRST[name]

                def load(i, j):
                    slot = (n0 + j) % RAW
                    if not (isinstance(i, int) and n0 + i < RAW):
                        sp.wait_ge(lo_ready, i + (n0 - RAW + 1))
                    src = w[name][i, :, :] if isinstance(i, int) else w[name][bass.ds(i, 1), :, :].rearrange("a p c -> (a p) c")
                    sp.dma_start(w_raw[slot][:, 0:tiles * P], src).then_inc(landed[slot], 16)

                if n0 == 0:
                    load(0, 0)
                    sp.dma_start(par[:, :], params).then_inc(par_loaded, 16)
                    sp.dma_start(h[:, :, :], h_in).then_inc(h_loaded, 16)
                    for i in range(1, RAW):
                        load(i, i)
                    sp.dma_start(sq4[:, :], squares).then_inc(consts_loaded, 16)
                    loop(sp, count, load, first=RAW)
                else:
                    loop(sp, count, load)
            for k in range(KD):
                sp.wait_ge(out_ready, k + 1)
                sp.dma_start(out[k * P:(k + 1) * P, :], fx[:, k, META:T]).then_inc(stored, 16)
            sp.wait_ge(stored, 16 * KD)

        @block.gpsimd
        def _(pool):
            pool.memset(ones[:, :], 1.0).then_inc(ones_ready, 1)
            pool.wait_ge(block_used, FIRST["qkv"])
            pool.dma_start(tabs[:, :], rope_mask).then_inc(tabs_loaded, 16)
            pool.memset(k_rot[:, :, :, :], 0.0).then_inc(k_zeroed, 1)
            pool.memset(v_tok[:, :, 0, :], 0.0).then_inc(k_zeroed, 1)
            pool.memset(a_tok[:, :, :], 0.0).then_inc(k_zeroed, 1)
            pool.wait_ge(block_used, FIRST["mix_in"])
            pool.memset(rel_sb[:, :], 0.0).then_inc(mix_zeroed, 1)
            pool.memset(gate_w_sb[:, :], 0.0).then_inc(mix_zeroed, 1)
            pool.memset(glow[:, :], 0.0).then_inc(mix_zeroed, 1)
            pool.wait_ge(mix_zeroed, 3)
            pool.memset(glow[32:33, :], 1.0).then_inc(mix_zeroed, 1)
            pool.dma_start(onehot_sb[:, :], onehot).then_inc(mix_loaded, 16)
            pool.dma_start(weight_sb[:, :], weight).then_inc(mix_loaded, 16)
            pool.dma_start(rel_sb[0:32, :], rel_bias).then_inc(mix_loaded, 16)
            pool.dma_start(w_glow_sb[:, :, :], w_glow).then_inc(mix_loaded, 16)
            pool.dma_start(gate_w_sb[0:16, :], gate_w[0:16, :]).then_inc(mix_loaded, 16)
            pool.dma_start(gate_w_sb[32:33, :], gate_w[16:17, :]).then_inc(mix_loaded, 16)
            pool.wait_ge(dist_ready, 1)
            pool.dma_start(by_dist_dram, by_dist[:, :]).then_inc(dist_stored, 16)
            pool.wait_ge(dist_stored, 16)
            toeplitz = bass.AP(tensor=by_dist_dram.tensor, offset=P, ap=[[1, P], [512, HEADS], [1, SEQ]])
            pool.dma_start(bias[:, :, :], toeplitz).then_inc(bias_loaded, 16)
            pool.memset(g_q[:, :, :], 0.0).then_inc(g_pool, 1)
            pool.wait_ge(g_act, 7)
            pool.memset(g_ke[:, :, :, :], 0.0).then_inc(g_pool, 1)
            pool.wait_ge(g_dve, 7)
            pool.wait_ge(g_pe, 6)
            pool.memset(g_att[:, :, :], 0.0).then_inc(g_pool, 1)
            pool.wait_ge(g_dve, 19)
            pool.affine_select(out=g_att, in_=g_att, compare_op=ALU.is_ge, fill=0.0, base=0,
                               pattern=[[0, 8], [1, P]], channel_multiplier=-1).then_inc(g_pool, 1)
            pool.memset(d_k[0][:, :], 0.0).then_inc(g_pool, 1)
            pool.memset(d_k[1][:, :], 0.0).then_inc(g_pool, 1)

        @block.scalar
        def _(act):
            def split_hi(n, j, width):
                act.wait_ge(landed[j], (n // 4 + 1) * 16 if isinstance(n, int) else n * 4 + (16 - 4 * j))
                if not (isinstance(n, int) and n < SPLIT):
                    act.wait_ge(block_used, n - (SPLIT - 1))
                act.activation(w_hi[j % SPLIT][:, 0:width], w_raw[j][:, 0:width], ACT.Copy).then_inc(hi_ready, 1)

            def next_hi(name, count, i, j):
                n0 = FIRST[name]
                if isinstance(i, int):
                    if n0 + i + 2 < BLOCKS:
                        split_hi(n0 + i + 2, (n0 + i + 2) % 4, WIDTH[n0 + i + 2])
                else:
                    split_hi(i + (n0 + 2), (n0 + j + 2) % 4, WIDTH[n0])

            def second_hi(q):
                n = FIRST[ENTER[q]] + 1
                split_hi(n, n % 4, WIDTH[n])

            def root(s, c0, from_psum=False):
                if from_psum:
                    act.wait_ge(sumsq_summed_act, s // 2 + 1)
                    act.activation(r0[:, c0:T], ps[:, SUM + 1, c0:T], ACT.Ln, scale=1.0 / D, bias=eps_col)\
                       .then_inc(ln_ready, 1)
                else:
                    act.wait_ge(ms_ready, s + 1)
                    act.activation(r0[:, c0:T], ms[:, c0:T], ACT.Ln).then_inc(ln_ready, 1)
                act.wait_ge(ln_ready, s + 1)
                act.activation(r0[:, c0:T], r0[:, c0:T], ACT.Exp, scale=-0.5).then_inc(r0_ready, 1)

            def pre_norm(q, s, c0, gain=None):
                for k in range(KD):
                    if q == 0:
                        act.wait_ge(h_loaded, 16)
                    else:
                        act.wait_ge(h_ready, KD * (q - 1) + k + 1)
                    if q == 7 and k == 0:
                        act.wait_ge(block_used, FIRST["ff1"])
                    if gain:
                        g = COL[gain] + k
                        act.activation(x_hi[:, k, c0:T], h[:, k, c0:T], ACT.Copy, scale=par[:, g:g + 1])\
                           .then_inc(x_hi_ready, 1)
                    if KD * q + k >= 2:
                        act.wait_ge(h_sq_summed, KD * q + k - 1)
                    act.activation(square[k % 2][:, c0:T], h[:, k, c0:T], ACT.Square).then_inc(h_sq_ready, 1)
                if q == 0:
                    second_hi(0)
                root(s, c0)

            def take_out(u, m, bank, c0, gain):
                act.wait_ge(sumsq_ready, 9 * u + m)
                act.activation(square[m % 2 if isinstance(m, int) else m_par[0]][:, c0:T], ps[:, bank, c0:T], ACT.Square).then_inc(f_sq_ready, 1)
                g = par[:, bass.ds(m + COL[gain], 1)]
                act.activation(fx[:, m if isinstance(m, int) else bass.ds(m, 1), c0:T], ps[:, bank, c0:T],
                               ACT.Copy, scale=g).then_inc(f_ready, 1)

            m_par = [0]

            def hidden(name, f, c0):
                n0, width = FIRST[name], T - c0

                def silu(i, j):
                    act.wait_ge(gu_scaled, i * 2 + (2 * KF * f + 1 + GU_CREDIT))
                    act.activation(gate[j % 2][:, 0:width], gate[j % 2][:, 0:width], ACT.Silu).then_inc(act_ready, 1)

                def hidden_hi(i, j):
                    act.wait_ge(hid_ready, i + (KF * f + 1))
                    act.activation(hid_hi[:, bass.ds(i * T + c0, width)], up[j % 2][:, 0:width], ACT.Copy)\
                       .then_inc(hid_hi_ready, 1)

                def step(i, j):
                    next_hi(name, GU_N, i, j)
                    silu(i, j)
                    hidden_hi(i - 1, (j + 3) % 4)

                next_hi(name, GU_N, 0, 0)
                silu(0, 0)
                loop(act, GU_N, step, first=1, peel=2)
                hidden_hi(GU_N - 1, (GU_N - 1) % 4)

            def out_projection(name, count, per, u, c0, gain):
                n0 = FIRST[name]

                def step(i, j):
                    act.wait_ge(block_used, i + (n0 + 1))
                    for s in range(per):
                        m_par[0] = (j * per + s) % 2
                        take_out(u, i * per + s, (j * per + s) % 4, c0, gain)
                    next_hi(name, count, i, j)

                loop(act, count - 1, step, peel=1)
                act.wait_ge(block_used, n0 + count)
                for s in range(per):
                    m = (count - 1) * per + s
                    take_out(u, m, m % 4, c0, gain)

            def convolution():
                n0 = FIRST["conv_in"]

                def step(i, j):
                    next_hi("conv_in", TRI_N, i, j)
                    act.wait_ge(cv_u_ready, i + (1 + CV_CREDIT))
                    act.activation(cv_a[:, :], cv_u[:, 0:T], ACT.Copy,
                                   scale=par[:, bass.ds(i + COL["conv_w"], 1)]).then_inc(cv_a_ready, 1)
                    act.wait_ge(cv_y_ready, i + 1)
                    act.activation(y_hi[:, i, :], cv_y[:, :], ACT.Copy).then_inc(cv_hi_ready, 1)

                loop(act, TRI_N, step, peel=2)

            def heads_in():
                n0 = FIRST["qkv"]
                for i in range(HEADS):
                    b, r = 3 * (i % 2), i % 2
                    act.wait_ge(part_done, 2 * i + 2)
                    if i >= 2:
                        act.wait_ge(rope_step, 7 * (i - 1))
                    act.activation(q_sb[r][:, :], ps[:, b + 1, 0:SEQ], ACT.Copy, scale=0.125).then_inc(part_copied, 1)
                    act.wait_ge(block_used, n0 + i + 1)
                    act.activation(k_sb[r][:, :], ps[:, b + 2, 0:T], ACT.Copy).then_inc(part_copied, 1)
                    next_hi("qkv", TRI_N, i, i % 4)
                    act.wait_ge(v_turned, i + 1)
                    if i == 0:
                        act.wait_ge(k_zeroed, 3)
                    act.activation(v_tok[:, i, 1:3, :], ps[:, 7, 0:2 * P].rearrange("p (c v) -> p c v", c=2),
                                   ACT.Copy).then_inc(v_tok_ready, 1)
                    act.activation(v_tok[0:META, i, 0, :], ps[0:META, 7, 2 * P:3 * P], ACT.Copy).then_inc(v_tok_ready, 1)

            def softmax_heads():
                act.wait_ge(lam_sum, 1)
                act.activation(small[:, 2:4], ps[:, 0, 0:2], ACT.Exp).then_inc(lam_exp, 1)

                def exponentials(i):
                    if i >= 2:
                        act.wait_ge(a_step, 4 * (i - 1))
                    for t in range(QT):
                        keys = META + P * (t + 1)
                        act.wait_ge(max_step, 3 * i + 3)
                        for c in range(2):
                            n = 4 * (i % 2) + 2 * t + c
                            act.activation(s_exp[:, i % 2, t, c, 0:keys], scores_at(i, t, c), ACT.Exp,
                                           bias=small[:, 8 + n:9 + n], accum_out=small[:, 16 + n:17 + n])\
                               .then_inc(exp_ready, 1)

                def attention_out(i):
                    r = i % 2
                    act.wait_ge(a_turned, 2 * i + 1)
                    if i >= 1:
                        act.wait_ge(o_done, i)
                    act.activation(a_tok[0:META, 0, :], ps[0:META, 4, 0:P], ACT.Copy).then_inc(a_tok_ready, 1)
                    act.activation(a_tok[:, 1, :], ps[:, 4, P:2 * P], ACT.Copy).then_inc(a_tok_ready, 1)
                    act.wait_ge(a_turned, 2 * i + 2)
                    act.activation(a_tok[0:META, 2, :], ps[0:META, 5, 0:P], ACT.Copy).then_inc(a_tok_ready, 1)
                    act.activation(a_tok[:, 3:5, :], ps[:, 5, P:3 * P].rearrange("p (c q) -> p c q", c=2),
                                   ACT.Copy).then_inc(a_tok_ready, 1)
                    if i >= 2:
                        act.wait_ge(o_scaled, 2 * (i - 1))
                    if i >= 1:
                        act.wait_ge(o_squared, 2 * i)
                    act.wait_ge(o_done, i + 1)
                    for t in range(QT):
                        act.activation(o_sq[:, t, :], ps[:, 6 + r, t * P:(t + 1) * P], ACT.Square,
                                       accum_out=o_ss[r][:, t:t + 1]).then_inc(o_squared, 1)
                    act.wait_ge(o_squared, 2 * i + 2)
                    act.activation(o_r0[r][:, :], o_ss[r][:, :], ACT.Ln, scale=1.0 / P, bias=subln_eps_col).then_inc(sub_ln, 1)
                    act.wait_ge(sub_ln, i + 1)
                    act.activation(o_r0[r][:, :], o_r0[r][:, :], ACT.Exp, scale=-0.5).then_inc(sub_r0_ready, 1)

                def out_hi(i):
                    act.wait_ge(o_turned, i + 1)
                    act.activation(x_hi[:, i, META:T], ps[:, 6 + i % 2, SEQ:2 * SEQ], ACT.Copy, scale=small[:, 5:6])\
                       .then_inc(out_hi_ready, 1)

                exponentials(0)
                for i in range(HEADS):
                    if i + 1 < HEADS:
                        exponentials(i + 1)
                    attention_out(i)
                    if i >= 1:
                        out_hi(i - 1)
                out_hi(HEADS - 1)

            def mixers():
                for k in range(KD):
                    g = COL["attn_norm"] + k
                    act.activation(fx[:, k, META:T], h[:, k, META:T], ACT.Copy, scale=par[:, g:g + 1]).then_inc(low_ready, 1)
                for i in range(3):
                    next_hi("mix_in", TRI_N, i, i)
                act.wait_ge(g_pe, 2)
                act.wait_ge(dist_stored, 16)
                act.activation(g_a[:, :, :], ps[:, 7, :].rearrange("p (t f) -> p t f", t=2), ACT.Abs).then_inc(g_act, 1)
                act.wait_ge(g_act, 1)
                act.activation(g_a[:, :, :], g_a[:, :, :], ACT.Exp, scale=-1.0).then_inc(g_act, 1)
                act.wait_ge(g_act, 2)
                act.activation(g_a[:, :, :], g_a[:, :, :], ACT.Ln, bias=1.0).then_inc(g_act, 1)
                next_hi("mix_in", TRI_N, 3, 3)
                act.wait_ge(g_pe, 4)
                b_t = ps[:, 6, :].rearrange("p (c s) -> p c s", c=2)
                act.activation(g_eb[:, :, :], b_t, ACT.Exp).then_inc(g_act, 1)
                act.activation(g_a[:, :, :], b_t, ACT.Exp, scale=-1.0).then_inc(g_act, 1)
                act.activation(g_et[:, :, :], ps[:, 7, :].rearrange("p (t f) -> p t f", t=2), ACT.Exp).then_inc(g_act, 1)
                act.wait_ge(g_pe, 5)
                act.activation(gv_tok[:, :, :], ps[:, 3:5, :], ACT.Copy).then_inc(g_act, 1)
                act.preload_act_table(ACT.Silu)
                act.wait_ge(proj_copied, GR + 4)
                act.activation(proj[:, GR:GR + 4, :], proj[:, GR:GR + 4, :], ACT.Silu).then_inc(g_act, 1)
                act.preload_act_table_set(LN_EXP_SET)
                next_hi("mix_in", TRI_N, 4, 0)
                act.wait_ge(g_pe, 10)
                act.wait_ge(g_dve, 25)
                act.activation(n_sq[:, :, :].rearrange("p a s -> p (a s)").rearrange("p (b s) -> p b s", b=2),
                               ps[:, 3:5, :], ACT.Square).then_inc(g_act, 1)
                next_hi("mix_in", TRI_N, 5, 1)
                act.wait_ge(g_dve, 26)
                act.activation(n_r0[:, :, :], n_ms[:, :, :], ACT.Ln).then_inc(g_act, 1)
                act.wait_ge(g_act, 10)
                act.activation(n_r0[:, :, :], n_r0[:, :, :], ACT.Exp, scale=-0.5).then_inc(g_act, 1)

                def exponentials(i):
                    if i >= 2:
                        act.wait_ge(d_p_step, 3 * (i - 1))
                    act.wait_ge(d_max_step, 3 * i + 3)
                    for t in range(QT):
                        a, b = (0, P) if t == 0 else (P, 3 * P)
                        n = 2 * (i % 2) + t
                        act.activation(d_s[i % 2][:, a:b], d_s[i % 2][:, a:b], ACT.Exp, bias=small[:, 8 + n:9 + n],
                                       accum_out=small[:, 16 + n:17 + n]).then_inc(d_exp, 1)

                def out_copy(i):
                    act.wait_ge(d_o_done, i + 1)
                    half = slice(64 * (i % 2), 64 * (i % 2) + 64)
                    act.activation(fx[half, 4 + i // 2, META:T], ps[half, 3, 0:SEQ], ACT.Copy).then_inc(d_o_copied, 1)

                def out_hi(k):
                    if k < 4:
                        act.wait_ge(g_dve, GD_DONE - 3 + k)
                    else:
                        act.wait_ge(d_o_copied, 2 * (k - 3))
                    act.activation(x_hi[:, k, META:T], fx[:, k, META:T], ACT.Copy).then_inc(out_hi_ready, 1)

                exponentials(0)
                for i in range(HEADS):
                    if i + 1 < HEADS:
                        exponentials(i + 1)
                    if i >= 1:
                        out_copy(i - 1)
                    if i % 2 == 0:
                        c = i // 2
                        act.wait_ge(dv_turned, c + 1)
                        act.activation(dv_tok[:, :, c * P:(c + 1) * P],
                                       ps[:, 3, SEQ:2 * SEQ].rearrange("p (t v) -> p t v", t=2), ACT.Copy).then_inc(dv_ready, 1)
                    act.wait_ge(d_turned, i + 1)
                    if i >= 1:
                        act.wait_ge(d_o_done, i)
                    act.activation(d_pt[:, :, :], ps[:, 7, 0:3 * P].rearrange("p (c q) -> p c q", c=3), ACT.Copy)\
                       .then_inc(d_pt_ready, 1)
                    if i == 0:
                        next_hi("mix_in", TRI_N, 6, 2)
                    if i == 2:
                        next_hi("mix_in", TRI_N, 7, 3)
                    for k in OUT_AFTER.get(i, ()):
                        out_hi(k)
                out_copy(HEADS - 1)
                out_hi(KD - 1)

            def wide_hidden():
                def step(i, j):
                    next_hi("ff1", FF1_N, i, j)
                    act.wait_ge(hid_ready, i + (4 * KF + 1))
                    act.activation(hid_hi[:, bass.ds(i * 2 * SEQ, 2 * SEQ)], hid[j % 2][:, :], ACT.Copy)\
                       .then_inc(hid_hi_ready, 1)

                loop(act, FF1_N, step, peel=2)

            act.preload_act_table_set(LN_EXP_SET)
            split_hi(0, 0, WIDTH[0])
            act.wait_ge(eps_ready, 2)
            act.wait_ge(par_loaded, 16)
            s = 0
            for u, (kind, pre, post, f) in enumerate(SUB):
                c0 = first_col(u)
                pre_norm(u, s, c0, pre)
                s += 1
                if kind == "ffn":
                    act.preload_act_table(ACT.Silu)
                    hidden(f"gu{f}", f, c0)
                    act.preload_act_table_set(LN_EXP_SET)
                    out_projection(f"dn{f}", DN_N, 1, u, c0, post)
                elif kind == "conv":
                    convolution()
                    out_projection("conv_out", PROJ_N, 2, u, c0, post)
                else:
                    c0 = META
                    heads_in()
                    softmax_heads()
                    out_projection("attn_out", PROJ_N, 2, u, c0, post)
                root(s, c0, from_psum=True)
                s += 1
                second_hi(u + 1)
            pre_norm(6, s, META, "attn_norm")
            s += 1
            mixers()
            for i in range(PROJ_N - 1):
                next_hi("mix_out", PROJ_N, i, i % 4)
            second_hi(7)
            pre_norm(7, s, META, "mlp_norm")
            s += 1
            wide_hidden()
            loop(act, FF2_N - 2, lambda i, j: next_hi("ff2", FF2_N, i, j), peel=0)
            pre_norm(8, s, META)

        @block.vector
        def _(dve):
            def split_lo(n, j, width):
                dve.wait_ge(hi_ready, n + 1)
                dve.tensor_tensor(w_lo[j % SPLIT][:, 0:width], w_raw[j][:, 0:width],
                                  w_hi[j % SPLIT][:, 0:width].bitcast(F32), ALU.subtract).then_inc(lo_ready, 1)

            def next_lo(name, count, i, j):
                n0 = FIRST[name]
                if isinstance(i, int):
                    if n0 + i + 2 < BLOCKS:
                        split_lo(n0 + i + 2, (n0 + i + 2) % 4, WIDTH[n0 + i + 2])
                else:
                    split_lo(i + (n0 + 2), (n0 + j + 2) % 4, WIDTH[n0])

            def root(s, c0, summed, count, eps):
                dve.wait_ge(summed, count)
                dve.tensor_scalar(ms[:, c0:T], ps[:, SUM, c0:T], 1.0 / D, eps, ALU.mult, ALU.add).then_inc(ms_ready, 1)
                dve.wait_ge(r0_ready, s + 1)
                dve.tensor_tensor(rstd[:, c0:T], r0[:, c0:T], r0[:, c0:T], ALU.mult).then_inc(newton, 1)
                dve.wait_ge(newton, 2 * s + 1)
                dve.scalar_tensor_tensor(out=rstd[:, c0:T], in0=rstd[:, c0:T], scalar=-0.5, in1=ms[:, c0:T],
                                         op0=ALU.mult, op1=ALU.mult).then_inc(newton, 1)
                dve.wait_ge(newton, 2 * s + 2)
                dve.scalar_tensor_tensor(out=rstd[:, c0:T], in0=rstd[:, c0:T], scalar=1.5, in1=r0[:, c0:T],
                                         op0=ALU.add, op1=ALU.mult).then_inc(rstd_ready, 1)
                dve.wait_ge(rstd_ready, s + 1)

            def lo_part(q, k, c0, gain):
                g = COL[gain] + k
                dve.wait_ge(x_hi_ready, KD * q + k + 1)
                dve.scalar_tensor_tensor(out=x_lo[:, k, c0:T], in0=h[:, k, c0:T], scalar=par[:, g:g + 1],
                                         in1=x_hi[:, k, c0:T].bitcast(F32), op0=ALU.mult, op1=ALU.subtract)\
                   .then_inc(x_lo_ready, 1)

            def pre_root(q, s, c0):
                root(s, c0, h_sq_summed, KD * (q + 1), NORM_EPS)

            def post_norm(u, s, c0, factor, gain):
                root(s, c0, sumsq_summed_dve, u + 1, NORM_EPS)
                for k in range(KD + 2):
                    if k < KD:
                        if k >= 2:
                            dve.wait_ge(h_ready, KD * u + k - 1)
                        dve.tensor_tensor(scaled[k % 2][:, c0:T], fx[:, k, c0:T], rstd[:, c0:T], ALU.mult)\
                           .then_inc(scaled_ready, 1)
                    if 1 <= k <= KD:
                        dve.wait_ge(scaled_ready, KD * u + k)
                        dve.scalar_tensor_tensor(out=h[:, k - 1, c0:T], in0=scaled[(k - 1) % 2][:, c0:T], scalar=factor,
                                                 in1=h[:, k - 1, c0:T], op0=ALU.mult, op1=ALU.add).then_inc(h_ready, 1)
                    if k >= 2:
                        lo_part(u + 1, k - 2, c0, gain)

            def hidden(name, f, c0):
                width = T - c0

                def take(i, j):
                    dve.wait_ge(block_used, i + (FIRST[name] + 1))
                    if not isinstance(i, int) or i >= 2:
                        dve.wait_ge(hid_lo_ready, i + (KF * f - 1))
                    dve.tensor_tensor(gate[j % 2][:, 0:width], rstd[:, c0:T], ps[:, 2 * (j % 2), c0:T], ALU.mult)\
                       .then_inc(gu_scaled, 1)
                    dve.tensor_tensor(up[j % 2][:, 0:width], rstd[:, c0:T], ps[:, 2 * (j % 2) + 1, c0:T], ALU.mult)\
                       .then_inc(gu_scaled, 1)

                def times_gate(i, j):
                    t = up[j % 2][:, 0:width]
                    dve.wait_ge(act_ready, i + (KF * f + 1))
                    dve.wait_ge(gu_scaled, i * 2 + (2 * KF * f + 2 + GU_CREDIT))
                    dve.tensor_tensor(t, t, gate[j % 2][:, 0:width], ALU.mult).then_inc(hid_ready, 1)

                def hidden_lo(i, j):
                    at = i * T + c0
                    dve.wait_ge(hid_hi_ready, i + (KF * f + 1))
                    dve.tensor_tensor(hid_lo[:, bass.ds(at, width)], up[j % 2][:, 0:width],
                                      hid_hi[:, bass.ds(at, width)].bitcast(F32), ALU.subtract).then_inc(hid_lo_ready, 1)

                def step(i, j):
                    take(i, j)
                    times_gate(i - 1, (j + 3) % 4)
                    next_lo(name, GU_N, i, j)
                    hidden_lo(i - 1, (j + 3) % 4)

                take(0, 0)
                next_lo(name, GU_N, 0, 0)
                step(1, 1)
                loop(dve, GU_N, step, first=2, peel=2)
                times_gate(GU_N - 1, (GU_N - 1) % 4)
                hidden_lo(GU_N - 1, (GU_N - 1) % 4)

            def add_square(u, m, par_, c0):
                dve.wait_ge(f_sq_ready, m + (KD * u + 1))
                dve.wait_ge(sumsq_ready, m + (9 * u + 1))
                dve.tensor_tensor(sumsq[:, c0:T], sumsq[:, c0:T], square[par_][:, c0:T], ALU.add).then_inc(sumsq_ready, 1)

            def out_projection(name, count, per, u, c0):
                if u > 0:
                    dve.wait_ge(h_ready, KD * u)
                dve.wait_ge(hid_lo_ready, 1)
                dve.memset(sumsq[:, :], 0.0).then_inc(sumsq_ready, 1)

                def step(i, j):
                    for s in range(per):
                        add_square(u, i * per + s, (j * per + s) % 2, c0)
                    next_lo(name, count, i, j)

                loop(dve, count - 1, step, peel=1)
                for s in range(per):
                    m = (count - 1) * per + s
                    add_square(u, m, m % 2, c0)

            def convolution():
                dve.tensor_tensor(rstd_sq[:, :], rstd[:, :], rstd[:, :], ALU.mult).then_inc(cv_step, 1)
                dve.memset(cv_u[:, 0:2], 0.0).then_inc(cv_u_ready, CV_CREDIT)
                dve.wait_ge(cv_step, 1)

                def step(i, j):
                    b = 3 * (j % 2)
                    w1 = par[:, bass.ds(i + (COL["conv_w"] + KD), 1)]
                    w2 = par[:, bass.ds(i + (COL["conv_w"] + 2 * KD), 1)]
                    dve.wait_ge(block_used, i + (FIRST["conv_in"] + 1))
                    dve.tensor_tensor(cv_c[:, :], rstd_sq[:, :], ps[:, b + 1, 0:T], ALU.mult).then_inc(cv_scaled, 1)
                    dve.tensor_tensor(cv_b[:, :], rstd[:, :], ps[:, b, 0:T], ALU.mult).then_inc(cv_scaled, 1)
                    dve.wait_ge(cv_scaled, i * 2 + 1)
                    dve.tensor_tensor(cv_u[:, 2:T + 2], cv_c[:, :], ps[:, b + 2, 0:T], ALU.mult).then_inc(cv_u_ready, 1)
                    next_lo("conv_in", TRI_N, i, j)
                    dve.wait_ge(cv_a_ready, i + 1)
                    dve.scalar_tensor_tensor(out=cv_a[:, :], in0=cv_u[:, 1:T + 1], scalar=w1, in1=cv_a[:, :],
                                             op0=ALU.mult, op1=ALU.add).then_inc(cv_step, 1)
                    dve.wait_ge(cv_step, i * 2 + 2)
                    dve.scalar_tensor_tensor(out=cv_a[:, :], in0=cv_u[:, 2:T + 2], scalar=w2, in1=cv_a[:, :],
                                             op0=ALU.mult, op1=ALU.add).then_inc(cv_step, 1)
                    dve.wait_ge(cv_step, i * 2 + 3)
                    dve.tensor_tensor(cv_y[:, :], cv_a[:, :], cv_b[:, :], ALU.mult).then_inc(cv_y_ready, 1)
                    dve.wait_ge(cv_hi_ready, i + 1)
                    dve.tensor_tensor(y_lo[:, i, :], cv_y[:, :], y_hi[:, i, :].bitcast(F32), ALU.subtract)\
                       .then_inc(cv_lo_ready, 1)

                loop(dve, TRI_N, step, peel=2)

            def lam():
                c = COL["lambda"]
                dve.wait_ge(k_zeroed, 3)
                dve.tensor_tensor(small[:, 0:2], par[:, c:c + 4:2], par[:, c + 1:c + 4:2], ALU.mult).then_inc(lam_step, 1)

            def heads_in():
                dve.wait_ge(tabs_loaded, 16)
                dve.wait_ge(k_zeroed, 3)
                dve.tensor_tensor(cos_t, cos_t, rstd[:, :], ALU.mult).then_inc(tabs_scaled, 1)
                dve.tensor_tensor(sin_t, sin_t, rstd[:, :], ALU.mult).then_inc(tabs_scaled, 1)
                dve.wait_ge(tabs_scaled, 2)
                for i in range(HEADS):
                    r = i % 2
                    dve.wait_ge(part_done, 2 * i + 1)
                    if i >= 2:
                        dve.wait_ge(v_turned, i - 1)
                    dve.tensor_tensor(v_sb[r][:, :], rstd[:, :], ps[:, 3 * r, 0:T], ALU.mult).then_inc(v_scaled, 1)
                    n = 7 * i
                    dve.wait_ge(rotated, 2 * i + 1)
                    if i >= 1:
                        dve.wait_ge(rope_step, n)
                    dve.tensor_tensor(rope_s[:, 0:SEQ], sin_t[:, META:T], ps[:, 3 * r + 1, SEQ:2 * SEQ], ALU.mult).then_inc(rope_step, 1)
                    dve.tensor_tensor(rope_c[:, 0:SEQ], q_sb[r][:, :], cos_t[:, META:T], ALU.mult).then_inc(rope_step, 1)
                    dve.wait_ge(rope_step, n + 2)
                    dve.tensor_tensor(q_rot[:, i, :], rope_s[:, 0:SEQ], rope_c[:, 0:SEQ], ALU.add).then_inc(rope_step, 1)
                    dve.wait_ge(rotated, 2 * i + 2)
                    dve.wait_ge(rope_step, n + 3)
                    dve.tensor_tensor(rope_s[:, :], sin_t, ps[:, 6, 0:T], ALU.mult).then_inc(rope_step, 1)
                    dve.tensor_tensor(rope_c[:, :], k_sb[r][:, :], cos_t, ALU.mult).then_inc(rope_step, 1)
                    dve.wait_ge(rope_step, n + 5)
                    for c in range(2):
                        rows = slice(64 * c, 64 * c + 64)
                        dve.tensor_tensor(k_rot[rows, i, c, :], rope_s[rows, :], rope_c[rows, :], ALU.add)\
                           .then_inc(rope_step, 1)
                    next_lo("qkv", TRI_N, i, i % 4)

            def softmax_heads():
                dve.wait_ge(lam_exp, 1)
                dve.scalar_tensor_tensor(out=small[:, 4:5], in0=small[:, 3:4], scalar=-LAMBDA_INIT, in1=small[:, 2:3],
                                         op0=ALU.add, op1=ALU.subtract).then_inc(lam_step, 1)
                c = COL["subln"]
                dve.tensor_scalar(small[:, 5:6], par[:, c:c + 1], 1.0 - LAMBDA_INIT, None, ALU.mult).then_inc(lam_step, 1)
                dve.wait_ge(rope_step, 7 * HEADS)

                def maxima(i):
                    o = 4 * (i % 2)
                    dve.wait_ge(scores_done, i + 1)
                    if i >= 1:
                        dve.wait_ge(max_step, 3 * i)
                    for t in range(QT):
                        dve.tensor_reduce(small[:, 24 + 2 * t:26 + 2 * t], scores_at(i, t), AX.X, ALU.max).then_inc(max_step, 1)
                    dve.wait_ge(max_step, 3 * i + 2)
                    dve.tensor_scalar(small[:, 8 + o:12 + o], small[:, 24:28], -1.0, None, ALU.mult).then_inc(max_step, 1)

                def difference(i):
                    o = 4 * (i % 2)
                    dve.wait_ge(exp_ready, 4 * i + 4)
                    if i >= 1:
                        dve.wait_ge(a_turned, 2 * i)
                        dve.wait_ge(a_step, 4 * i)
                    rs, cl = small[:, 16 + o:20 + o], small[:, 28:30]
                    dve.reciprocal(rs, rs).then_inc(rs_step, 1)
                    dve.wait_ge(rs_step, 2 * i + 1)
                    dve.tensor_scalar(cl, small[:, 17 + o:20 + o:2], small[:, 4:5], None, ALU.mult).then_inc(rs_step, 1)
                    for t in range(QT):
                        keys = META + P * (t + 1)
                        dve.tensor_scalar(a_sb[:, t, 0:keys], s_exp[:, i % 2, t, 0, 0:keys],
                                          small[:, 16 + o + 2 * t:17 + o + 2 * t], None, ALU.mult).then_inc(a_step, 1)
                    dve.wait_ge(rs_step, 2 * i + 2)
                    for t in range(QT):
                        keys = META + P * (t + 1)
                        dve.wait_ge(a_step, 4 * i + 1 + t)
                        dve.scalar_tensor_tensor(out=a_sb[:, t, 0:keys], in0=s_exp[:, i % 2, t, 1, 0:keys],
                                                 scalar=small[:, 28 + t:29 + t], in1=a_sb[:, t, 0:keys],
                                                 op0=ALU.mult, op1=ALU.add).then_inc(a_step, 1)

                def sub_norm(i):
                    r = i % 2
                    dve.wait_ge(o_squared, 2 * i + 2)
                    dve.tensor_scalar(o_ms[r][:, :], o_ss[r][:, :], 1.0 / P, SUBLN_EPS, ALU.mult, ALU.add).then_inc(sub_step, 1)
                    dve.wait_ge(sub_r0_ready, i + 1)
                    newton_steps(o_ms[r][:, :], o_r0[r][:, :], o_r[r][:, :], sub_step, 4 * i + 1)
                    if i >= 2:
                        dve.wait_ge(o_turned, i - 1)
                    for t in range(QT):
                        dve.tensor_scalar(o_sb[r][:, t, :], ps[:, 6 + r, t * P:(t + 1) * P], o_r[r][:, t:t + 1], None,
                                          ALU.mult).then_inc(o_scaled, 1)

                def out_lo(i):
                    dve.wait_ge(out_hi_ready, i + 1)
                    dve.scalar_tensor_tensor(out=x_lo[:, i, META:T], in0=ps[:, 6 + i % 2, SEQ:2 * SEQ], scalar=small[:, 5:6],
                                             in1=x_hi[:, i, META:T].bitcast(F32), op0=ALU.mult, op1=ALU.subtract)\
                       .then_inc(out_lo_ready, 1)

                maxima(0)
                for i in range(HEADS):
                    if i + 1 < HEADS:
                        maxima(i + 1)
                    difference(i)
                    if i >= 1:
                        sub_norm(i - 1)
                    if i >= 2:
                        out_lo(i - 2)
                sub_norm(HEADS - 1)
                out_lo(HEADS - 2)
                out_lo(HEADS - 1)

            def newton_steps(ms_, r0_, r_, step_sem, base):
                dve.tensor_tensor(r_, r0_, r0_, ALU.mult).then_inc(step_sem, 1)
                dve.wait_ge(step_sem, base + 1)
                dve.scalar_tensor_tensor(out=r_, in0=r_, scalar=-0.5, in1=ms_, op0=ALU.mult, op1=ALU.mult).then_inc(step_sem, 1)
                dve.wait_ge(step_sem, base + 2)
                dve.scalar_tensor_tensor(out=r_, in0=r_, scalar=1.5, in1=r0_, op0=ALU.add, op1=ALU.mult).then_inc(step_sem, 1)
                dve.wait_ge(step_sem, base + 3)

            def distances():
                dve.wait_ge(dist_done, 1)
                dve.tensor_tensor(by_dist[:, :], weight_sb[:, :], ps[0:HEADS, 7, :], ALU.add).then_inc(dist_ready, 1)

            def take(i, s):
                if i < 4:
                    bank = 3 * (i % 2) + s
                    dve.wait_ge(block_used, FIRST["mix_in"] + i + 1)
                else:
                    bank = s
                    if s < 2:
                        dve.wait_ge(mix_part, 2 * (i - 4) + s + 1)
                    else:
                        dve.wait_ge(block_used, FIRST["mix_in"] + i + 1)
                dve.tensor_tensor(proj[:, 3 * i + s, :], rstd[:, META:T], ps[:, bank, 0:SEQ], ALU.mult).then_inc(proj_copied, 1)

            def gated():
                for i in range(4):
                    for s in range(3):
                        take(i, s)
                    next_lo("mix_in", TRI_N, i, i)
                    if i == 0:
                        distances()
                    if i == 1:
                        dve.wait_ge(g_pe, 1)
                        dve.tensor_tensor(glow[0:16, :], rstd[0:16, META:T], ps[0:16, 6, 0:SEQ], ALU.mult).then_inc(glow_ready, 1)
                    if i == 2:
                        dve.wait_ge(g_act, 1)
                        dve.tensor_scalar(g_ls[:, :, :], ps[:, 7, :].rearrange("p (t f) -> p t f", t=2), 0.0, None, ALU.min)\
                           .then_inc(g_dve, 1)
                        dve.wait_ge(g_dve, 1)
                        dve.wait_ge(g_act, 3)
                        dve.tensor_tensor(g_ls[:, :, :], g_ls[:, :, :], g_a[:, :, :], ALU.subtract).then_inc(g_dve, 1)
                dve.wait_ge(g_act, 5)
                dve.wait_ge(g_pool, 1)
                for i in range(GLA_HEADS):
                    rows, c = slice(64 * (i % 2), 64 * (i % 2) + 64), i // 2
                    dve.scalar_tensor_tensor(out=g_q[rows, i, :], in0=proj[rows, GQ + c, :], scalar=0.125,
                                             in1=g_eb[rows, c, :], op0=ALU.mult, op1=ALU.mult).then_inc(g_dve, 1)
                dve.tensor_tensor(g_k[:, :, :], proj[:, GK:GK + 2, :], g_a[:, :, :], ALU.mult).then_inc(g_dve, 1)
                take(4, 0)
                dve.wait_ge(g_act, 6)
                dve.wait_ge(g_pool, 2)
                for t in range(QT):
                    for c in range(2):
                        rows = slice(64 * c, 64 * c + 64)
                        dve.tensor_tensor(g_ke[rows, t, c, :], g_et[rows, t, :], ps[rows, 5, t * SEQ:(t + 1) * SEQ],
                                          ALU.mult).then_inc(g_dve, 1)
                take(4, 1)
                dve.wait_ge(g_pe, 8)
                dve.wait_ge(g_pool, 3)
                for c in range(2):
                    rows = slice(64 * c, 64 * c + 64)
                    for b in range(2):
                        half = ps[rows, 3 + b, :].rearrange("p (n i) -> p n i", n=4)[:, :, rows]
                        dve.tensor_copy(g_att[rows, 4 * b:4 * b + 4, rows], half).then_inc(g_dve, 2)
                take(4, 2)
                next_lo("mix_in", TRI_N, 4, 0)
                dve.wait_ge(g_pe, 9)
                for c in range(3):
                    for p in range(2):
                        inc = ps[:, STATE_BANK[c], p * SEQ:(p + 1) * SEQ]
                        if c == 0:
                            dve.tensor_copy(g_s[:, 0, p, :], inc).then_inc(g_dve, 1)
                        else:
                            last = GLA_CHUNK * (c + 1) - 1
                            dve.wait_ge(g_dve, 19 + 2 * c - 1 + p)
                            dve.scalar_tensor_tensor(out=g_s[:, c, p, :], in0=g_s[:, c - 1, p, :],
                                                     scalar=g_eb[:, p, last:last + 1], in1=inc,
                                                     op0=ALU.mult, op1=ALU.add).then_inc(g_dve, 1)
                for s in range(3):
                    take(5, s)
                next_lo("mix_in", TRI_N, 5, 1)
                take(6, 0)
                dve.wait_ge(g_pe, 11)
                dve.tensor_scalar(n_ms[:, :, :].rearrange("p a s -> p (a s)").rearrange("p (b s) -> p b s", b=2),
                                  ps[:, 6:8, :], 1.0 / P, NORM_EPS, ALU.mult, ALU.add).then_inc(g_dve, 1)
                take(6, 1)
                dve.wait_ge(g_act, 11)
                newton_steps(n_ms[:, :, :], n_r0[:, :, :], n_r[:, :, :], g_dve, 26)
                for i in range(GLA_HEADS):
                    dve.tensor_tensor(n_r[:, i, :], n_r[:, i, :], ps[:, 3 + i // 2, (i % 2) * SEQ:(i % 2 + 1) * SEQ],
                                      ALU.mult).then_inc(g_dve, 1)
                take(6, 2)
                for i in range(GLA_HEADS):
                    dve.wait_ge(g_dve, 30 + i)
                    c = COL["gla_norm"] + i
                    dve.scalar_tensor_tensor(out=fx[:, i, META:T], in0=n_r[:, i, :], scalar=par[:, c:c + 1],
                                             in1=proj[:, GR + i, :], op0=ALU.mult, op1=ALU.mult).then_inc(g_dve, 1)

            def dilated():
                def key(i):
                    rows = slice(64 * (i % 2), 64 * (i % 2) + 64)
                    if i == 0:
                        dve.wait_ge(g_pool, 6)
                    if i >= 2:
                        dve.wait_ge(d_scores, i - 1)
                    dve.tensor_scalar(d_k[i % 2][rows, :], proj[rows, DK + 3 * (i // 2), :], 0.125, None, ALU.mult)\
                       .then_inc(d_k_ready, 1)

                def biased(i):
                    d, n = d_s[i % 2], 2 * (i % 2)
                    dve.wait_ge(d_scores, i + 1)
                    if i >= 2:
                        dve.wait_ge(d_p_step, 3 * (i - 1))
                    dve.tensor_tensor(d[:, 0:P], ps[:, 5 + i % 2, 0:P], bias[:, i, P - 1::-1], ALU.add).then_inc(d_s_ready, 1)
                    dve.tensor_tensor(d[:, P:3 * P], ps[:, 5 + i % 2, P:3 * P], bias[:, i, ::-1], ALU.add).then_inc(d_s_ready, 1)
                    if i >= 1:
                        dve.wait_ge(d_max_step, 3 * i)
                    for t in range(QT):
                        a, b = (0, P) if t == 0 else (P, 3 * P)
                        dve.wait_ge(d_s_ready, 2 * i + t + 1)
                        dve.tensor_reduce(small[:, 24 + t:25 + t], d[:, a:b], AX.X, ALU.max).then_inc(d_max_step, 1)
                    dve.wait_ge(d_max_step, 3 * i + 2)
                    dve.tensor_scalar(small[:, 8 + n:10 + n], small[:, 24:26], -1.0, None, ALU.mult).then_inc(d_max_step, 1)

                def normalised(i):
                    n = 2 * (i % 2)
                    dve.wait_ge(d_exp, 2 * i + 2)
                    rs = small[:, 16 + n:18 + n]
                    dve.reciprocal(rs, rs).then_inc(d_p_step, 1)
                    if i >= 1:
                        dve.wait_ge(d_turned, i)
                    dve.wait_ge(d_p_step, 3 * i + 1)
                    for t in range(QT):
                        a, b = (0, P) if t == 0 else (P, 3 * P)
                        dve.tensor_scalar(d_p[:, a:b], d_s[i % 2][:, a:b], small[:, 16 + n + t:17 + n + t], None, ALU.mult)\
                           .then_inc(d_p_step, 1)

                def out_lo(k):
                    dve.wait_ge(out_hi_ready, KD + k + 1)
                    dve.tensor_tensor(x_lo[:, k, META:T], fx[:, k, META:T], x_hi[:, k, META:T].bitcast(F32),
                                      ALU.subtract).then_inc(out_lo_ready, 1)

                key(0)
                key(1)
                take(7, 0)
                dve.wait_ge(bias_loaded, 16)
                biased(0)
                for i in range(HEADS):
                    if i + 1 < HEADS:
                        biased(i + 1)
                    if i + 2 < HEADS:
                        key(i + 2)
                    normalised(i)
                    if i < 2:
                        take(7, i + 1)
                    if i == 1:
                        next_lo("mix_in", TRI_N, 6, 2)
                    if i == 3:
                        next_lo("mix_in", TRI_N, 7, 3)
                    for k in OUT_AFTER.get(i - 1, ()):
                        out_lo(k)
                for k in OUT_AFTER[HEADS - 1] + (KD - 1,):
                    out_lo(k)

            def residual(m, j, u):
                hm = h[:, m, META:T] if isinstance(m, int) else h[:, bass.ds(m, 1), META:T]
                dve.tensor_tensor(hm, hm, ps[:, j % 4, META:T], ALU.add).then_inc(h_ready, 1)

            def wide_hidden():

                def step(i, j):
                    t = hid[j % 2][:, :]
                    dve.wait_ge(block_used, i + (FIRST["ff1"] + 1))
                    for c in range(2):
                        dve.scalar_tensor_tensor(out=t[:, c * SEQ:(c + 1) * SEQ], in0=ps[:, 2 * (j % 2) + c, 0:SEQ], scalar=0.0,
                                                 in1=rstd[:, META:T], op0=ALU.max, op1=ALU.mult).then_inc(relu_ready, 1)
                    dve.wait_ge(relu_ready, i * 2 + 2)
                    dve.tensor_tensor(t, t, t, ALU.mult).then_inc(hid_ready, 1)
                    next_lo("ff1", FF1_N, i, j)
                    dve.wait_ge(hid_hi_ready, i + (4 * KF + 1))
                    dve.tensor_tensor(hid_lo[:, bass.ds(i * 2 * SEQ, 2 * SEQ)], t,
                                      hid_hi[:, bass.ds(i * 2 * SEQ, 2 * SEQ)].bitcast(F32), ALU.subtract)\
                       .then_inc(hid_lo_ready, 1)

                loop(dve, FF1_N, step, peel=2)

            def second_lo(q):
                n = FIRST[ENTER[q]] + 1
                split_lo(n, n % 4, WIDTH[n])

            dve.memset(small[:, 30:31], 0.0).then_inc(gu_scaled, GU_CREDIT)
            dve.memset(eps_col, NORM_EPS).then_inc(eps_ready, 1)
            dve.memset(subln_eps_col, SUBLN_EPS).then_inc(eps_ready, 1)
            dve.memset(small[:, 29:30], 0.0).then_inc(f_ready, F_CREDIT)
            split_lo(0, 0, WIDTH[0])
            dve.wait_ge(par_loaded, 16)
            for k in range(KD):
                lo_part(0, k, 0, "ffn1_pre0")
            gains = [pre for _, pre, _, _ in SUB[1:]] + ["attn_norm"]
            s = 0
            for u, (kind, pre, post, f) in enumerate(SUB):
                c0 = first_col(u)
                if u == 0:
                    second_lo(0)
                pre_root(u, s, c0)
                s += 1
                if kind == "ffn":
                    hidden(f"gu{f}", f, c0)
                    out_projection(f"dn{f}", DN_N, 1, u, c0)
                elif kind == "conv":
                    convolution()
                    out_projection("conv_out", PROJ_N, 2, u, c0)
                else:
                    c0 = META
                    lam()
                    heads_in()
                    softmax_heads()
                    out_projection("attn_out", PROJ_N, 2, u, c0)
                post_norm(u, s, c0, 0.5 if kind == "ffn" else 1.0, gains[u])
                s += 1
                second_lo(u + 1)
            pre_root(6, s, META)
            s += 1
            gated()
            dilated()
            for i in range(PROJ_N):
                dve.wait_ge(block_used, FIRST["mix_out"] + i + 1)
                residual(2 * i, 2 * i, 6)
                residual(2 * i + 1, 2 * i + 1, 6)
                if i < PROJ_N - 1:
                    next_lo("mix_out", PROJ_N, i, i)
            for k in range(KD):
                lo_part(7, k, META, "mlp_norm")
            second_lo(7)
            pre_root(7, s, META)
            s += 1
            wide_hidden()
            n0 = FIRST["ff2"]
            for m in range(KD):
                dve.wait_ge(block_used, n0 + 2 * m + 1)
                if 2 * m + 2 < FF2_N:
                    next_lo("ff2", FF2_N, 2 * m, 2 * m % 4)
                dve.wait_ge(block_used, n0 + 2 * m + 2)
                residual(m, m, 7)
                if 2 * m + 3 < FF2_N:
                    next_lo("ff2", FF2_N, 2 * m + 1, (2 * m + 1) % 4)
            dve.wait_ge(h_ready, 8 * KD)
            root(s, META, h_sq_summed, 9 * KD, NORM_EPS)
            for k in range(KD):
                g = COL["final_norm"] + k
                dve.scalar_tensor_tensor(out=fx[:, k, META:T], in0=h[:, k, META:T], scalar=par[:, g:g + 1],
                                         in1=rstd[:, META:T], op0=ALU.mult, op1=ALU.mult).then_inc(out_ready, 1)

        @block.tensor
        def _(pe):
            def product(out_ap, slot, t0, tiles, hi, lo, start=True, stop=True, before=None, step=1):
                for k in range(tiles):
                    if before:
                        before(k)
                    cols = slice((t0 + k) * P, (t0 + k + 1) * P)
                    first, last = start and k == 0, stop and k == tiles - 1
                    pe.matmul(out_ap, w_hi[slot][:, cols], hi(k), start=first, stop=False)
                    pe.matmul(out_ap, w_hi[slot][:, cols], lo(k), start=False, stop=False)
                    mm = pe.matmul(out_ap, w_lo[slot][:, cols], hi(k), start=False, stop=last)
                return mm

            def x_parts(c0):
                return (lambda k: x_hi[:, k, c0:T]), (lambda k: x_lo[:, k, c0:T])

            def split_ready(n0, i):
                pe.wait_ge(lo_ready, i + (n0 + 1))

            def first_block(q, n0, parts, c0):
                split_ready(n0, 0)
                for k in range(KD):
                    pe.wait_ge(x_lo_ready, KD * q + k + 1)
                    for s, (o, first_col_) in enumerate(parts):
                        cols = slice((s * KD + k) * P, (s * KD + k + 1) * P)
                        hi, lo = x_hi[:, k, first_col_:T], x_lo[:, k, first_col_:T]
                        pe.matmul(o, w_hi[0][:, cols], hi, start=k == 0, stop=False)
                        pe.matmul(o, w_hi[0][:, cols], lo, start=False, stop=False)
                        mm = pe.matmul(o, w_lo[0][:, cols], hi, start=False, stop=k == KD - 1)
                        if k == KD - 1 and s == len(parts) - 1:
                            mm.then_inc(block_used, 1)
                    pe.wait_ge(h_sq_ready, KD * q + k + 1)
                    pe.matmul(ps[:, SUM, c0:T], ones[:, :], square[k % 2][:, c0:T], start=k == 0, stop=k == KD - 1)\
                      .then_inc(h_sq_summed, 1)

            def hidden(name, f, q, c0):
                n0 = FIRST[name]
                hi, lo = x_parts(c0)
                first_block(q, n0, [(ps[:, 0, c0:T], c0), (ps[:, 1, c0:T], c0)], c0)

                def step(i, j):
                    split_ready(n0, i)
                    pe.wait_ge(gu_scaled, i * 2 + (2 * KF * f + 2))
                    product(ps[:, 2 * (j % 2), c0:T], j % 2, 0, KD, hi, lo)
                    product(ps[:, 2 * (j % 2) + 1, c0:T], j % 2, KD, KD, hi, lo).then_inc(block_used, 1)

                step(1, 1)
                loop(pe, GU_N, step, first=2)

            def down(name, f, u, c0):
                n0 = FIRST[name]
                hi = lambda k: hid_hi[:, k * T + c0:(k + 1) * T]
                lo = lambda k: hid_lo[:, k * T + c0:(k + 1) * T]

                def step(i, j):
                    split_ready(n0, i)
                    pe.wait_ge(f_ready, i + (KD * u + 1))
                    before = (lambda k: pe.wait_ge(hid_lo_ready, KF * f + k + 1) if k >= KF - 4 else None) if j == 0 else None
                    product(ps[:, j, c0:T], j % 2, 0, KF, hi, lo, before=before).then_inc(block_used, 1)

                loop(pe, DN_N, step)

            def keep_warm(count):
                pe.wait_ge(consts_loaded, 16)
                for _ in range(count):
                    pe.matmul(ps[:, 5, :], ones[:, :], sq4[:, :], start=True, stop=True)

            def sum_squares(u, c0):
                pe.wait_ge(sumsq_ready, 9 * (u + 1))
                pe.matmul(ps[:, SUM + 1, c0:T], ones[:, :], sumsq[:, c0:T], start=True, stop=True).then_inc(sumsq_summed_act, 1)
                pe.matmul(ps[:, SUM, c0:T], ones[:, :], sumsq[:, c0:T], start=True, stop=True).then_inc(sumsq_summed_dve, 1)
                keep_warm(5)

            def pre_norm(q, c0):
                for k in range(KD):
                    pe.wait_ge(h_sq_ready, KD * q + k + 1)
                    pe.matmul(ps[:, SUM, c0:T], ones[:, :], square[k % 2][:, c0:T], start=k == 0, stop=k == KD - 1)\
                      .then_inc(h_sq_summed, 1)

            def convolution(q):
                n0 = FIRST["conv_in"]
                hi, lo = x_parts(0)

                first_block(q, n0, [(ps[:, s, 0:T], 0) for s in range(3)], 0)

                def step(i, j):
                    b = 3 * (j % 2)
                    split_ready(n0, i)
                    if not isinstance(i, int) or i >= 2:
                        pe.wait_ge(cv_u_ready, i - 1 + CV_CREDIT)
                    for s in range(3):
                        mm = product(ps[:, b + s, 0:T], j % 2, s * KD, KD, hi, lo)
                    mm.then_inc(block_used, 1)

                loop(pe, TRI_N, step, first=1)
                pe.wait_ge(cv_u_ready, TRI_N - 1 + CV_CREDIT)

            def out_projection(name, u, hi, lo, ready, sem_, base, c0):
                n0 = FIRST[name]
                for i in range(PROJ_N):
                    split_ready(n0, i)
                    pe.wait_ge(sem_, base + 2 * i + 2)
                    for s in range(2):
                        before = (lambda k: pe.wait_ge(ready[0], ready[1] + k + 1)) if i == 0 and s == 0 else None
                        mm = product(ps[:, (2 * i + s) % 4, c0:T], i % 2, s * KD, KD, hi, lo, before=before)
                    mm.then_inc(block_used, 1)

            def heads_in(q):
                n0 = FIRST["qkv"]
                for i in range(HEADS):
                    b, r = 3 * (i % 2), i % 2
                    if i == 0:
                        first_block(q, n0, [(ps[:, s, 0:T - c0], c0) for s, c0 in enumerate((0, META, 0))], 0)
                        pe.matmul(ps[:, SUM + 1, 0:2], ones[:, :], ones[:, 0:2], start=True, stop=True)\
                          .then_inc(part_done, 2)
                    else:
                        split_ready(n0, i)
                    for s, c0 in enumerate((0, META, 0)):
                        if i == 0:
                            break
                        hi, lo = x_parts(c0)
                        if i >= 2:
                            pe.wait_ge(v_scaled if s == 0 else part_copied, 2 * (i - 2) + s if s else i - 1)
                        mm = product(ps[:, b + s, 0:T - c0], r, s * KD, KD, hi, lo)
                        mm.then_inc(block_used if s == 2 else part_done, 1)
                    pe.wait_ge(v_scaled, i + 1)
                    if i >= 1:
                        pe.wait_ge(v_tok_ready, 2 * i)
                        pe.wait_ge(rope_step, 7 * i)
                    pe.transpose(ps[:, 7, 0:P], v_sb[r][:, META:META + P], ident)
                    pe.transpose(ps[:, 7, P:2 * P], v_sb[r][:, META + P:T], ident)
                    pe.transpose(ps[:, 7, 2 * P:3 * P], v_sb[r][:, 0:P], ident).then_inc(v_turned, 1)
                    pe.wait_ge(part_copied, 2 * i + 1)
                    pe.matmul(ps[:, b + 1, SEQ:2 * SEQ], rotate, q_sb[r][:, :], start=True, stop=True).then_inc(rotated, 1)
                    pe.wait_ge(part_copied, 2 * i + 2)
                    pe.matmul(ps[:, 6, 0:T], rotate, k_sb[r][:, :], start=True, stop=True).then_inc(rotated, 1)

            def softmax_heads():
                pe.wait_ge(lam_step, 1)
                pe.wait_ge(part_copied, 2 * HEADS)
                pe.matmul(ps[:, 0, 0:2], ones[:, :], small[:, 0:2], start=True, stop=True).then_inc(lam_sum, 1)
                pe.wait_ge(rope_step, 7 * HEADS)
                pe.wait_ge(v_tok_ready, 2 * HEADS)
                pe.wait_ge(lam_exp, 1)

                def scores(i):
                    if i >= 2:
                        pe.wait_ge(exp_ready, 4 * (i - 1))
                    for t in range(QT):
                        for c in range(2):
                            o = scores_at(i, t, c)
                            keys = o.shape[-1]
                            pe.matmul(o, q_rot[:, i, t * P:(t + 1) * P], k_rot[:, i, c, 0:keys], start=True, stop=False)
                            mm = pe.matmul(o[:, keys - P:keys], ident, mask, start=False, stop=True)
                    mm.then_inc(scores_done, 1)

                def turn_out(i):
                    pe.wait_ge(o_scaled, 2 * i + 2)
                    for t in range(QT):
                        mm = pe.transpose(ps[:, 6 + i % 2, SEQ + t * P:SEQ + (t + 1) * P], o_sb[i % 2][:, t, :], ident)
                    mm.then_inc(o_turned, 1)

                scores(0)
                scores(1)
                for i in range(HEADS):
                    if i + 2 < HEADS:
                        scores(i + 2)
                    pe.wait_ge(a_step, 4 * i + 3)
                    pe.transpose(ps[:, 4, 0:P], a_sb[:, 0, 0:P], ident)
                    pe.transpose(ps[:, 4, P:2 * P], a_sb[:, 0, META:META + P], ident).then_inc(a_turned, 1)
                    pe.wait_ge(a_step, 4 * i + 4)
                    pe.transpose(ps[:, 5, 0:P], a_sb[:, 1, 0:P], ident)
                    pe.transpose(ps[:, 5, P:2 * P], a_sb[:, 1, META:META + P], ident)
                    pe.transpose(ps[:, 5, 2 * P:3 * P], a_sb[:, 1, META + P:T], ident).then_inc(a_turned, 1)
                    if i >= 2:
                        pe.wait_ge(out_lo_ready, i - 1)
                    for t in range(QT):
                        pe.wait_ge(a_tok_ready, 4 * i + 2 * t + 2)
                        for n in range(t + 2):
                            mm = pe.matmul(ps[:, 6 + i % 2, t * P:(t + 1) * P], a_tok[:, 2 * t + n, :], v_tok[:, i, n, :],
                                           start=n == 0, stop=n == t + 1)
                    mm.then_inc(o_done, 1)
                    if i >= 1:
                        turn_out(i - 1)
                turn_out(HEADS - 1)

            def mixers(q):
                n0 = FIRST["mix_in"]
                hi, lo = x_parts(META)

                def part(i, s):
                    if s == 0:
                        split_ready(n0, i)
                    pe.wait_ge(proj_copied, 3 * (i - 2) + 3 if i == 4 else 3 * (i - 1) + s + 1)
                    product(ps[:, s, 0:SEQ], i % 2, s * KD, KD, hi, lo).then_inc(mix_part if s < 2 else block_used, 1)

                for i in range(4):
                    if i == 0:
                        first_block(q, n0, [(ps[:, s, 0:SEQ], META) for s in range(3)], META)
                        pe.wait_ge(mix_loaded, 6 * 16)
                        pe.wait_ge(mix_zeroed, 4)
                        pe.matmul(ps[0:HEADS, 7, :], rel_sb[:, :], onehot_sb[:, :], start=True, stop=True)\
                          .then_inc(dist_done, 1)
                        continue
                    split_ready(n0, i)
                    if i >= 2:
                        pe.wait_ge(proj_copied, 3 * (i - 1))
                    for s in range(3):
                        mm = product(ps[:, 3 * (i % 2) + s, 0:SEQ], i % 2, s * KD, KD, hi, lo)
                    mm.then_inc(block_used, 1)
                    if i == 1:
                        pe.wait_ge(low_ready, KD)
                        pe.wait_ge(proj_copied, 3)
                        for k in range(KD):
                            mm = pe.matmul(ps[0:16, 6, 0:SEQ], w_glow_sb[:, k, :], fx[:, k, META:T], start=k == 0, stop=k == KD - 1)
                        mm.then_inc(g_pe, 1)
                    if i == 2:
                        pe.wait_ge(glow_ready, 1)
                        pe.wait_ge(dist_ready, 1)
                        for t in range(QT):
                            mm = pe.matmul(ps[:, 7, t * SEQ:(t + 1) * SEQ], glow[:, t * P:(t + 1) * P], gate_w_sb[:, :],
                                           start=True, stop=True)
                        mm.then_inc(g_pe, 1)
                pe.wait_ge(g_dve, 2)
                for c in range(2):
                    for t in range(QT):
                        mm = pe.matmul(ps[:, 6, c * SEQ + t * P:c * SEQ + (t + 1) * P], g_ls[:, t, c * P:(c + 1) * P], upto,
                                       start=True, stop=True)
                mm.then_inc(g_pe, 1)
                for t in range(QT):
                    mm = pe.matmul(ps[:, 7, t * SEQ:(t + 1) * SEQ], after, g_ls[:, t, :], start=True, stop=True)
                mm.then_inc(g_pe, 1)
                pe.wait_ge(proj_copied, 12)
                for t in range(QT):
                    for c in range(4):
                        mm = pe.transpose(ps[:, 3 + t, c * P:(c + 1) * P], proj[:, GV + c, t * P:(t + 1) * P], ident)
                mm.then_inc(g_pe, 1)
                for t in range(QT):
                    for c in range(2):
                        mm = pe.transpose(ps[:, 5, t * SEQ + c * P:t * SEQ + (c + 1) * P], proj[:, GK + c, t * P:(t + 1) * P],
                                          ident)
                mm.then_inc(g_pe, 1)
                part(4, 0)
                part(4, 1)
                pe.wait_ge(g_act, 7)
                pe.wait_ge(g_dve, 7)
                for i in range(GLA_HEADS):
                    for t in range(QT):
                        n = 2 * i + t
                        mm = pe.matmul(ps[:, 3 + n // 4, (n % 4) * P:(n % 4 + 1) * P], g_k[:, i // 2, t * P:(t + 1) * P],
                                       g_q[:, i, t * P:(t + 1) * P], start=True, stop=True)
                    if i % 2:
                        mm.then_inc(g_pe, 1)
                part(4, 2)
                pe.wait_ge(g_dve, 11)
                for c in range(3):
                    for p in range(2):
                        mm = pe.matmul(ps[:, STATE_BANK[c], p * SEQ:(p + 1) * SEQ], g_ke[:, c // 2, c % 2, p * P:(p + 1) * P],
                                       gv_tok[:, c // 2, p * SEQ:(p + 1) * SEQ], start=True, stop=True)
                mm.then_inc(g_pe, 1)
                part(5, 0)
                part(5, 1)
                pe.wait_ge(g_pool, 4)
                pe.wait_ge(g_dve, 25)
                for i in range(GLA_HEADS):
                    for t in range(QT):
                        o = (i % 2) * SEQ + t * P
                        v = gv_tok[:, t, i * P:(i + 1) * P]
                        mm = pe.matmul(ps[:, 3 + i // 2, o:o + P], v, g_att[:, 2 * i + t, :], start=True, stop=False)
                        for c in range(2):
                            n = 2 * t + c
                            if n:
                                mm = pe.matmul(ps[:, 3 + i // 2, o + 64 * c:o + 64 * c + 64],
                                               g_s[:, n - 1, i // 2, (i % 2) * P:(i % 2 + 1) * P],
                                               g_q[:, i, 64 * n:64 * n + 64], start=False, stop=c == 1)
                mm.then_inc(g_pe, 1)
                part(5, 2)
                part(6, 0)
                pe.wait_ge(g_act, 9)
                flat = n_sq[:, :, :].rearrange("p a s -> p (a s)")
                for b in range(2):
                    mm = pe.matmul(ps[:, 6 + b, :], ones[:, :], flat[:, b * 512:(b + 1) * 512], start=True, stop=True)
                mm.then_inc(g_pe, 1)
                part(6, 1)
                part(6, 2)

                def scores(i):
                    pe.wait_ge(d_k_ready, i + 1)
                    if i >= 2:
                        pe.wait_ge(d_s_ready, 2 * (i - 1))
                    query = proj[:, DQ + 3 * (i // 2), :]
                    pe.matmul(ps[:, 5 + i % 2, 0:P], query[:, 0:P], d_k[i % 2][:, 0:P], start=True, stop=True)
                    pe.matmul(ps[:, 5 + i % 2, P:3 * P], query[:, P:2 * P], d_k[i % 2][:, :], start=True, stop=True)\
                      .then_inc(d_scores, 1)

                part(7, 0)
                part(7, 1)
                pe.wait_ge(g_dve, 33)
                scores(0)
                scores(1)
                for i in range(HEADS):
                    c = i // 2
                    if i == 0:
                        part(7, 2)
                    if i + 2 < HEADS:
                        scores(i + 2)
                    if i >= 1:
                        pe.wait_ge(d_o_copied, i)
                    if i % 2 == 0:
                        for t in range(QT):
                            mm = pe.transpose(ps[:, 3, SEQ + t * P:SEQ + (t + 1) * P], proj[:, DV + 3 * c, t * P:(t + 1) * P], ident)
                        mm.then_inc(dv_turned, 1)
                    pe.wait_ge(d_p_step, 3 * i + 3)
                    if i >= 1:
                        pe.wait_ge(d_pt_ready, i)
                    for n in range(3):
                        mm = pe.transpose(ps[:, 7, n * P:(n + 1) * P], d_p[:, n * P:(n + 1) * P], ident)
                    mm.then_inc(d_turned, 1)
                    pe.wait_ge(d_pt_ready, i + 1)
                    pe.wait_ge(dv_ready, c + 1)
                    v = slice(c * P, (c + 1) * P)
                    pe.matmul(ps[:, 3, 0:P], dv_tok[:, 0, v], d_pt[:, 0, :], start=True, stop=True)
                    pe.matmul(ps[:, 3, P:2 * P], dv_tok[:, 0, v], d_pt[:, 1, :], start=True, stop=False)
                    pe.matmul(ps[:, 3, P:2 * P], dv_tok[:, 1, v], d_pt[:, 2, :], start=False, stop=True).then_inc(d_o_done, 1)

            def wide_hidden(q):
                n0 = FIRST["ff1"]
                hi, lo = x_parts(META)

                first_block(q, n0, [(ps[:, s, 0:SEQ], META) for s in range(2)], META)

                def step(i, j):
                    split_ready(n0, i)
                    if not isinstance(i, int) or i >= 2:
                        pe.wait_ge(relu_ready, i * 2 - 2)
                    for s in range(2):
                        mm = product(ps[:, 2 * (j % 2) + s, 0:SEQ], j % 2, s * KD, KD, hi, lo)
                    mm.then_inc(block_used, 1)

                for i in (1, 2, 3):
                    step(i, i)
                loop(pe, FF1_N, step, first=4)

            def wide_down():
                n0 = FIRST["ff2"]
                half = KF2 // 2

                for i in range(FF2_N):
                    m, s = i // 2, i % 2
                    hi = lambda k: hid_hi[:, (s * half + k) * SEQ:(s * half + k + 1) * SEQ]
                    lo = lambda k: hid_lo[:, (s * half + k) * SEQ:(s * half + k + 1) * SEQ]
                    split_ready(n0, i)
                    if i == 0:
                        pe.wait_ge(hid_lo_ready, 4 * KF + FF1_N - 2)
                    if i == 1:
                        pe.wait_ge(hid_lo_ready, 4 * KF + FF1_N)
                    if s == 0:
                        pe.wait_ge(h_ready, 7 * KD + max(0, m - 3))
                    product(ps[:, m % 4, META:T], i % 2, 0, half, hi, lo, start=s == 0, stop=s == 1).then_inc(block_used, 1)

            pe.wait_ge(ones_ready, 1)
            for u, (kind, pre, post, f) in enumerate(SUB):
                c0 = first_col(u)
                if kind == "ffn":
                    hidden(f"gu{f}", f, u, c0)
                    down(f"dn{f}", f, u, c0)
                elif kind == "conv":
                    convolution(u)
                    out_projection("conv_out", u, lambda k: y_hi[:, k, :], lambda k: y_lo[:, k, :],
                                   (cv_lo_ready, 0), f_ready, KD * u, 0)
                else:
                    c0 = META
                    heads_in(u)
                    softmax_heads()
                    hi, lo = x_parts(META)
                    out_projection("attn_out", u, hi, lo, (out_lo_ready, 0), f_ready, KD * u, META)
                sum_squares(u, c0)
            mixers(6)
            hi, lo = x_parts(META)
            out_projection("mix_out", 6, hi, lo, (out_lo_ready, KD), h_ready, 6 * KD - F_CREDIT, META)
            wide_hidden(7)
            wide_down()
            pre_norm(8, META)


GD_DONE = 37


def blocks_of(w, pieces):
    rows = np.array([[r for r, _ in p] for p in pieces])
    cols = np.array([[c for _, c in p] for p in pieces])
    k, m = w.shape
    tiled = w.reshape(k // P, P, m // P, P).transpose(0, 2, 1, 3)
    picked = tiled[rows // P, cols // P]
    return np.ascontiguousarray(picked.transpose(0, 2, 1, 3).reshape(len(pieces), P, -1))


def columns(v):
    return v.reshape(-1, P).T


def kernel(**inputs):
    import concourse.bacc as bacc
    from concourse.bass_utils import run_bass_kernel_spmd

    a = {k: np.asarray(v) for k, v in inputs.items()}
    ks = range(KD)
    rows = lambda n: [k * P for k in range(n)]

    def swiglu_in(w):
        return blocks_of(w, [[(r, i * P) for r in rows(KD)] + [(r, D_FF + i * P) for r in rows(KD)] for i in range(KF)])

    def down(w):
        return blocks_of(w, [[(r, m * P) for r in rows(KF)] for m in ks])

    def triple(w, order):
        return blocks_of(w, [[(r, s * D + i * P) for s in order for r in rows(KD)] for i in ks])

    def pairs(w, n):
        return blocks_of(w, [[(r, (2 * b + s) * P) for s in range(2) for r in rows(KD)] for b in range(n)])

    w_in = a["w_in_2"][0]
    low = 2 * SEQ + 2 * 512
    w_mix = np.concatenate([w_in[:, :low], w_in[:, low + 16:]], axis=1)
    mix_chunks = [(3 * i, 3 * i + 1, 3 * i + 2) for i in range(4)] + [(12 + c, 16 + c, 20 + c) for c in range(4)]
    arrays = {
        "gu0": swiglu_in(a["ffn1_w_gu"][0]), "dn0": down(a["ffn1_w_down"][0]),
        "conv_in": triple(a["conv_w_in"][0], (0, 1, 2)), "conv_out": pairs(a["conv_w_out"][0], PROJ_N),
        "gu1": swiglu_in(a["ffn2_w_gu"][0]), "dn1": down(a["ffn2_w_down"][0]),
        "gu2": swiglu_in(a["ffn1_w_gu"][1]), "dn2": down(a["ffn1_w_down"][1]),
        "qkv": triple(a["attn_w_qkv"][0], (2, 0, 1)), "attn_out": pairs(a["attn_w_o"][0], PROJ_N),
        "gu3": swiglu_in(a["ffn2_w_gu"][1]), "dn3": down(a["ffn2_w_down"][1]),
        "mix_in": blocks_of(w_mix, [[(r, m * P) for m in chunks for r in rows(KD)] for chunks in mix_chunks]),
        "mix_out": pairs(a["w_out_2"][0], PROJ_N),
        "ff1": pairs(a["w_ff1_2"][0], FF1_N),
        "ff2": blocks_of(a["w_ff2_2"][0], [[((s * 16 + k) * P, m * P) for k in range(16)] for m in ks for s in range(2)]),
    }
    lam = np.zeros((P, 4), np.float32)
    lam[:64] = a["attn_lambda"][0].T
    par = [a["ln_ffn1"][0, 0], a["ln_ffn1"][0, 1], a["ln_mix"][0, 0], a["ln_mix"][0, 1], a["ln_ffn2"][0, 0],
           a["ln_ffn2"][0, 1], a["ln_ffn1"][1, 0], a["ln_ffn1"][1, 1], a["ln_mix"][1, 0], a["ln_mix"][1, 1],
           a["ln_ffn2"][1, 0], a["ln_ffn2"][1, 1], a["attn_norm_g_2"][0], a["mlp_norm_g_2"][0], a["final_norm_g_2"],
           a["conv_w"][0], a["attn_subln_g"][0], a["gla_norm_g_2"][0]]
    small = {}
    small["params"] = np.ascontiguousarray(np.concatenate([columns(v) for v in par] + [lam], axis=1))
    tokens = np.concatenate([a["meta_tokens"], a["x"][0]], axis=0)
    small["h_in"] = np.ascontiguousarray(tokens.T.reshape(KD, P, T).transpose(1, 0, 2))
    small["squares"], small["rope_mask"], small["onehot"], small["weight"] = shape_constants()
    small["w_glow"] = np.ascontiguousarray(w_in[:, low:low + 16].reshape(KD, P, 16).transpose(1, 0, 2))
    small["gate_w"] = np.concatenate([a["gla_gate_w2_2"][0], a["gla_gate_b_2"]], axis=0)
    small["rel_bias"] = np.ascontiguousarray(a["rel_bias_2"])

    nc = bacc.Bacc("TRN2", target_bir_lowering=False, num_devices=1)
    dram = lambda name, v: nc.dram_tensor(name, v.shape, F32, kind="ExternalInput").ap()
    w = {name: dram(f"w_{name}", v) for name, v in arrays.items()}
    s = {name: dram(name, v) for name, v in small.items()}
    out = nc.dram_tensor("out", (D, SEQ), F32, kind="ExternalOutput").ap()
    two_blocks(nc, w, out=out, **s)
    feed = {f"w_{name}": v for name, v in arrays.items()} | small
    r = run_bass_kernel_spmd(nc, [feed], core_ids=[0])
    return np.asarray(r.results[0]["out"]).T.reshape(1, SEQ, D)
```

```python
import math
from contextlib import ExitStack

import numpy as np
import concourse.bass as bass
from concourse import mybir

F32 = mybir.dt.float32
F32R = mybir.dt.float32r
ALU = mybir.AluOpType
ACT = mybir.ActivationFunctionType
AX = mybir.AxisListType

P = 128
D = 1024
KD = D // P
META = 16
SEQ = 256
T = META + SEQ
D_FF = 2816
KF = D_FF // P
D_FF2 = 4096
KF2 = D_FF2 // P
HEADS = 8
QT = SEQ // P
LAMBDA_INIT = 0.8 - 0.6 * math.exp(-0.3 * 1)
NORM_EPS, SUBLN_EPS = 1e-6, 1e-5
NEG = -1e30
ROT_HALF = 8
GLA_HEADS, GLA_CHUNK, GLA_TAU = 4, 64, 16.0
LN_EXP_SET = "natural_log_exp_and_others"

GU_T, DN_T, TRI_T, PROJ_T, FF_T = 2 * KD, KF, 3 * KD, 2 * KD, 2 * KD
RAW, SPLIT = 4, 2
SLOT = TRI_T * P
GU_N, DN_N, TRI_N, PROJ_N, FF1_N, FF2_N = KF, KD, KD, KD // 2, KF2 // 2, 2 * KD

STREAM = [
    ("gu0", GU_N, GU_T), ("dn0", DN_N, DN_T),
    ("conv_in", TRI_N, TRI_T), ("conv_out", PROJ_N, PROJ_T),
    ("gu1", GU_N, GU_T), ("dn1", DN_N, DN_T),
    ("gu2", GU_N, GU_T), ("dn2", DN_N, DN_T),
    ("qkv", TRI_N, TRI_T), ("attn_out", PROJ_N, PROJ_T),
    ("gu3", GU_N, GU_T), ("dn3", DN_N, DN_T),
    ("mix_in", TRI_N, TRI_T), ("mix_out", PROJ_N, PROJ_T),
    ("ff1", FF1_N, FF_T), ("ff2", FF2_N, FF_T),
]
FIRST = {}
WIDTH = []
for _name, _n, _t in STREAM:
    FIRST[_name] = len(WIDTH)
    WIDTH += [_t * P] * _n
BLOCKS = len(WIDTH)

COL = {}
_at = 0
for _name, _n in [("ffn1_pre0", 8), ("ffn1_post0", 8), ("mix_pre0", 8), ("mix_post0", 8), ("ffn2_pre0", 8),
                  ("ffn2_post0", 8), ("ffn1_pre1", 8), ("ffn1_post1", 8), ("mix_pre1", 8), ("mix_post1", 8),
                  ("ffn2_pre1", 8), ("ffn2_post1", 8), ("attn_norm", 8), ("mlp_norm", 8), ("final_norm", 8),
                  ("conv_w", 24), ("subln", 1), ("gla_norm", 4), ("lambda", 4)]:
    COL[_name] = _at
    _at += _n
PARAMS = _at


def shape_constants():
    ident = np.eye(P, dtype=np.float32)
    rotate = np.zeros((P, P), np.float32)
    for c in range(2):
        for i in range(ROT_HALF):
            a, b = 64 * c + i, 64 * c + ROT_HALF + i
            rotate[b, a] = -1.0
            rotate[a, b] = 1.0
    j, i = np.arange(P)[:, None], np.arange(P)[None, :]
    same = j // GLA_CHUNK == i // GLA_CHUNK
    upto = (same & (j <= i)).astype(np.float32) / np.float32(GLA_TAU)
    after = (same & (j > i)).astype(np.float32) / np.float32(GLA_TAU)
    squares = np.concatenate([ident, rotate, upto, after], axis=1)

    pos = np.arange(T, dtype=np.float32)
    inv_freq = (np.float32(500000.0) ** (-np.arange(0, 16, 2, dtype=np.float32) / np.float32(16))).astype(np.float32)
    ang = pos[None, :] * inv_freq[:, None]
    cos, sin = np.ones((P, T), np.float32), np.zeros((P, T), np.float32)
    for c in range(2):
        for h in range(2):
            rows = slice(64 * c + ROT_HALF * h, 64 * c + ROT_HALF * (h + 1))
            cos[rows], sin[rows] = np.cos(ang), np.sin(ang)
    q, k = np.arange(P)[:, None], np.arange(P)[None, :]
    mask = np.where(k <= q, 0.0, NEG).astype(np.float32)
    rope_mask = np.concatenate([cos, sin, mask, mask], axis=1)

    d = np.arange(512) - (SEQ - 1)
    n = np.maximum(d, 0)
    large = 16 + (np.log(np.maximum(n, 1) / 16) / math.log(2048 / 16) * 16).astype(np.int32)
    bucket = np.where(n < 16, n, np.minimum(large, 31)).astype(np.int32)
    count = np.zeros(512)
    for window, dilation in ((128, 1), (512, 4), (2048, 16)):
        count += (d >= 0) & (d % dilation == 0) & (d <= window)
    seen = (count > 0) & (d < SEQ)
    onehot = np.zeros((P, 512), np.float32)
    onehot[bucket[seen], np.arange(512)[seen]] = 1.0
    weight = np.where(seen, np.log(np.maximum(count, 1)), NEG).astype(np.float32)
    weight = np.broadcast_to(weight, (HEADS, 512)).copy()
    return squares, rope_mask, onehot, weight


def two_blocks(nc, w, params, h_in, squares, rope_mask, onehot, weight, w_glow, gate_w, rel_bias, out):
    with ExitStack() as ctx:
        def sb(name, shape, dt=F32, at=ctx):
            return at.enter_context(nc.sbuf_tensor(name, shape, dt))

        def sem(name):
            return ctx.enter_context(nc.semaphore(name))

        w_raw = [sb(f"w_raw{i}", [P, SLOT]) for i in range(RAW)]
        w_hi = [sb(f"w_hi{i}", [P, SLOT], F32R) for i in range(SPLIT)]
        w_lo = [sb(f"w_lo{i}", [P, SLOT], F32R) for i in range(SPLIT)]
        x_hi = sb("x_hi", [P, KD, T], F32R)
        x_lo = sb("x_lo", [P, KD, T], F32R)
        h = sb("h", [P, KD, T])
        fx = sb("fx", [P, KD, T])
        par = sb("par", [P, PARAMS])
        eps_col = sb("eps_col", [P, 1])[:, :]
        subln_eps_col = sb("subln_eps_col", [P, 1])[:, :]
        sq4 = sb("sq4", [P, 4 * P])
        ident, rotate, upto, after = (sq4[:, P * i:P * (i + 1)] for i in range(4))
        ones = sb("ones", [P, P])
        ms = sb("ms", [P, T])
        r0 = sb("r0", [P, T])
        rstd = sb("rstd", [P, T])
        rstd_sq = sb("rstd_sq", [P, T])
        small = sb("small", [P, 32])
        with ExitStack() as s:
            hid = [sb(f"hid{i}", [P, 2 * SEQ], at=s) for i in range(2)]
        with ExitStack() as s:
            gate = [sb(f"gate{i}", [P, T], at=s) for i in range(2)]
            up = [sb(f"up{i}", [P, T], at=s) for i in range(2)]
        with ExitStack() as s:
            d_k = [sb(f"d_k{i}", [P, SEQ], at=s) for i in range(2)]
            d_s = [sb(f"d_s{i}", [P, 3 * P], at=s) for i in range(2)]
        with ExitStack() as s:
            square = [sb(f"square{i}", [P, T], at=s) for i in range(2)]
            sumsq = sb("sumsq", [P, T], at=s)
            scaled = [sb(f"scaled{i}", [P, T], at=s) for i in range(2)]
        sb("shared_by_all", [P, 5 * T])
        with ExitStack() as s:
            hid_hi = sb("hid_hi", [P, KF2 * SEQ], F32R, at=s)
            hid_lo = sb("hid_lo", [P, KF2 * SEQ], F32R, at=s)
        with ExitStack() as s:
            y_hi = sb("y_hi", [P, KD, T], F32R, at=s)
            y_lo = sb("y_lo", [P, KD, T], F32R, at=s)
            cv_c = sb("cv_c", [P, T], at=s)
            cv_u = sb("cv_u", [P, T + 2], at=s)
            cv_a = sb("cv_a", [P, T], at=s)
            cv_b = sb("cv_b", [P, T], at=s)
            cv_y = sb("cv_y", [P, T], at=s)
        with ExitStack() as s:
            q_rot = [sb(f"q_rot{i}", [P, SEQ], at=s) for i in range(2)]
            k_rot = [sb(f"k_rot{i}", [P, 2, T], at=s) for i in range(2)]
            v_tok = sb("v_tok", [P, HEADS, 3, P], at=s)
            v_sb = [sb(f"v_sb{i}", [P, T], at=s) for i in range(2)]
            q_sb = [sb(f"q_sb{i}", [P, SEQ], at=s) for i in range(2)]
            k_sb = [sb(f"k_sb{i}", [P, T], at=s) for i in range(2)]
            tabs = sb("tabs", [P, 2 * T + 2 * P], at=s)
            cos_t, sin_t = tabs[:, 0:T], tabs[:, T:2 * T]
            mask = tabs[:, 2 * T:].rearrange("p (c k) -> p c k", c=2)
            rope_s = sb("rope_s", [P, T], at=s)
            rope_c = sb("rope_c", [P, T], at=s)
            s_exp = sb("s_exp", [P, 2, 2, 2, T], at=s)
            a_sb = sb("a_sb", [P, 2, T], at=s)
            a_tok = sb("a_tok", [P, 5, P], at=s)
            o_sq = sb("o_sq", [P, QT, P], at=s)
            o_sb = [sb(f"o_sb{i}", [P, QT, P], at=s) for i in range(2)]
            o_ss = [sb(f"o_ss{i}", [P, QT], at=s) for i in range(2)]
            o_ms = [sb(f"o_ms{i}", [P, QT], at=s) for i in range(2)]
            o_r0 = [sb(f"o_r0{i}", [P, QT], at=s) for i in range(2)]
            o_r = [sb(f"o_r{i}", [P, QT], at=s) for i in range(2)]
            z_hi = sb("z_hi", [P, HEADS, SEQ], F32R, at=s)
            z_lo = sb("z_lo", [P, HEADS, SEQ], F32R, at=s)
        with ExitStack() as s:
            proj = sb("proj", [P, 3 * TRI_N, SEQ], at=s)
            bias = sb("bias", [P, HEADS, SEQ], at=s)
            gv_tok = sb("gv_tok", [P, QT, 4 * P], at=s)
            dv_tok = sb("dv_tok", [P, QT, 4 * P], at=s)
            w_glow_sb = sb("w_glow_sb", [P, KD, 16], at=s)
            d_pt = sb("d_pt", [P, 3, P], at=s)
            with ExitStack() as s2:
                d_p = sb("d_p", [P, 3 * P], at=s2)
            gate_w_sb = sb("gate_w_sb", [P, SEQ], at=s)
            glow = sb("glow", [P, SEQ], at=s)
            with ExitStack() as s2:
                onehot_sb = sb("onehot_sb", [P, 512], at=s2)
                weight_sb = sb("weight_sb", [HEADS, 512], at=s2)
                by_dist = sb("by_dist", [HEADS, 512], at=s2)
                rel_sb = sb("rel_sb", [P, HEADS], at=s2)
            with ExitStack() as s2:
                g_a = sb("g_a", [P, QT, SEQ], at=s2)
                g_ls = sb("g_ls", [P, QT, SEQ], at=s2)
                g_eb = sb("g_eb", [P, QT, SEQ], at=s2)
                g_et = sb("g_et", [P, QT, SEQ], at=s2)
                g_q = sb("g_q", [P, GLA_HEADS, SEQ], at=s2)
                g_k = sb("g_k", [P, 2, SEQ], at=s2)
                g_s = sb("g_s", [P, 3, 2, SEQ], at=s2)
            with ExitStack() as s2:
                n_sq = sb("n_sq", [P, GLA_HEADS, SEQ], at=s2)
                n_r0 = sb("n_r0", [P, GLA_HEADS, SEQ], at=s2)
                n_r = sb("n_r", [P, GLA_HEADS, SEQ], at=s2)
                n_ms = sb("n_ms", [P, GLA_HEADS, SEQ], at=s2)
        GQ, GK, GV, GR = 0, 2, 4, 8
        DQ, DK, DV = 12, 13, 14
        g_ke = proj[:, GV:GV + 4, :].rearrange("p (t c) s -> p t c s", t=2)
        g_att = proj[:, GQ:GQ + 4, :].rearrange("p a s -> p (a s)").rearrange("p (n i) -> p n i", n=8)

        by_dist_dram = nc.dram_tensor("by_dist_dram", [HEADS, 512], F32, kind="Internal").ap()
        ps = ctx.enter_context(nc.psum_tensor("ps", [P, 8, 512], F32))
        SUM = 6

        landed = [sem(f"landed{i}") for i in range(RAW)]
        hi_ready, lo_ready, block_used = sem("hi_ready"), sem("lo_ready"), sem("block_used")
        h_loaded, par_loaded, consts_loaded = sem("h_loaded"), sem("par_loaded"), sem("consts_loaded")
        ones_ready, eps_ready = sem("ones_ready"), sem("eps_ready")
        h_sq_ready, h_sq_summed, sumsq_summed_act, sumsq_summed_dve = (
            sem("h_sq_ready"), sem("h_sq_summed"), sem("sumsq_summed_act"), sem("sumsq_summed_dve"))
        ms_ready, ln_ready, r0_ready, newton, rstd_ready = (
            sem("ms_ready"), sem("ln_ready"), sem("r0_ready"), sem("newton"), sem("rstd_ready"))
        x_hi_ready, x_lo_ready = sem("x_hi_ready"), sem("x_lo_ready")
        scaled_ready, h_ready = sem("scaled_ready"), sem("h_ready")
        gu_scaled, act_ready, relu_ready, hid_ready, hid_hi_ready, hid_lo_ready = (
            sem("gu_scaled"), sem("act_ready"), sem("relu_ready"), sem("hid_ready"), sem("hid_hi_ready"),
            sem("hid_lo_ready"))
        f_sq_ready, f_ready, sumsq_ready = sem("f_sq_ready"), sem("f_ready"), sem("sumsq_ready")
        cv_scaled, cv_u_ready, cv_a_ready, cv_step, cv_y_ready, cv_hi_ready, cv_lo_ready = (
            sem("cv_scaled"), sem("cv_u_ready"), sem("cv_a_ready"), sem("cv_step"), sem("cv_y_ready"),
            sem("cv_hi_ready"), sem("cv_lo_ready"))
        tabs_loaded, k_zeroed, part_done, part_copied = (
            sem("tabs_loaded"), sem("k_zeroed"), sem("part_done"), sem("part_copied"))
        tabs_scaled, v_scaled = sem("tabs_scaled"), sem("v_scaled")
        rotated, v_turned, v_tok_ready, rope_step = (
            sem("rotated"), sem("v_turned"), sem("v_tok_ready"), sem("rope_step"))
        lam_step, lam_exp = sem("lam_step"), sem("lam_exp")
        masked = sem("masked")
        scores_done, max_step, exp_ready, rs_step, a_step, a_turned, a_tok_ready, o_done = (
            sem("scores_done"), sem("max_step"), sem("exp_ready"), sem("rs_step"), sem("a_step"),
            sem("a_turned"), sem("a_tok_ready"), sem("o_done"))
        o_squared, sub_step, sub_ln, sub_r0_ready, o_scaled, o_turned, out_hi_ready, out_lo_ready = (
            sem("o_squared"), sem("sub_step"), sem("sub_ln"), sem("sub_r0_ready"), sem("o_scaled"),
            sem("o_turned"), sem("out_hi_ready"), sem("out_lo_ready"))
        low_ready, glow_ready = sem("low_ready"), sem("glow_ready")
        mix_part, dv_turned, dv_ready = sem("mix_part"), sem("dv_turned"), sem("dv_ready")
        mix_loaded, mix_zeroed, proj_copied = sem("mix_loaded"), sem("mix_zeroed"), sem("proj_copied")
        dist_done, dist_ready, dist_stored, bias_loaded = (
            sem("dist_done"), sem("dist_ready"), sem("dist_stored"), sem("bias_loaded"))
        g_pe, g_act, g_dve, g_pool = sem("g_pe"), sem("g_act"), sem("g_dve"), sem("g_pool")
        d_k_ready, d_scores, d_s_ready, d_max_step, d_exp, d_p_step, d_turned, d_pt_ready, d_o_done, d_o_copied = (
            sem("d_k_ready"), sem("d_scores"), sem("d_s_ready"), sem("d_max_step"), sem("d_exp"), sem("d_p_step"),
            sem("d_turned"), sem("d_pt_ready"), sem("d_o_done"), sem("d_o_copied"))
        out_ready, stored = sem("out_ready"), sem("stored")

        GU_CREDIT, F_CREDIT, CV_CREDIT = 4, 4, 2

        SUB = [("ffn", "ffn1_pre0", "ffn1_post0", 0), ("conv", "mix_pre0", "mix_post0", None),
               ("ffn", "ffn2_pre0", "ffn2_post0", 1), ("ffn", "ffn1_pre1", "ffn1_post1", 2),
               ("attn", "mix_pre1", "mix_post1", None), ("ffn", "ffn2_pre1", "ffn2_post1", 3)]

        ENTER = ["gu0", "conv_in", "gu1", "gu2", "qkv", "gu3", "mix_in", "ff1"]

        STATE_BANK = (6, 7, 5)
        OUT_AFTER = {4: (0, 1), 5: (2, 3), 6: (4, 5), 7: (6,)}
        MIX_OUTPUTS = {6: (0, 1), 7: (2, 3)}

        VALUE_BANK = {1: 3}
        FIRST_OUTPUTS = {HEADS: ((0, 1, 2), ()), HEADS + 1: ((3, 4), (5,)), HEADS + 2: ((6,), (7,))}

        def first_col(u):
            return 0 if u <= 4 else META

        def loop(eng, count, body, first=0, peel=0):
            rounds = (count - peel - first) // 4
            if rounds > 1:
                with eng.Fori(0, rounds) as it:
                    for j in range(4):
                        body(it * 4 + (first + j), (first + j) % 4)
            else:
                rounds = 0
            for i in range(first + rounds * 4, count):
                body(i, i % 4)

        def scores_at(t, c=None):
            keys = META + P * (t + 1)
            at = t * (META + P)
            return ps[:, 3:5, at:at + keys] if c is None else ps[:, 3 + c, at:at + keys]

        block = ctx.enter_context(nc.Block())

        @block.sync
        def _(sp):
            for name, count, tiles in STREAM:
                n0 = FIRST[name]

                def load(i, j):
                    slot = (n0 + j) % RAW
                    if not (isinstance(i, int) and n0 + i < RAW):
                        sp.wait_ge(lo_ready, i + (n0 - RAW + 1))
                    src = w[name][i, :, :] if isinstance(i, int) else w[name][bass.ds(i, 1), :, :].rearrange("a p c -> (a p) c")
                    sp.dma_start(w_raw[slot][:, 0:tiles * P], src).then_inc(landed[slot], 16)

                if n0 == 0:
                    load(0, 0)
                    sp.dma_start(par[:, :], params).then_inc(par_loaded, 16)
                    sp.dma_start(h[:, :, :], h_in).then_inc(h_loaded, 16)
                    for i in range(1, RAW):
                        load(i, i)
                    sp.dma_start(sq4[:, :], squares).then_inc(consts_loaded, 16)
                    loop(sp, count, load, first=RAW)
                else:
                    loop(sp, count, load)
            for k in range(KD):
                sp.wait_ge(out_ready, k + 1)
                sp.dma_start(out[k * P:(k + 1) * P, :], fx[:, k, META:T]).then_inc(stored, 16)
            sp.wait_ge(stored, 16 * KD)

        @block.gpsimd
        def _(pool):
            pool.memset(ones[:, :], 1.0).then_inc(ones_ready, 1)
            pool.wait_ge(block_used, FIRST["qkv"])
            pool.dma_start(tabs[:, :], rope_mask).then_inc(tabs_loaded, 16)
            pool.memset(k_rot[0][:, :, :], 0.0).then_inc(k_zeroed, 1)
            pool.memset(k_rot[1][:, :, :], 0.0).then_inc(k_zeroed, 1)
            pool.memset(v_tok[:, :, 0, :], 0.0).then_inc(k_zeroed, 1)
            pool.memset(a_tok[:, :, :], 0.0).then_inc(k_zeroed, 1)
            pool.wait_ge(block_used, FIRST["mix_in"])
            pool.memset(rel_sb[:, :], 0.0).then_inc(mix_zeroed, 1)
            pool.memset(gate_w_sb[:, :], 0.0).then_inc(mix_zeroed, 1)
            pool.memset(glow[:, :], 0.0).then_inc(mix_zeroed, 1)
            pool.wait_ge(mix_zeroed, 3)
            pool.memset(glow[32:33, :], 1.0).then_inc(mix_zeroed, 1)
            pool.dma_start(onehot_sb[:, :], onehot).then_inc(mix_loaded, 16)
            pool.dma_start(weight_sb[:, :], weight).then_inc(mix_loaded, 16)
            pool.dma_start(rel_sb[0:32, :], rel_bias).then_inc(mix_loaded, 16)
            pool.dma_start(w_glow_sb[:, :, :], w_glow).then_inc(mix_loaded, 16)
            pool.dma_start(gate_w_sb[0:16, :], gate_w[0:16, :]).then_inc(mix_loaded, 16)
            pool.dma_start(gate_w_sb[32:33, :], gate_w[16:17, :]).then_inc(mix_loaded, 16)
            pool.wait_ge(dist_ready, 1)
            pool.dma_start(by_dist_dram, by_dist[:, :]).then_inc(dist_stored, 16)
            pool.wait_ge(dist_stored, 16)
            toeplitz = bass.AP(tensor=by_dist_dram.tensor, offset=P, ap=[[1, P], [512, HEADS], [1, SEQ]])
            pool.dma_start(bias[:, :, :], toeplitz).then_inc(bias_loaded, 16)
            pool.memset(g_q[:, :, :], 0.0).then_inc(g_pool, 1)
            pool.wait_ge(g_act, 7)
            pool.memset(g_ke[:, :, :, :], 0.0).then_inc(g_pool, 1)
            pool.wait_ge(g_dve, 7)
            pool.wait_ge(g_pe, 6)
            pool.memset(g_att[:, :, :], 0.0).then_inc(g_pool, 1)
            pool.wait_ge(g_dve, 19)
            pool.affine_select(out=g_att, in_=g_att, compare_op=ALU.is_ge, fill=0.0, base=0,
                               pattern=[[0, 8], [1, P]], channel_multiplier=-1).then_inc(g_pool, 1)
            pool.memset(d_k[0][:, :], 0.0).then_inc(g_pool, 1)
            pool.memset(d_k[1][:, :], 0.0).then_inc(g_pool, 1)

        @block.scalar
        def _(act):
            def split_hi(n, j, width):
                act.wait_ge(landed[j], (n // 4 + 1) * 16 if isinstance(n, int) else n * 4 + (16 - 4 * j))
                if not (isinstance(n, int) and n < SPLIT):
                    act.wait_ge(block_used, n - (SPLIT - 1))
                act.activation(w_hi[j % SPLIT][:, 0:width], w_raw[j][:, 0:width], ACT.Copy).then_inc(hi_ready, 1)

            def next_hi(name, count, i, j):
                n0 = FIRST[name]
                if isinstance(i, int):
                    if n0 + i + 2 < BLOCKS:
                        split_hi(n0 + i + 2, (n0 + i + 2) % 4, WIDTH[n0 + i + 2])
                else:
                    split_hi(i + (n0 + 2), (n0 + j + 2) % 4, WIDTH[n0])

            def second_hi(q):
                n = FIRST[ENTER[q]] + 1
                split_hi(n, n % 4, WIDTH[n])

            def root(s, c0, from_psum=False):
                if from_psum:
                    act.wait_ge(sumsq_summed_act, s // 2 + 1)
                    act.activation(r0[:, c0:T], ps[:, SUM + 1, c0:T], ACT.Ln, scale=1.0 / D, bias=eps_col)\
                       .then_inc(ln_ready, 1)
                else:
                    act.wait_ge(ms_ready, s + 1)
                    act.activation(r0[:, c0:T], ms[:, c0:T], ACT.Ln).then_inc(ln_ready, 1)
                act.wait_ge(ln_ready, s + 1)
                act.activation(r0[:, c0:T], r0[:, c0:T], ACT.Exp, scale=-0.5).then_inc(r0_ready, 1)

            def h_square(q, k, c0):
                if q > 0:
                    act.wait_ge(h_ready, KD * (q - 1) + k + 1)
                if KD * q + k >= 2:
                    act.wait_ge(h_sq_summed, KD * q + k - 1)
                act.activation(square[k % 2][:, c0:T], h[:, k, c0:T], ACT.Square).then_inc(h_sq_ready, 1)

            def pre_norm(q, s, c0, gain):
                for k in range(KD):
                    if q == 0:
                        act.wait_ge(h_loaded, 16)
                    else:
                        act.wait_ge(h_ready, KD * (q - 1) + k + 1)
                    if q == 7 and k == 0:
                        act.wait_ge(block_used, FIRST["ff1"])
                    g = COL[gain] + k
                    act.activation(x_hi[:, k, c0:T], h[:, k, c0:T], ACT.Copy, scale=par[:, g:g + 1])\
                       .then_inc(x_hi_ready, 1)
                    h_square(q, k, c0)
                if q == 0:
                    second_hi(0)
                root(s, c0)

            def take_out(u, m, j, c0, gain):
                if u > 0 or m > 0:
                    act.wait_ge(sumsq_ready, KD * u + m)
                act.activation(square[j % 2][:, c0:T], ps[:, j, c0:T], ACT.Square).then_inc(f_sq_ready, 1)
                g = par[:, bass.ds(m + COL[gain], 1)]
                act.activation(fx[:, m if isinstance(m, int) else bass.ds(m, 1), c0:T], ps[:, j, c0:T],
                               ACT.Copy, scale=g).then_inc(f_ready, 1)

            def hidden(name, f, c0):
                n0, width = FIRST[name], T - c0

                def silu(i, j):
                    act.wait_ge(gu_scaled, i * 2 + (2 * KF * f + 1 + GU_CREDIT))
                    act.activation(gate[j % 2][:, 0:width], gate[j % 2][:, 0:width], ACT.Silu).then_inc(act_ready, 1)

                def hidden_hi(i, j):
                    act.wait_ge(hid_ready, i + (KF * f + 1))
                    act.activation(hid_hi[:, bass.ds(i * T + c0, width)], up[j % 2][:, 0:width], ACT.Copy)\
                       .then_inc(hid_hi_ready, 1)

                def step(i, j):
                    next_hi(name, GU_N, i, j)
                    silu(i, j)
                    hidden_hi(i - 1, (j + 3) % 4)

                next_hi(name, GU_N, 0, 0)
                silu(0, 0)
                loop(act, GU_N, step, first=1, peel=2)
                hidden_hi(GU_N - 1, (GU_N - 1) % 4)

            def out_projection(name, count, per, u, c0, gain):
                n0 = FIRST[name]

                def step(i, j):
                    act.wait_ge(block_used, i + (n0 + 1))
                    for s in range(per):
                        take_out(u, i * per + s, (j * per + s) % 4, c0, gain)
                    next_hi(name, count, i, j)

                loop(act, count - 1, step, peel=1)
                act.wait_ge(block_used, n0 + count)
                for s in range(per):
                    m = (count - 1) * per + s
                    take_out(u, m, m % 4, c0, gain)

            def convolution():
                n0 = FIRST["conv_in"]

                def step(i, j, last=False):
                    if not last:
                        next_hi("conv_in", TRI_N, i, j)
                    act.wait_ge(cv_u_ready, i + (1 + CV_CREDIT))
                    act.activation(cv_a[:, :], cv_u[:, 0:T], ACT.Copy,
                                   scale=par[:, bass.ds(i + COL["conv_w"], 1)]).then_inc(cv_a_ready, 1)
                    act.wait_ge(cv_y_ready, i + 1)
                    act.activation(y_hi[:, i, :], cv_y[:, :], ACT.Copy).then_inc(cv_hi_ready, 1)
                    if last:
                        next_hi("conv_in", TRI_N, i, j)

                loop(act, TRI_N - 1, step, peel=1)
                step(TRI_N - 1, (TRI_N - 1) % 4, last=True)

            def heads():
                n0 = FIRST["qkv"]

                def query(i):
                    act.wait_ge(part_done, 2 * i + 2)
                    if i >= 2:
                        act.wait_ge(rope_step, 7 * (i - 1))
                    act.activation(q_sb[i % 2][:, :], ps[:, 1, 0:SEQ], ACT.Copy, scale=0.125).then_inc(part_copied, 1)

                def key(i):
                    act.wait_ge(block_used, n0 + i + 1)
                    act.activation(k_sb[i % 2][:, :], ps[:, 2, 0:T], ACT.Copy).then_inc(part_copied, 1)

                def value(i):
                    act.wait_ge(v_turned, i + 1)
                    if i == 0:
                        act.wait_ge(k_zeroed, 4)
                    act.activation(v_tok[:, i, 1:3, :], ps[:, 5, 0:2 * P].rearrange("p (c v) -> p c v", c=2),
                                   ACT.Copy).then_inc(v_tok_ready, 1)
                    act.activation(v_tok[0:META, i, 0, :], ps[0:META, 5, 2 * P:3 * P], ACT.Copy).then_inc(v_tok_ready, 1)

                def exponentials(i):
                    if i >= 2:
                        act.wait_ge(a_step, 4 * (i - 1))
                    for t in range(QT):
                        keys = META + P * (t + 1)
                        act.wait_ge(max_step, 3 * i + 3)
                        for c in range(2):
                            n = 4 * (i % 2) + 2 * t + c
                            act.activation(s_exp[:, i % 2, t, c, 0:keys], scores_at(t, c), ACT.Exp,
                                           bias=small[:, 8 + n:9 + n], accum_out=small[:, 16 + n:17 + n])\
                               .then_inc(exp_ready, 1)

                def turned(i):
                    act.wait_ge(a_turned, 2 * i + 1)
                    if i >= 1:
                        act.wait_ge(o_done, i)
                    act.activation(a_tok[0:META, 0, :], ps[0:META, 5, 0:P], ACT.Copy).then_inc(a_tok_ready, 1)
                    act.activation(a_tok[:, 1, :], ps[:, 5, P:2 * P], ACT.Copy).then_inc(a_tok_ready, 1)
                    act.wait_ge(a_turned, 2 * i + 2)
                    act.activation(a_tok[0:META, 2, :], ps[0:META, 6, 0:P], ACT.Copy).then_inc(a_tok_ready, 1)
                    act.activation(a_tok[:, 3:5, :], ps[:, 6, P:3 * P].rearrange("p (c q) -> p c q", c=2),
                                   ACT.Copy).then_inc(a_tok_ready, 1)

                def out_root(i):
                    r = i % 2
                    if i >= 2:
                        act.wait_ge(o_scaled, 2 * (i - 1))
                    if i >= 1:
                        act.wait_ge(o_squared, 2 * i)
                    act.wait_ge(o_done, i + 1)
                    for t in range(QT):
                        act.activation(o_sq[:, t, :], ps[:, 7, t * P:(t + 1) * P], ACT.Square,
                                       accum_out=o_ss[r][:, t:t + 1]).then_inc(o_squared, 1)
                    act.wait_ge(o_squared, 2 * i + 2)
                    act.activation(o_r0[r][:, :], o_ss[r][:, :], ACT.Ln, scale=1.0 / P, bias=subln_eps_col).then_inc(sub_ln, 1)
                    act.wait_ge(sub_ln, i + 1)
                    act.activation(o_r0[r][:, :], o_r0[r][:, :], ACT.Exp, scale=-0.5).then_inc(sub_r0_ready, 1)

                def out_hi(i):
                    act.wait_ge(o_turned, i + 1)
                    act.activation(z_hi[:, i, :], ps[:, 7, SEQ:2 * SEQ], ACT.Copy, scale=small[:, 5:6]).then_inc(out_hi_ready, 1)

                for i in range(HEADS + 3):
                    if i == 0:
                        act.wait_ge(part_done, 2)
                        act.activation(small[:, 2:4], ps[:, 7, 0:2], ACT.Exp).then_inc(lam_exp, 1)
                    if 0 <= i - 1 < HEADS:
                        key(i - 1)
                    if 0 <= i - 3 < HEADS:
                        out_root(i - 3)
                    if 0 <= i - 1 < HEADS:
                        next_hi("qkv", TRI_N, i - 1, (i - 1) % 4)
                        value(i - 1)
                    if i < HEADS:
                        query(i)
                    if 0 <= i - 3 < HEADS:
                        out_hi(i - 3)
                    if 0 <= i - 2 < HEADS:
                        turned(i - 2)
                    if 0 <= i - 1 < HEADS:
                        exponentials(i - 1)

            def mixers():
                for k in range(KD):
                    g = COL["attn_norm"] + k
                    act.activation(fx[:, k, META:T], h[:, k, META:T], ACT.Copy, scale=par[:, g:g + 1]).then_inc(low_ready, 1)
                for i in range(3):
                    next_hi("mix_in", TRI_N, i, i)
                act.wait_ge(g_pe, 2)
                act.wait_ge(dist_stored, 16)
                act.activation(g_a[:, :, :], ps[:, 7, :].rearrange("p (t f) -> p t f", t=2), ACT.Abs).then_inc(g_act, 1)
                act.wait_ge(g_act, 1)
                act.activation(g_a[:, :, :], g_a[:, :, :], ACT.Exp, scale=-1.0).then_inc(g_act, 1)
                act.wait_ge(g_act, 2)
                act.activation(g_a[:, :, :], g_a[:, :, :], ACT.Ln, bias=1.0).then_inc(g_act, 1)
                next_hi("mix_in", TRI_N, 3, 3)
                act.wait_ge(g_pe, 4)
                b_t = ps[:, 6, :].rearrange("p (c s) -> p c s", c=2)
                act.activation(g_eb[:, :, :], b_t, ACT.Exp).then_inc(g_act, 1)
                act.activation(g_a[:, :, :], b_t, ACT.Exp, scale=-1.0).then_inc(g_act, 1)
                act.activation(g_et[:, :, :], ps[:, 7, :].rearrange("p (t f) -> p t f", t=2), ACT.Exp).then_inc(g_act, 1)
                act.wait_ge(g_pe, 5)
                act.activation(gv_tok[:, :, :], ps[:, 3:5, :], ACT.Copy).then_inc(g_act, 1)
                act.preload_act_table(ACT.Silu)
                act.wait_ge(proj_copied, GR + 4)
                act.activation(proj[:, GR:GR + 4, :], proj[:, GR:GR + 4, :], ACT.Silu).then_inc(g_act, 1)
                act.preload_act_table_set(LN_EXP_SET)
                next_hi("mix_in", TRI_N, 4, 0)
                act.wait_ge(g_pe, 10)
                act.wait_ge(g_dve, 25)
                act.activation(n_sq[:, :, :].rearrange("p a s -> p (a s)").rearrange("p (b s) -> p b s", b=2),
                               ps[:, 3:5, :], ACT.Square).then_inc(g_act, 1)
                next_hi("mix_in", TRI_N, 5, 1)
                act.wait_ge(g_dve, 26)
                act.activation(n_r0[:, :, :], n_ms[:, :, :], ACT.Ln).then_inc(g_act, 1)
                act.wait_ge(g_act, 10)
                act.activation(n_r0[:, :, :], n_r0[:, :, :], ACT.Exp, scale=-0.5).then_inc(g_act, 1)

                def exponentials(i):
                    if i >= 2:
                        act.wait_ge(d_p_step, 3 * (i - 1))
                    act.wait_ge(d_max_step, 3 * i + 3)
                    for t in range(QT):
                        a, b = (0, P) if t == 0 else (P, 3 * P)
                        n = 2 * (i % 2) + t
                        act.activation(d_s[i % 2][:, a:b], d_s[i % 2][:, a:b], ACT.Exp, bias=small[:, 8 + n:9 + n],
                                       accum_out=small[:, 16 + n:17 + n]).then_inc(d_exp, 1)

                def out_copy(i):
                    act.wait_ge(d_o_done, i + 1)
                    half = slice(64 * (i % 2), 64 * (i % 2) + 64)
                    act.activation(fx[half, 4 + i // 2, META:T], ps[half, 3, 0:SEQ], ACT.Copy).then_inc(d_o_copied, 1)

                def out_hi(k):
                    if k < 4:
                        act.wait_ge(g_dve, GD_DONE - 3 + k)
                    else:
                        act.wait_ge(d_o_copied, 2 * (k - 3))
                    act.activation(x_hi[:, k, META:T], fx[:, k, META:T], ACT.Copy).then_inc(out_hi_ready, 1)

                exponentials(0)
                for i in range(HEADS):
                    if i + 1 < HEADS:
                        exponentials(i + 1)
                    if i >= 1:
                        out_copy(i - 1)
                    if i % 2 == 0:
                        c = i // 2
                        act.wait_ge(dv_turned, c + 1)
                        act.activation(dv_tok[:, :, c * P:(c + 1) * P],
                                       ps[:, 3, SEQ:2 * SEQ].rearrange("p (t v) -> p t v", t=2), ACT.Copy).then_inc(dv_ready, 1)
                    act.wait_ge(d_turned, i + 1)
                    if i >= 1:
                        act.wait_ge(d_o_done, i)
                    act.activation(d_pt[:, :, :], ps[:, 7, 0:3 * P].rearrange("p (c q) -> p c q", c=3), ACT.Copy)\
                       .then_inc(d_pt_ready, 1)
                    if i == 0:
                        next_hi("mix_in", TRI_N, 6, 2)
                    if i == 2:
                        next_hi("mix_in", TRI_N, 7, 3)
                    for k in OUT_AFTER.get(i, ()):
                        out_hi(k)
                out_copy(HEADS - 1)
                out_hi(KD - 1)

            def wide_hidden():
                def step(i, j):
                    next_hi("ff1", FF1_N, i, j)
                    act.wait_ge(hid_ready, i + (4 * KF + 1))
                    act.activation(hid_hi[:, bass.ds(i * 2 * SEQ, 2 * SEQ)], hid[j % 2][:, :], ACT.Copy)\
                       .then_inc(hid_hi_ready, 1)

                loop(act, FF1_N, step, peel=2)

            act.preload_act_table_set(LN_EXP_SET)
            split_hi(0, 0, WIDTH[0])
            act.wait_ge(eps_ready, 2)
            act.wait_ge(par_loaded, 16)
            s = 0
            for u, (kind, pre, post, f) in enumerate(SUB):
                c0 = first_col(u)
                pre_norm(u, s, c0, pre)
                s += 1
                if kind == "ffn":
                    act.preload_act_table(ACT.Silu)
                    hidden(f"gu{f}", f, c0)
                    act.preload_act_table_set(LN_EXP_SET)
                    out_projection(f"dn{f}", DN_N, 1, u, c0, post)
                elif kind == "conv":
                    convolution()
                    out_projection("conv_out", PROJ_N, 2, u, c0, post)
                else:
                    c0 = META
                    heads()
                    out_projection("attn_out", PROJ_N, 2, u, c0, post)
                root(s, c0, from_psum=True)
                s += 1
                second_hi(u + 1)
            pre_norm(6, s, META, "attn_norm")
            s += 1
            mixers()
            for i in range(PROJ_N - 1):
                next_hi("mix_out", PROJ_N, i, i % 4)
            second_hi(7)
            pre_norm(7, s, META, "mlp_norm")
            s += 1
            wide_hidden()
            for m in range(KD):
                for i in (2 * m, 2 * m + 1):
                    next_hi("ff2", FF2_N, i, i % 4)
                h_square(8, m, META)
            root(s, META)

        @block.vector
        def _(dve):
            def split_lo(n, j, width):
                dve.wait_ge(hi_ready, n + 1)
                dve.tensor_tensor(w_lo[j % SPLIT][:, 0:width], w_raw[j][:, 0:width],
                                  w_hi[j % SPLIT][:, 0:width].bitcast(F32), ALU.subtract).then_inc(lo_ready, 1)

            def next_lo(name, count, i, j):
                n0 = FIRST[name]
                if isinstance(i, int):
                    if n0 + i + 2 < BLOCKS:
                        split_lo(n0 + i + 2, (n0 + i + 2) % 4, WIDTH[n0 + i + 2])
                else:
                    split_lo(i + (n0 + 2), (n0 + j + 2) % 4, WIDTH[n0])

            def root(s, c0, summed, count, eps):
                dve.wait_ge(summed, count)
                dve.tensor_scalar(ms[:, c0:T], ps[:, SUM, c0:T], 1.0 / D, eps, ALU.mult, ALU.add).then_inc(ms_ready, 1)
                dve.wait_ge(r0_ready, s + 1)
                dve.tensor_tensor(rstd[:, c0:T], r0[:, c0:T], r0[:, c0:T], ALU.mult).then_inc(newton, 1)
                dve.wait_ge(newton, 2 * s + 1)
                dve.scalar_tensor_tensor(out=rstd[:, c0:T], in0=rstd[:, c0:T], scalar=-0.5, in1=ms[:, c0:T],
                                         op0=ALU.mult, op1=ALU.mult).then_inc(newton, 1)
                dve.wait_ge(newton, 2 * s + 2)
                dve.scalar_tensor_tensor(out=rstd[:, c0:T], in0=rstd[:, c0:T], scalar=1.5, in1=r0[:, c0:T],
                                         op0=ALU.add, op1=ALU.mult).then_inc(rstd_ready, 1)
                dve.wait_ge(rstd_ready, s + 1)

            def lo_part(q, k, c0, gain):
                g = COL[gain] + k
                dve.wait_ge(x_hi_ready, KD * q + k + 1)
                dve.scalar_tensor_tensor(out=x_lo[:, k, c0:T], in0=h[:, k, c0:T], scalar=par[:, g:g + 1],
                                         in1=x_hi[:, k, c0:T].bitcast(F32), op0=ALU.mult, op1=ALU.subtract)\
                   .then_inc(x_lo_ready, 1)

            def pre_root(q, s, c0):
                root(s, c0, h_sq_summed, KD * (q + 1), NORM_EPS)

            def post_norm(u, s, c0, factor, gain):
                root(s, c0, sumsq_summed_dve, u + 1, NORM_EPS)
                for k in range(KD + 2):
                    if k < KD:
                        if k >= 2:
                            dve.wait_ge(h_ready, KD * u + k - 1)
                        dve.tensor_tensor(scaled[k % 2][:, c0:T], fx[:, k, c0:T], rstd[:, c0:T], ALU.mult)\
                           .then_inc(scaled_ready, 1)
                    if 1 <= k <= KD:
                        dve.wait_ge(scaled_ready, KD * u + k)
                        dve.scalar_tensor_tensor(out=h[:, k - 1, c0:T], in0=scaled[(k - 1) % 2][:, c0:T], scalar=factor,
                                                 in1=h[:, k - 1, c0:T], op0=ALU.mult, op1=ALU.add).then_inc(h_ready, 1)
                    if k >= 2:
                        lo_part(u + 1, k - 2, c0, gain)

            def hidden(name, f, c0):
                width = T - c0

                def take(i, j):
                    dve.wait_ge(block_used, i + (FIRST[name] + 1))
                    if not isinstance(i, int) or i >= 2:
                        dve.wait_ge(hid_lo_ready, i + (KF * f - 1))
                    dve.tensor_tensor(gate[j % 2][:, 0:width], rstd[:, c0:T], ps[:, 2 * (j % 2), c0:T], ALU.mult)\
                       .then_inc(gu_scaled, 1)
                    dve.tensor_tensor(up[j % 2][:, 0:width], rstd[:, c0:T], ps[:, 2 * (j % 2) + 1, c0:T], ALU.mult)\
                       .then_inc(gu_scaled, 1)

                def times_gate(i, j):
                    t = up[j % 2][:, 0:width]
                    dve.wait_ge(act_ready, i + (KF * f + 1))
                    dve.wait_ge(gu_scaled, i * 2 + (2 * KF * f + 2 + GU_CREDIT))
                    dve.tensor_tensor(t, t, gate[j % 2][:, 0:width], ALU.mult).then_inc(hid_ready, 1)

                def hidden_lo(i, j):
                    at = i * T + c0
                    dve.wait_ge(hid_hi_ready, i + (KF * f + 1))
                    dve.tensor_tensor(hid_lo[:, bass.ds(at, width)], up[j % 2][:, 0:width],
                                      hid_hi[:, bass.ds(at, width)].bitcast(F32), ALU.subtract).then_inc(hid_lo_ready, 1)

                def step(i, j):
                    take(i, j)
                    times_gate(i - 1, (j + 3) % 4)
                    next_lo(name, GU_N, i, j)
                    hidden_lo(i - 1, (j + 3) % 4)

                take(0, 0)
                next_lo(name, GU_N, 0, 0)
                step(1, 1)
                loop(dve, GU_N, step, first=2, peel=2)
                times_gate(GU_N - 1, (GU_N - 1) % 4)
                hidden_lo(GU_N - 1, (GU_N - 1) % 4)

            def add_square(u, m, par_, c0):
                dve.wait_ge(f_sq_ready, m + (KD * u + 1))
                dve.wait_ge(sumsq_ready, m + (KD * u + 1))
                dve.tensor_tensor(sumsq[:, c0:T], sumsq[:, c0:T], square[par_][:, c0:T], ALU.add).then_inc(sumsq_ready, 1)

            def out_projection(name, count, per, u, c0):
                if u > 0:
                    dve.wait_ge(h_ready, KD * u)
                dve.wait_ge(hid_lo_ready, 1)
                dve.memset(sumsq[:, :], 0.0).then_inc(sumsq_ready, 1)

                def step(i, j):
                    for s in range(per):
                        add_square(u, i * per + s, (j * per + s) % 2, c0)
                    next_lo(name, count, i, j)

                loop(dve, count - 1, step, peel=1)
                for m in range((count - 1) * per, KD - 1):
                    add_square(u, m, m % 2, c0)

            def convolution():
                dve.tensor_tensor(rstd_sq[:, :], rstd[:, :], rstd[:, :], ALU.mult).then_inc(cv_step, 1)
                dve.memset(cv_u[:, 0:2], 0.0).then_inc(cv_u_ready, CV_CREDIT)
                dve.wait_ge(cv_step, 1)

                def step(i, j, last=False):
                    b = 3 * (j % 2)
                    w1 = par[:, bass.ds(i + (COL["conv_w"] + KD), 1)]
                    w2 = par[:, bass.ds(i + (COL["conv_w"] + 2 * KD), 1)]
                    dve.wait_ge(block_used, i + (FIRST["conv_in"] + 1))
                    dve.tensor_tensor(cv_c[:, :], rstd_sq[:, :], ps[:, b + 1, 0:T], ALU.mult).then_inc(cv_scaled, 1)
                    dve.tensor_tensor(cv_b[:, :], rstd[:, :], ps[:, b, 0:T], ALU.mult).then_inc(cv_scaled, 1)
                    dve.wait_ge(cv_scaled, i * 2 + 1)
                    dve.tensor_tensor(cv_u[:, 2:T + 2], cv_c[:, :], ps[:, b + 2, 0:T], ALU.mult).then_inc(cv_u_ready, 1)
                    if not last:
                        next_lo("conv_in", TRI_N, i, j)
                    dve.wait_ge(cv_a_ready, i + 1)
                    dve.scalar_tensor_tensor(out=cv_a[:, :], in0=cv_u[:, 1:T + 1], scalar=w1, in1=cv_a[:, :],
                                             op0=ALU.mult, op1=ALU.add).then_inc(cv_step, 1)
                    dve.wait_ge(cv_step, i * 2 + 2)
                    dve.scalar_tensor_tensor(out=cv_a[:, :], in0=cv_u[:, 2:T + 2], scalar=w2, in1=cv_a[:, :],
                                             op0=ALU.mult, op1=ALU.add).then_inc(cv_step, 1)
                    dve.wait_ge(cv_step, i * 2 + 3)
                    dve.tensor_tensor(cv_y[:, :], cv_a[:, :], cv_b[:, :], ALU.mult).then_inc(cv_y_ready, 1)
                    dve.wait_ge(cv_hi_ready, i + 1)
                    dve.tensor_tensor(y_lo[:, i, :], cv_y[:, :], y_hi[:, i, :].bitcast(F32), ALU.subtract)\
                       .then_inc(cv_lo_ready, 1)
                    if last:
                        next_lo("conv_in", TRI_N, i, j)

                loop(dve, TRI_N - 1, step, peel=1)
                step(TRI_N - 1, (TRI_N - 1) % 4, last=True)

            def lam():
                c = COL["lambda"]
                dve.tensor_tensor(small[:, 0:2], par[:, c:c + 4:2], par[:, c + 1:c + 4:2], ALU.mult).then_inc(lam_step, 1)

            def heads():
                dve.wait_ge(tabs_loaded, 16)
                dve.wait_ge(k_zeroed, 4)
                dve.tensor_tensor(cos_t, cos_t, rstd[:, :], ALU.mult).then_inc(tabs_scaled, 1)
                dve.tensor_tensor(sin_t, sin_t, rstd[:, :], ALU.mult).then_inc(tabs_scaled, 1)
                dve.wait_ge(lam_exp, 1)
                dve.scalar_tensor_tensor(out=small[:, 4:5], in0=small[:, 3:4], scalar=-LAMBDA_INIT, in1=small[:, 2:3],
                                         op0=ALU.add, op1=ALU.subtract).then_inc(lam_step, 1)
                c = COL["subln"]
                dve.tensor_scalar(small[:, 5:6], par[:, c:c + 1], 1.0 - LAMBDA_INIT, None, ALU.mult).then_inc(lam_step, 1)
                dve.wait_ge(tabs_scaled, 2)

                def value(i):
                    dve.wait_ge(part_done, 2 * i + 1)
                    if i >= 2:
                        dve.wait_ge(v_turned, i - 1)
                    dve.tensor_tensor(v_sb[i % 2][:, :], rstd[:, :], ps[:, VALUE_BANK.get(i, 0), 0:T], ALU.mult)\
                       .then_inc(v_scaled, 1)

                def rotary(i):
                    r, n = i % 2, 7 * i
                    dve.wait_ge(rotated, 2 * i + 1)
                    if i >= 1:
                        dve.wait_ge(rope_step, n)
                    dve.tensor_tensor(rope_s[:, 0:SEQ], sin_t[:, META:T], ps[:, 3, 0:SEQ], ALU.mult).then_inc(rope_step, 1)
                    dve.tensor_tensor(rope_c[:, 0:SEQ], q_sb[r][:, :], cos_t[:, META:T], ALU.mult).then_inc(rope_step, 1)
                    dve.wait_ge(rope_step, n + 2)
                    dve.tensor_tensor(q_rot[r][:, :], rope_s[:, 0:SEQ], rope_c[:, 0:SEQ], ALU.add).then_inc(rope_step, 1)
                    dve.wait_ge(rotated, 2 * i + 2)
                    dve.wait_ge(rope_step, n + 3)
                    dve.tensor_tensor(rope_s[:, :], sin_t, ps[:, 4, 0:T], ALU.mult).then_inc(rope_step, 1)
                    dve.tensor_tensor(rope_c[:, :], k_sb[r][:, :], cos_t, ALU.mult).then_inc(rope_step, 1)
                    dve.wait_ge(rope_step, n + 5)
                    for c in range(2):
                        rows = slice(64 * c, 64 * c + 64)
                        dve.tensor_tensor(k_rot[r][rows, c, :], rope_s[rows, :], rope_c[rows, :], ALU.add)\
                           .then_inc(rope_step, 1)

                def maxima(i):
                    o = 4 * (i % 2)
                    dve.wait_ge(scores_done, i + 1)
                    for t in range(QT):
                        diagonal = scores_at(t)[:, :, META + P * t:META + P * (t + 1)]
                        dve.tensor_tensor(diagonal, diagonal, mask, ALU.add).then_inc(masked, 1)
                    dve.wait_ge(masked, 2 * (i + 1))
                    if i >= 1:
                        dve.wait_ge(max_step, 3 * i)
                    for t in range(QT):
                        dve.tensor_reduce(small[:, 24 + 2 * t:26 + 2 * t], scores_at(t), AX.X, ALU.max).then_inc(max_step, 1)
                    dve.wait_ge(max_step, 3 * i + 2)
                    dve.tensor_scalar(small[:, 8 + o:12 + o], small[:, 24:28], -1.0, None, ALU.mult).then_inc(max_step, 1)

                def difference(i):
                    o = 4 * (i % 2)
                    dve.wait_ge(exp_ready, 4 * i + 4)
                    if i >= 1:
                        dve.wait_ge(a_turned, 2 * i)
                        dve.wait_ge(a_step, 4 * i)
                    rs, cl = small[:, 16 + o:20 + o], small[:, 28:30]
                    dve.reciprocal(rs, rs).then_inc(rs_step, 1)
                    dve.wait_ge(rs_step, 2 * i + 1)
                    dve.tensor_scalar(cl, small[:, 17 + o:20 + o:2], small[:, 4:5], None, ALU.mult).then_inc(rs_step, 1)
                    for t in range(QT):
                        keys = META + P * (t + 1)
                        dve.tensor_scalar(a_sb[:, t, 0:keys], s_exp[:, i % 2, t, 0, 0:keys],
                                          small[:, 16 + o + 2 * t:17 + o + 2 * t], None, ALU.mult).then_inc(a_step, 1)
                    dve.wait_ge(rs_step, 2 * i + 2)
                    for t in range(QT):
                        keys = META + P * (t + 1)
                        dve.wait_ge(a_step, 4 * i + 1 + t)
                        dve.scalar_tensor_tensor(out=a_sb[:, t, 0:keys], in0=s_exp[:, i % 2, t, 1, 0:keys],
                                                 scalar=small[:, 28 + t:29 + t], in1=a_sb[:, t, 0:keys],
                                                 op0=ALU.mult, op1=ALU.add).then_inc(a_step, 1)

                def sub_norm(i):
                    r = i % 2
                    dve.wait_ge(o_squared, 2 * i + 2)
                    dve.tensor_scalar(o_ms[r][:, :], o_ss[r][:, :], 1.0 / P, SUBLN_EPS, ALU.mult, ALU.add).then_inc(sub_step, 1)
                    dve.wait_ge(sub_r0_ready, i + 1)
                    newton_steps(o_ms[r][:, :], o_r0[r][:, :], o_r[r][:, :], sub_step, 4 * i + 1)
                    if i >= 2:
                        dve.wait_ge(o_turned, i - 1)
                    for t in range(QT):
                        dve.tensor_scalar(o_sb[r][:, t, :], ps[:, 7, t * P:(t + 1) * P], o_r[r][:, t:t + 1], None,
                                          ALU.mult).then_inc(o_scaled, 1)

                def out_lo(i):
                    dve.wait_ge(out_hi_ready, i + 1)
                    dve.scalar_tensor_tensor(out=z_lo[:, i, :], in0=ps[:, 7, SEQ:2 * SEQ], scalar=small[:, 5:6],
                                             in1=z_hi[:, i, :].bitcast(F32), op0=ALU.mult, op1=ALU.subtract)\
                       .then_inc(out_lo_ready, 1)

                for i in range(HEADS + 3):
                    if 0 <= i - 2 < HEADS:
                        difference(i - 2)
                    if 0 <= i - 3 < HEADS:
                        sub_norm(i - 3)
                    if i < HEADS:
                        value(i)
                    if 0 <= i - 1 < HEADS:
                        rotary(i - 1)
                    if 0 <= i - 1 < HEADS - 1:
                        next_lo("qkv", TRI_N, i - 1, (i - 1) % 4)
                    if 0 <= i - 3 < HEADS:
                        out_lo(i - 3)
                    if 0 <= i - 1 < HEADS:
                        maxima(i - 1)
                    if i == HEADS:
                        next_lo("qkv", TRI_N, i - 1, (i - 1) % 4)

            def newton_steps(ms_, r0_, r_, step_sem, base):
                dve.tensor_tensor(r_, r0_, r0_, ALU.mult).then_inc(step_sem, 1)
                dve.wait_ge(step_sem, base + 1)
                dve.scalar_tensor_tensor(out=r_, in0=r_, scalar=-0.5, in1=ms_, op0=ALU.mult, op1=ALU.mult).then_inc(step_sem, 1)
                dve.wait_ge(step_sem, base + 2)
                dve.scalar_tensor_tensor(out=r_, in0=r_, scalar=1.5, in1=r0_, op0=ALU.add, op1=ALU.mult).then_inc(step_sem, 1)
                dve.wait_ge(step_sem, base + 3)

            def distances():
                dve.wait_ge(dist_done, 1)
                dve.tensor_tensor(by_dist[:, :], weight_sb[:, :], ps[0:HEADS, 7, :], ALU.add).then_inc(dist_ready, 1)

            def take(i, s):
                if i < 4:
                    bank = 3 * (i % 2) + s
                    dve.wait_ge(block_used, FIRST["mix_in"] + i + 1)
                else:
                    bank = s
                    if s < 2:
                        dve.wait_ge(mix_part, 2 * (i - 4) + s + 1)
                    else:
                        dve.wait_ge(block_used, FIRST["mix_in"] + i + 1)
                dve.tensor_tensor(proj[:, 3 * i + s, :], rstd[:, META:T], ps[:, bank, 0:SEQ], ALU.mult).then_inc(proj_copied, 1)

            def gated():
                for i in range(4):
                    for s in range(3):
                        take(i, s)
                    next_lo("mix_in", TRI_N, i, i)
                    if i == 0:
                        distances()
                    if i == 1:
                        dve.wait_ge(g_pe, 1)
                        dve.tensor_tensor(glow[0:16, :], rstd[0:16, META:T], ps[0:16, 6, 0:SEQ], ALU.mult).then_inc(glow_ready, 1)
                    if i == 2:
                        dve.wait_ge(g_act, 1)
                        dve.tensor_scalar(g_ls[:, :, :], ps[:, 7, :].rearrange("p (t f) -> p t f", t=2), 0.0, None, ALU.min)\
                           .then_inc(g_dve, 1)
                        dve.wait_ge(g_dve, 1)
                        dve.wait_ge(g_act, 3)
                        dve.tensor_tensor(g_ls[:, :, :], g_ls[:, :, :], g_a[:, :, :], ALU.subtract).then_inc(g_dve, 1)
                dve.wait_ge(g_act, 5)
                dve.wait_ge(g_pool, 1)
                for i in range(GLA_HEADS):
                    rows, c = slice(64 * (i % 2), 64 * (i % 2) + 64), i // 2
                    dve.scalar_tensor_tensor(out=g_q[rows, i, :], in0=proj[rows, GQ + c, :], scalar=0.125,
                                             in1=g_eb[rows, c, :], op0=ALU.mult, op1=ALU.mult).then_inc(g_dve, 1)
                dve.tensor_tensor(g_k[:, :, :], proj[:, GK:GK + 2, :], g_a[:, :, :], ALU.mult).then_inc(g_dve, 1)
                take(4, 0)
                dve.wait_ge(g_act, 6)
                dve.wait_ge(g_pool, 2)
                for t in range(QT):
                    for c in range(2):
                        rows = slice(64 * c, 64 * c + 64)
                        dve.tensor_tensor(g_ke[rows, t, c, :], g_et[rows, t, :], ps[rows, 5, t * SEQ:(t + 1) * SEQ],
                                          ALU.mult).then_inc(g_dve, 1)
                take(4, 1)
                dve.wait_ge(g_pe, 8)
                dve.wait_ge(g_pool, 3)
                for c in range(2):
                    rows = slice(64 * c, 64 * c + 64)
                    for b in range(2):
                        half = ps[rows, 3 + b, :].rearrange("p (n i) -> p n i", n=4)[:, :, rows]
                        dve.tensor_copy(g_att[rows, 4 * b:4 * b + 4, rows], half).then_inc(g_dve, 2)
                take(4, 2)
                next_lo("mix_in", TRI_N, 4, 0)
                dve.wait_ge(g_pe, 9)
                for c in range(3):
                    for p in range(2):
                        inc = ps[:, STATE_BANK[c], p * SEQ:(p + 1) * SEQ]
                        if c == 0:
                            dve.tensor_copy(g_s[:, 0, p, :], inc).then_inc(g_dve, 1)
                        else:
                            last = GLA_CHUNK * (c + 1) - 1
                            dve.wait_ge(g_dve, 19 + 2 * c - 1 + p)
                            dve.scalar_tensor_tensor(out=g_s[:, c, p, :], in0=g_s[:, c - 1, p, :],
                                                     scalar=g_eb[:, p, last:last + 1], in1=inc,
                                                     op0=ALU.mult, op1=ALU.add).then_inc(g_dve, 1)
                for s in range(3):
                    take(5, s)
                next_lo("mix_in", TRI_N, 5, 1)
                take(6, 0)
                dve.wait_ge(g_pe, 11)
                dve.tensor_scalar(n_ms[:, :, :].rearrange("p a s -> p (a s)").rearrange("p (b s) -> p b s", b=2),
                                  ps[:, 6:8, :], 1.0 / P, NORM_EPS, ALU.mult, ALU.add).then_inc(g_dve, 1)
                take(6, 1)
                dve.wait_ge(g_act, 11)
                newton_steps(n_ms[:, :, :], n_r0[:, :, :], n_r[:, :, :], g_dve, 26)
                for i in range(GLA_HEADS):
                    dve.tensor_tensor(n_r[:, i, :], n_r[:, i, :], ps[:, 3 + i // 2, (i % 2) * SEQ:(i % 2 + 1) * SEQ],
                                      ALU.mult).then_inc(g_dve, 1)
                take(6, 2)
                for i in range(GLA_HEADS):
                    dve.wait_ge(g_dve, 30 + i)
                    c = COL["gla_norm"] + i
                    dve.scalar_tensor_tensor(out=fx[:, i, META:T], in0=n_r[:, i, :], scalar=par[:, c:c + 1],
                                             in1=proj[:, GR + i, :], op0=ALU.mult, op1=ALU.mult).then_inc(g_dve, 1)

            def dilated():
                def key(i):
                    rows = slice(64 * (i % 2), 64 * (i % 2) + 64)
                    if i == 0:
                        dve.wait_ge(g_pool, 6)
                    if i >= 2:
                        dve.wait_ge(d_scores, i - 1)
                    dve.tensor_scalar(d_k[i % 2][rows, :], proj[rows, DK + 3 * (i // 2), :], 0.125, None, ALU.mult)\
                       .then_inc(d_k_ready, 1)

                def biased(i):
                    d, n = d_s[i % 2], 2 * (i % 2)
                    dve.wait_ge(d_scores, i + 1)
                    if i >= 2:
                        dve.wait_ge(d_p_step, 3 * (i - 1))
                    dve.tensor_tensor(d[:, 0:P], ps[:, 5 + i % 2, 0:P], bias[:, i, P - 1::-1], ALU.add).then_inc(d_s_ready, 1)
                    dve.tensor_tensor(d[:, P:3 * P], ps[:, 5 + i % 2, P:3 * P], bias[:, i, ::-1], ALU.add).then_inc(d_s_ready, 1)
                    if i >= 1:
                        dve.wait_ge(d_max_step, 3 * i)
                    for t in range(QT):
                        a, b = (0, P) if t == 0 else (P, 3 * P)
                        dve.wait_ge(d_s_ready, 2 * i + t + 1)
                        dve.tensor_reduce(small[:, 24 + t:25 + t], d[:, a:b], AX.X, ALU.max).then_inc(d_max_step, 1)
                    dve.wait_ge(d_max_step, 3 * i + 2)
                    dve.tensor_scalar(small[:, 8 + n:10 + n], small[:, 24:26], -1.0, None, ALU.mult).then_inc(d_max_step, 1)

                def normalised(i):
                    n = 2 * (i % 2)
                    dve.wait_ge(d_exp, 2 * i + 2)
                    rs = small[:, 16 + n:18 + n]
                    dve.reciprocal(rs, rs).then_inc(d_p_step, 1)
                    if i >= 1:
                        dve.wait_ge(d_turned, i)
                    dve.wait_ge(d_p_step, 3 * i + 1)
                    for t in range(QT):
                        a, b = (0, P) if t == 0 else (P, 3 * P)
                        dve.tensor_scalar(d_p[:, a:b], d_s[i % 2][:, a:b], small[:, 16 + n + t:17 + n + t], None, ALU.mult)\
                           .then_inc(d_p_step, 1)

                def out_lo(k):
                    dve.wait_ge(out_hi_ready, KD + k + 1)
                    dve.tensor_tensor(x_lo[:, k, META:T], fx[:, k, META:T], x_hi[:, k, META:T].bitcast(F32),
                                      ALU.subtract).then_inc(out_lo_ready, 1)

                key(0)
                key(1)
                take(7, 0)
                dve.wait_ge(bias_loaded, 16)
                biased(0)
                for i in range(HEADS):
                    if i + 1 < HEADS:
                        biased(i + 1)
                    if i + 2 < HEADS:
                        key(i + 2)
                    normalised(i)
                    if i < 2:
                        take(7, i + 1)
                    if i == 1:
                        next_lo("mix_in", TRI_N, 6, 2)
                    if i == 3:
                        next_lo("mix_in", TRI_N, 7, 3)
                    for k in OUT_AFTER.get(i - 1, ()):
                        out_lo(k)
                for k in OUT_AFTER[HEADS - 1] + (KD - 1,):
                    out_lo(k)

            def residual(m, j, u):
                hm = h[:, m, META:T] if isinstance(m, int) else h[:, bass.ds(m, 1), META:T]
                dve.tensor_tensor(hm, hm, ps[:, j % 4, META:T], ALU.add).then_inc(h_ready, 1)

            def wide_hidden():

                def step(i, j):
                    t = hid[j % 2][:, :]
                    dve.wait_ge(block_used, i + (FIRST["ff1"] + 1))
                    for c in range(2):
                        dve.scalar_tensor_tensor(out=t[:, c * SEQ:(c + 1) * SEQ], in0=ps[:, 2 * (j % 2) + c, 0:SEQ], scalar=0.0,
                                                 in1=rstd[:, META:T], op0=ALU.max, op1=ALU.mult).then_inc(relu_ready, 1)
                    dve.wait_ge(relu_ready, i * 2 + 2)
                    dve.tensor_tensor(t, t, t, ALU.mult).then_inc(hid_ready, 1)
                    next_lo("ff1", FF1_N, i, j)
                    dve.wait_ge(hid_hi_ready, i + (4 * KF + 1))
                    dve.tensor_tensor(hid_lo[:, bass.ds(i * 2 * SEQ, 2 * SEQ)], t,
                                      hid_hi[:, bass.ds(i * 2 * SEQ, 2 * SEQ)].bitcast(F32), ALU.subtract)\
                       .then_inc(hid_lo_ready, 1)

                loop(dve, FF1_N, step, peel=2)

            def second_lo(q):
                n = FIRST[ENTER[q]] + 1
                split_lo(n, n % 4, WIDTH[n])

            dve.memset(small[:, 30:31], 0.0).then_inc(gu_scaled, GU_CREDIT)
            dve.memset(eps_col, NORM_EPS).then_inc(eps_ready, 1)
            dve.memset(subln_eps_col, SUBLN_EPS).then_inc(eps_ready, 1)
            dve.memset(small[:, 29:30], 0.0).then_inc(f_ready, F_CREDIT)
            split_lo(0, 0, WIDTH[0])
            dve.wait_ge(par_loaded, 16)
            for k in range(KD):
                lo_part(0, k, 0, "ffn1_pre0")
            gains = [pre for _, pre, _, _ in SUB[1:]] + ["attn_norm"]
            s = 0
            for u, (kind, pre, post, f) in enumerate(SUB):
                c0 = first_col(u)
                if u == 0:
                    second_lo(0)
                if kind == "attn":
                    lam()
                pre_root(u, s, c0)
                s += 1
                if kind == "ffn":
                    hidden(f"gu{f}", f, c0)
                    out_projection(f"dn{f}", DN_N, 1, u, c0)
                elif kind == "conv":
                    convolution()
                    out_projection("conv_out", PROJ_N, 2, u, c0)
                else:
                    c0 = META
                    heads()
                    out_projection("attn_out", PROJ_N, 2, u, c0)
                post_norm(u, s, c0, 0.5 if kind == "ffn" else 1.0, gains[u])
                s += 1
                second_lo(u + 1)
            pre_root(6, s, META)
            s += 1
            gated()
            dilated()
            for i in range(PROJ_N):
                dve.wait_ge(block_used, FIRST["mix_out"] + i + 1)
                residual(2 * i, 2 * i, 6)
                residual(2 * i + 1, 2 * i + 1, 6)
                if i < PROJ_N - 1:
                    next_lo("mix_out", PROJ_N, i, i)
            for k in range(KD):
                lo_part(7, k, META, "mlp_norm")
            second_lo(7)
            pre_root(7, s, META)
            s += 1
            wide_hidden()
            n0 = FIRST["ff2"]
            for m in range(KD):
                dve.wait_ge(block_used, n0 + 2 * m + 1)
                if 2 * m + 2 < FF2_N:
                    next_lo("ff2", FF2_N, 2 * m, 2 * m % 4)
                dve.wait_ge(block_used, n0 + 2 * m + 2)
                residual(m, m, 7)
                if 2 * m + 3 < FF2_N:
                    next_lo("ff2", FF2_N, 2 * m + 1, (2 * m + 1) % 4)
            dve.wait_ge(h_ready, 8 * KD)
            root(s, META, h_sq_summed, 9 * KD, NORM_EPS)
            for k in range(KD):
                g = COL["final_norm"] + k
                dve.scalar_tensor_tensor(out=fx[:, k, META:T], in0=h[:, k, META:T], scalar=par[:, g:g + 1],
                                         in1=rstd[:, META:T], op0=ALU.mult, op1=ALU.mult).then_inc(out_ready, 1)

        @block.tensor
        def _(pe):
            def product(out_ap, slot, t0, tiles, hi, lo, start=True, stop=True, before=None, step=1):
                for k in range(tiles):
                    if before:
                        before(k)
                    cols = slice((t0 + k) * P, (t0 + k + 1) * P)
                    first, last = start and k == 0, stop and k == tiles - 1
                    pe.matmul(out_ap, w_hi[slot][:, cols], hi(k), start=first, stop=False)
                    pe.matmul(out_ap, w_hi[slot][:, cols], lo(k), start=False, stop=False)
                    mm = pe.matmul(out_ap, w_lo[slot][:, cols], hi(k), start=False, stop=last)
                return mm

            def x_parts(c0):
                return (lambda k: x_hi[:, k, c0:T]), (lambda k: x_lo[:, k, c0:T])

            def split_ready(n0, i):
                pe.wait_ge(lo_ready, i + (n0 + 1))

            def add_square(q, k, c0):
                pe.wait_ge(h_sq_ready, KD * q + k + 1)
                pe.matmul(ps[:, SUM, c0:T], ones[:, :], square[k % 2][:, c0:T], start=k == 0, stop=k == KD - 1)\
                  .then_inc(h_sq_summed, 1)

            def first_block(q, n0, parts, c0):
                split_ready(n0, 0)
                for k in range(KD):
                    pe.wait_ge(x_hi_ready, KD * q + k + 1)
                    for s, (o, c) in enumerate(parts):
                        cols = slice((s * KD + k) * P, (s * KD + k + 1) * P)
                        pe.matmul(o, w_hi[0][:, cols], x_hi[:, k, c:T], start=k == 0, stop=False)
                        pe.matmul(o, w_lo[0][:, cols], x_hi[:, k, c:T], start=False, stop=False)
                    pe.wait_ge(x_lo_ready, KD * q + k + 1)
                    for s, (o, c) in enumerate(parts):
                        cols = slice((s * KD + k) * P, (s * KD + k + 1) * P)
                        mm = pe.matmul(o, w_hi[0][:, cols], x_lo[:, k, c:T], start=False, stop=k == KD - 1)
                    if k == KD - 1:
                        mm.then_inc(block_used, 1)
                    add_square(q, k, c0)

            def hidden(name, f, q, c0):
                n0 = FIRST[name]
                hi, lo = x_parts(c0)
                first_block(q, n0, [(ps[:, 0, c0:T], c0), (ps[:, 1, c0:T], c0)], c0)

                def step(i, j):
                    split_ready(n0, i)
                    pe.wait_ge(gu_scaled, i * 2 + (2 * KF * f + 2))
                    product(ps[:, 2 * (j % 2), c0:T], j % 2, 0, KD, hi, lo)
                    product(ps[:, 2 * (j % 2) + 1, c0:T], j % 2, KD, KD, hi, lo).then_inc(block_used, 1)

                step(1, 1)
                loop(pe, GU_N, step, first=2)

            def down(name, f, u, c0):
                n0 = FIRST[name]
                hi = lambda k: hid_hi[:, k * T + c0:(k + 1) * T]
                lo = lambda k: hid_lo[:, k * T + c0:(k + 1) * T]

                def step(i, j):
                    split_ready(n0, i)
                    pe.wait_ge(f_ready, i + (KD * u + 1))
                    before = (lambda k: pe.wait_ge(hid_lo_ready, KF * f + k + 1) if k >= KF - 4 else None) if j == 0 else None
                    product(ps[:, j, c0:T], j % 2, 0, KF, hi, lo, before=before).then_inc(block_used, 1)

                loop(pe, DN_N, step)

            def keep_warm(count):
                pe.wait_ge(consts_loaded, 16)
                for _ in range(count):
                    pe.matmul(ps[:, 5, :], ones[:, :], sq4[:, :], start=True, stop=True)

            def sum_squares(u, c0):
                pe.wait_ge(sumsq_ready, KD * (u + 1))
                pe.matmul(ps[:, SUM + 1, c0:T], ones[:, :], sumsq[:, c0:T], start=True, stop=False)
                pe.matmul(ps[:, SUM, c0:T], ones[:, :], sumsq[:, c0:T], start=True, stop=False)
                pe.wait_ge(f_sq_ready, KD * (u + 1))
                last = square[(KD - 1) % 2]
                pe.matmul(ps[:, SUM + 1, c0:T], ones[:, :], last[:, c0:T], start=False, stop=True).then_inc(sumsq_summed_act, 1)
                pe.matmul(ps[:, SUM, c0:T], ones[:, :], last[:, c0:T], start=False, stop=True).then_inc(sumsq_summed_dve, 1)
                keep_warm(5)

            def convolution(q):
                n0 = FIRST["conv_in"]
                hi, lo = x_parts(0)

                first_block(q, n0, [(ps[:, s, 0:T], 0) for s in range(3)], 0)

                def step(i, j):
                    b = 3 * (j % 2)
                    split_ready(n0, i)
                    if not isinstance(i, int) or i >= 2:
                        pe.wait_ge(cv_u_ready, i - 1 + CV_CREDIT)
                    for s in range(3):
                        mm = product(ps[:, b + s, 0:T], j % 2, s * KD, KD, hi, lo)
                    mm.then_inc(block_used, 1)

                loop(pe, TRI_N, step, first=1)
                pe.wait_ge(cv_u_ready, TRI_N - 1 + CV_CREDIT)

            def first_outputs(name, hi, lo, ready, chunks, c0):
                for k in chunks:
                    if k == 0:
                        split_ready(FIRST[name], 0)
                    pe.wait_ge(ready[0], ready[1] + k + 1)
                    for s in range(2):
                        cols, o = slice((s * KD + k) * P, (s * KD + k + 1) * P), ps[:, s, c0:T]
                        pe.matmul(o, w_hi[0][:, cols], hi(k), start=k == 0, stop=False)
                        pe.matmul(o, w_hi[0][:, cols], lo(k), start=False, stop=False)
                        mm = pe.matmul(o, w_lo[0][:, cols], hi(k), start=False, stop=k == KD - 1)
                    if k == KD - 1:
                        mm.then_inc(block_used, 1)

            def out_projection(name, u, hi, lo, sem_, base, c0):
                n0 = FIRST[name]
                for i in range(1, PROJ_N):
                    split_ready(n0, i)
                    pe.wait_ge(sem_, base + 2 * i + 2)
                    for s in range(2):
                        mm = product(ps[:, (2 * i + s) % 4, c0:T], i % 2, s * KD, KD, hi, lo)
                    mm.then_inc(block_used, 1)

            def heads(q):
                n0 = FIRST["qkv"]

                def part(i, s):
                    c0 = META if s == 1 else 0
                    hi, lo = x_parts(c0)
                    bank = VALUE_BANK.get(i, 0) if s == 0 else s
                    if s == 0:
                        split_ready(n0, i)
                        if i >= 2:
                            pe.wait_ge(v_scaled, i)
                    else:
                        pe.wait_ge(part_copied, 2 * (i - 1) + s)
                    product(ps[:, bank, 0:T - c0], i % 2, s * KD, KD, hi, lo).then_inc(block_used if s == 2 else part_done, 1)

                def turn_and_rotate(i):
                    v = v_sb[i % 2]
                    pe.wait_ge(v_scaled, i + 1)
                    if i >= 1:
                        pe.wait_ge(v_tok_ready, 2 * i)
                    pe.transpose(ps[:, 5, 0:P], v[:, META:META + P], ident)
                    pe.transpose(ps[:, 5, P:2 * P], v[:, META + P:T], ident)
                    pe.transpose(ps[:, 5, 2 * P:3 * P], v[:, 0:P], ident).then_inc(v_turned, 1)
                    pe.wait_ge(part_copied, 2 * i + 2)
                    if i == 0:
                        pe.wait_ge(v_scaled, 2)
                    else:
                        pe.wait_ge(exp_ready, 4 * i)
                    pe.matmul(ps[:, 3, 0:SEQ], rotate, q_sb[i % 2][:, :], start=True, stop=True).then_inc(rotated, 1)
                    pe.matmul(ps[:, 4, 0:T], rotate, k_sb[i % 2][:, :], start=True, stop=True).then_inc(rotated, 1)

                def scores(i):
                    pe.wait_ge(rope_step, 7 * (i + 1))
                    for t in range(QT):
                        for c in range(2):
                            o = scores_at(t, c)
                            keys = o.shape[-1]
                            mm = pe.matmul(o, q_rot[i % 2][:, t * P:(t + 1) * P], k_rot[i % 2][:, c, 0:keys], start=True, stop=True)
                    mm.then_inc(scores_done, 1)

                def turn_attention(i):
                    if i + 1 < HEADS:
                        pe.wait_ge(v_tok_ready, 2 * (i + 2))
                    pe.wait_ge(a_step, 4 * i + 3)
                    pe.transpose(ps[:, 5, 0:P], a_sb[:, 0, 0:P], ident)
                    pe.transpose(ps[:, 5, P:2 * P], a_sb[:, 0, META:META + P], ident).then_inc(a_turned, 1)
                    pe.wait_ge(a_step, 4 * i + 4)
                    pe.transpose(ps[:, 6, 0:P], a_sb[:, 1, 0:P], ident)
                    pe.transpose(ps[:, 6, P:2 * P], a_sb[:, 1, META:META + P], ident)
                    pe.transpose(ps[:, 6, 2 * P:3 * P], a_sb[:, 1, META + P:T], ident).then_inc(a_turned, 1)

                def attend(i):
                    if i >= 1:
                        pe.wait_ge(out_lo_ready, i)
                    for t in range(QT):
                        pe.wait_ge(a_tok_ready, 4 * i + 2 * t + 2)
                        for n in range(t + 2):
                            mm = pe.matmul(ps[:, 7, t * P:(t + 1) * P], a_tok[:, 2 * t + n, :], v_tok[:, i, n, :],
                                           start=n == 0, stop=n == t + 1)
                    mm.then_inc(o_done, 1)

                def turn_out(i):
                    pe.wait_ge(o_scaled, 2 * i + 2)
                    for t in range(QT):
                        mm = pe.transpose(ps[:, 7, SEQ + t * P:SEQ + (t + 1) * P], o_sb[i % 2][:, t, :], ident)
                    mm.then_inc(o_turned, 1)

                z_hi_, z_lo_ = (lambda k: z_hi[:, k, :]), (lambda k: z_lo[:, k, :])
                first_block(q, n0, [(ps[:, s, 0:T - c0], c0) for s, c0 in enumerate((0, META, 0))], 0)
                pe.wait_ge(lam_step, 1)
                pe.matmul(ps[:, 7, 0:2], ones[:, :], small[:, 0:2], start=True, stop=True).then_inc(part_done, 2)
                for i in range(1, HEADS + 3):
                    if i < HEADS:
                        part(i, 0)
                    if 0 <= i - 1 < HEADS:
                        turn_and_rotate(i - 1)
                    if i in FIRST_OUTPUTS:
                        first_outputs("attn_out", z_hi_, z_lo_, (out_lo_ready, 0), FIRST_OUTPUTS[i][0], META)
                    if i < HEADS:
                        part(i, 1)
                    if 0 <= i - 3 < HEADS:
                        turn_out(i - 3)
                    if i in FIRST_OUTPUTS:
                        first_outputs("attn_out", z_hi_, z_lo_, (out_lo_ready, 0), FIRST_OUTPUTS[i][1], META)
                    if 0 <= i - 2 < HEADS:
                        turn_attention(i - 2)
                    if 0 <= i - 1 < HEADS:
                        scores(i - 1)
                    if i < HEADS:
                        part(i, 2)
                    if 0 <= i - 2 < HEADS:
                        attend(i - 2)

            def mixers(q):
                n0 = FIRST["mix_in"]
                hi, lo = x_parts(META)

                def part(i, s):
                    if s == 0:
                        split_ready(n0, i)
                    pe.wait_ge(proj_copied, 3 * (i - 2) + 3 if i == 4 else 3 * (i - 1) + s + 1)
                    product(ps[:, s, 0:SEQ], i % 2, s * KD, KD, hi, lo).then_inc(mix_part if s < 2 else block_used, 1)

                for i in range(4):
                    if i == 0:
                        first_block(q, n0, [(ps[:, s, 0:SEQ], META) for s in range(3)], META)
                        pe.wait_ge(mix_loaded, 6 * 16)
                        pe.wait_ge(mix_zeroed, 4)
                        pe.matmul(ps[0:HEADS, 7, :], rel_sb[:, :], onehot_sb[:, :], start=True, stop=True)\
                          .then_inc(dist_done, 1)
                        continue
                    split_ready(n0, i)
                    if i >= 2:
                        pe.wait_ge(proj_copied, 3 * (i - 1))
                    for s in range(3):
                        mm = product(ps[:, 3 * (i % 2) + s, 0:SEQ], i % 2, s * KD, KD, hi, lo)
                    mm.then_inc(block_used, 1)
                    if i == 1:
                        pe.wait_ge(low_ready, KD)
                        pe.wait_ge(proj_copied, 3)
                        for k in range(KD):
                            mm = pe.matmul(ps[0:16, 6, 0:SEQ], w_glow_sb[:, k, :], fx[:, k, META:T], start=k == 0, stop=k == KD - 1)
                        mm.then_inc(g_pe, 1)
                    if i == 2:
                        pe.wait_ge(glow_ready, 1)
                        pe.wait_ge(dist_ready, 1)
                        for t in range(QT):
                            mm = pe.matmul(ps[:, 7, t * SEQ:(t + 1) * SEQ], glow[:, t * P:(t + 1) * P], gate_w_sb[:, :],
                                           start=True, stop=True)
                        mm.then_inc(g_pe, 1)
                pe.wait_ge(g_dve, 2)
                for c in range(2):
                    for t in range(QT):
                        mm = pe.matmul(ps[:, 6, c * SEQ + t * P:c * SEQ + (t + 1) * P], g_ls[:, t, c * P:(c + 1) * P], upto,
                                       start=True, stop=True)
                mm.then_inc(g_pe, 1)
                for t in range(QT):
                    mm = pe.matmul(ps[:, 7, t * SEQ:(t + 1) * SEQ], after, g_ls[:, t, :], start=True, stop=True)
                mm.then_inc(g_pe, 1)
                pe.wait_ge(proj_copied, 12)
                for t in range(QT):
                    for c in range(4):
                        mm = pe.transpose(ps[:, 3 + t, c * P:(c + 1) * P], proj[:, GV + c, t * P:(t + 1) * P], ident)
                mm.then_inc(g_pe, 1)
                for t in range(QT):
                    for c in range(2):
                        mm = pe.transpose(ps[:, 5, t * SEQ + c * P:t * SEQ + (c + 1) * P], proj[:, GK + c, t * P:(t + 1) * P],
                                          ident)
                mm.then_inc(g_pe, 1)
                part(4, 0)
                part(4, 1)
                pe.wait_ge(g_act, 7)
                pe.wait_ge(g_dve, 7)
                for i in range(GLA_HEADS):
                    for t in range(QT):
                        n = 2 * i + t
                        mm = pe.matmul(ps[:, 3 + n // 4, (n % 4) * P:(n % 4 + 1) * P], g_k[:, i // 2, t * P:(t + 1) * P],
                                       g_q[:, i, t * P:(t + 1) * P], start=True, stop=True)
                    if i % 2:
                        mm.then_inc(g_pe, 1)
                part(4, 2)
                pe.wait_ge(g_dve, 11)
                for c in range(3):
                    for p in range(2):
                        mm = pe.matmul(ps[:, STATE_BANK[c], p * SEQ:(p + 1) * SEQ], g_ke[:, c // 2, c % 2, p * P:(p + 1) * P],
                                       gv_tok[:, c // 2, p * SEQ:(p + 1) * SEQ], start=True, stop=True)
                mm.then_inc(g_pe, 1)
                part(5, 0)
                part(5, 1)
                pe.wait_ge(g_pool, 4)
                pe.wait_ge(g_dve, 25)
                for i in range(GLA_HEADS):
                    for t in range(QT):
                        o = (i % 2) * SEQ + t * P
                        v = gv_tok[:, t, i * P:(i + 1) * P]
                        mm = pe.matmul(ps[:, 3 + i // 2, o:o + P], v, g_att[:, 2 * i + t, :], start=True, stop=False)
                        for c in range(2):
                            n = 2 * t + c
                            if n:
                                mm = pe.matmul(ps[:, 3 + i // 2, o + 64 * c:o + 64 * c + 64],
                                               g_s[:, n - 1, i // 2, (i % 2) * P:(i % 2 + 1) * P],
                                               g_q[:, i, 64 * n:64 * n + 64], start=False, stop=c == 1)
                mm.then_inc(g_pe, 1)
                part(5, 2)
                part(6, 0)
                pe.wait_ge(g_act, 9)
                flat = n_sq[:, :, :].rearrange("p a s -> p (a s)")
                for b in range(2):
                    mm = pe.matmul(ps[:, 6 + b, :], ones[:, :], flat[:, b * 512:(b + 1) * 512], start=True, stop=True)
                mm.then_inc(g_pe, 1)
                part(6, 1)
                part(6, 2)

                def scores(i):
                    pe.wait_ge(d_k_ready, i + 1)
                    if i >= 2:
                        pe.wait_ge(d_s_ready, 2 * (i - 1))
                    query = proj[:, DQ + 3 * (i // 2), :]
                    pe.matmul(ps[:, 5 + i % 2, 0:P], query[:, 0:P], d_k[i % 2][:, 0:P], start=True, stop=True)
                    pe.matmul(ps[:, 5 + i % 2, P:3 * P], query[:, P:2 * P], d_k[i % 2][:, :], start=True, stop=True)\
                      .then_inc(d_scores, 1)

                part(7, 0)
                part(7, 1)
                pe.wait_ge(g_dve, 33)
                scores(0)
                scores(1)
                for i in range(HEADS):
                    c = i // 2
                    if i == 0:
                        part(7, 2)
                    if i + 2 < HEADS:
                        scores(i + 2)
                    if i >= 1:
                        pe.wait_ge(d_o_copied, i)
                    if i % 2 == 0:
                        for t in range(QT):
                            mm = pe.transpose(ps[:, 3, SEQ + t * P:SEQ + (t + 1) * P], proj[:, DV + 3 * c, t * P:(t + 1) * P], ident)
                        mm.then_inc(dv_turned, 1)
                    if i in MIX_OUTPUTS:
                        pe.wait_ge(proj_copied, 3 * TRI_N)
                        first_outputs("mix_out", hi, lo, (out_lo_ready, KD), MIX_OUTPUTS[i], META)
                    pe.wait_ge(d_p_step, 3 * i + 3)
                    if i >= 1:
                        pe.wait_ge(d_pt_ready, i)
                    for n in range(3):
                        mm = pe.transpose(ps[:, 7, n * P:(n + 1) * P], d_p[:, n * P:(n + 1) * P], ident)
                    mm.then_inc(d_turned, 1)
                    pe.wait_ge(d_pt_ready, i + 1)
                    pe.wait_ge(dv_ready, c + 1)
                    v = slice(c * P, (c + 1) * P)
                    pe.matmul(ps[:, 3, 0:P], dv_tok[:, 0, v], d_pt[:, 0, :], start=True, stop=True)
                    pe.matmul(ps[:, 3, P:2 * P], dv_tok[:, 0, v], d_pt[:, 1, :], start=True, stop=False)
                    pe.matmul(ps[:, 3, P:2 * P], dv_tok[:, 1, v], d_pt[:, 2, :], start=False, stop=True).then_inc(d_o_done, 1)
                first_outputs("mix_out", hi, lo, (out_lo_ready, KD), (4, 5, 6, 7), META)

            def wide_hidden(q):
                n0 = FIRST["ff1"]
                hi, lo = x_parts(META)

                first_block(q, n0, [(ps[:, s, 0:SEQ], META) for s in range(2)], META)

                def step(i, j):
                    split_ready(n0, i)
                    if not isinstance(i, int) or i >= 2:
                        pe.wait_ge(relu_ready, i * 2 - 2)
                    for s in range(2):
                        mm = product(ps[:, 2 * (j % 2) + s, 0:SEQ], j % 2, s * KD, KD, hi, lo)
                    mm.then_inc(block_used, 1)

                for i in (1, 2, 3):
                    step(i, i)
                loop(pe, FF1_N, step, first=4)

            def wide_down():
                n0 = FIRST["ff2"]
                half = KF2 // 2

                for i in range(FF2_N):
                    m, s = i // 2, i % 2
                    hi = lambda k: hid_hi[:, (s * half + k) * SEQ:(s * half + k + 1) * SEQ]
                    lo = lambda k: hid_lo[:, (s * half + k) * SEQ:(s * half + k + 1) * SEQ]
                    split_ready(n0, i)
                    if i == 0:
                        pe.wait_ge(hid_lo_ready, 4 * KF + FF1_N - 2)
                    if i == 1:
                        pe.wait_ge(hid_lo_ready, 4 * KF + FF1_N)
                    if s == 0:
                        pe.wait_ge(h_ready, 7 * KD + max(0, m - 3))
                    product(ps[:, m % 4, META:T], i % 2, 0, half, hi, lo, start=s == 0, stop=s == 1).then_inc(block_used, 1)
                    if s == 1 and m >= 1:
                        add_square(8, m - 1, META)
                add_square(8, KD - 1, META)

            pe.wait_ge(ones_ready, 1)
            for u, (kind, pre, post, f) in enumerate(SUB):
                c0 = first_col(u)
                if kind == "ffn":
                    hidden(f"gu{f}", f, u, c0)
                    down(f"dn{f}", f, u, c0)
                elif kind == "conv":
                    convolution(u)
                    y_parts = (lambda k: y_hi[:, k, :]), (lambda k: y_lo[:, k, :])
                    first_outputs("conv_out", *y_parts, (cv_lo_ready, 0), range(KD), 0)
                    out_projection("conv_out", u, *y_parts, f_ready, KD * u, 0)
                else:
                    c0 = META
                    heads(u)
                    out_projection("attn_out", u, lambda k: z_hi[:, k, :], lambda k: z_lo[:, k, :], f_ready, KD * u, META)
                sum_squares(u, c0)
            mixers(6)
            hi, lo = x_parts(META)
            out_projection("mix_out", 6, hi, lo, h_ready, 6 * KD - F_CREDIT, META)
            wide_hidden(7)
            wide_down()


GD_DONE = 37


def blocks_of(w, pieces):
    rows = np.array([[r for r, _ in p] for p in pieces])
    cols = np.array([[c for _, c in p] for p in pieces])
    k, m = w.shape
    tiled = w.reshape(k // P, P, m // P, P).transpose(0, 2, 1, 3)
    picked = tiled[rows // P, cols // P]
    return np.ascontiguousarray(picked.transpose(0, 2, 1, 3).reshape(len(pieces), P, -1))


def columns(v):
    return v.reshape(-1, P).T


def kernel(**inputs):
    import concourse.bacc as bacc
    from concourse.bass_utils import run_bass_kernel_spmd

    a = {k: np.asarray(v) for k, v in inputs.items()}
    ks = range(KD)
    rows = lambda n: [k * P for k in range(n)]

    def swiglu_in(w):
        return blocks_of(w, [[(r, i * P) for r in rows(KD)] + [(r, D_FF + i * P) for r in rows(KD)] for i in range(KF)])

    def down(w):
        return blocks_of(w, [[(r, m * P) for r in rows(KF)] for m in ks])

    def triple(w, order):
        return blocks_of(w, [[(r, s * D + i * P) for s in order for r in rows(KD)] for i in ks])

    def pairs(w, n):
        return blocks_of(w, [[(r, (2 * b + s) * P) for s in range(2) for r in rows(KD)] for b in range(n)])

    w_in = a["w_in_2"][0]
    low = 2 * SEQ + 2 * 512
    w_mix = np.concatenate([w_in[:, :low], w_in[:, low + 16:]], axis=1)
    mix_chunks = [(3 * i, 3 * i + 1, 3 * i + 2) for i in range(4)] + [(12 + c, 16 + c, 20 + c) for c in range(4)]
    arrays = {
        "gu0": swiglu_in(a["ffn1_w_gu"][0]), "dn0": down(a["ffn1_w_down"][0]),
        "conv_in": triple(a["conv_w_in"][0], (0, 1, 2)), "conv_out": pairs(a["conv_w_out"][0], PROJ_N),
        "gu1": swiglu_in(a["ffn2_w_gu"][0]), "dn1": down(a["ffn2_w_down"][0]),
        "gu2": swiglu_in(a["ffn1_w_gu"][1]), "dn2": down(a["ffn1_w_down"][1]),
        "qkv": triple(a["attn_w_qkv"][0], (2, 0, 1)), "attn_out": pairs(a["attn_w_o"][0], PROJ_N),
        "gu3": swiglu_in(a["ffn2_w_gu"][1]), "dn3": down(a["ffn2_w_down"][1]),
        "mix_in": blocks_of(w_mix, [[(r, m * P) for m in chunks for r in rows(KD)] for chunks in mix_chunks]),
        "mix_out": pairs(a["w_out_2"][0], PROJ_N),
        "ff1": pairs(a["w_ff1_2"][0], FF1_N),
        "ff2": blocks_of(a["w_ff2_2"][0], [[((s * 16 + k) * P, m * P) for k in range(16)] for m in ks for s in range(2)]),
    }
    lam = np.zeros((P, 4), np.float32)
    lam[:64] = a["attn_lambda"][0].T
    par = [a["ln_ffn1"][0, 0], a["ln_ffn1"][0, 1], a["ln_mix"][0, 0], a["ln_mix"][0, 1], a["ln_ffn2"][0, 0],
           a["ln_ffn2"][0, 1], a["ln_ffn1"][1, 0], a["ln_ffn1"][1, 1], a["ln_mix"][1, 0], a["ln_mix"][1, 1],
           a["ln_ffn2"][1, 0], a["ln_ffn2"][1, 1], a["attn_norm_g_2"][0], a["mlp_norm_g_2"][0], a["final_norm_g_2"],
           a["conv_w"][0], a["attn_subln_g"][0], a["gla_norm_g_2"][0]]
    small = {}
    small["params"] = np.ascontiguousarray(np.concatenate([columns(v) for v in par] + [lam], axis=1))
    tokens = np.concatenate([a["meta_tokens"], a["x"][0]], axis=0)
    small["h_in"] = np.ascontiguousarray(tokens.T.reshape(KD, P, T).transpose(1, 0, 2))
    small["squares"], small["rope_mask"], small["onehot"], small["weight"] = shape_constants()
    small["w_glow"] = np.ascontiguousarray(w_in[:, low:low + 16].reshape(KD, P, 16).transpose(1, 0, 2))
    small["gate_w"] = np.concatenate([a["gla_gate_w2_2"][0], a["gla_gate_b_2"]], axis=0)
    small["rel_bias"] = np.ascontiguousarray(a["rel_bias_2"])

    nc = bacc.Bacc("TRN2", target_bir_lowering=False, num_devices=1)
    dram = lambda name, v: nc.dram_tensor(name, v.shape, F32, kind="ExternalInput").ap()
    w = {name: dram(f"w_{name}", v) for name, v in arrays.items()}
    s = {name: dram(name, v) for name, v in small.items()}
    out = nc.dram_tensor("out", (D, SEQ), F32, kind="ExternalOutput").ap()
    two_blocks(nc, w, out=out, **s)
    feed = {f"w_{name}": v for name, v in arrays.items()} | small
    r = run_bass_kernel_spmd(nc, [feed], core_ids=[0])
    return np.asarray(r.results[0]["out"]).T.reshape(1, SEQ, D)
```
